# Optimizing a Trainium2 kernel written in Bass

```python
import jax, jax.numpy as jnp
from jax import lax
import numpy as np

D_MODEL = 1024
BATCH = 1
SEQ = 128
DEPTH = 1
DEC_BATCH = 1
DEC_SEQ = 128
PAST_LEN = 128

GRID_W = 64
POOL_WIDTH = 512
POOL_GROUPS = 4
POOL_GROUP_DIM = POOL_WIDTH // POOL_GROUPS
POOL_WINDOWS = (2, 4, 8, 16)
RWKV_WIDTH = 512
RWKV_HEAD_SIZE = 64
RWKV_HEADS = RWKV_WIDTH // RWKV_HEAD_SIZE
DECAY_LORA = 64
AAA_LORA = 64
GATE_LORA = 128
N_EXPERTS = 32
TOP_K = 4
D_FF = 1024
SWIGLU_ALPHA = 1.702
SWIGLU_LIMIT = 7.0
RMS_EPS = 1e-6
GN_EPS = 1e-5 * RWKV_HEAD_SIZE
N_MOD = 6

OFF_R = POOL_WIDTH
OFF_MERGE = OFF_R + 3 * RWKV_WIDTH + 2 * DECAY_LORA + 2 * AAA_LORA + GATE_LORA
IN_COLS = OFF_MERGE + 2 * D_MODEL
SHIFT_COLS = OFF_MERGE - OFF_R

kernel_name = "pool_birwkv7_moe_prefix_dit"

def rmsnorm(x, w):
    xf = x.astype(jnp.float32)
    y = xf * lax.rsqrt(jnp.mean(xf * xf, axis=-1, keepdims=True) + RMS_EPS)
    return (y * w).astype(x.dtype)

def modulation(cvec, w_mod, b_mod):
    m = jax.nn.silu(cvec.astype(jnp.float32)) @ w_mod + b_mod
    return jnp.split(m[:, None, :], N_MOD, axis=-1)

def shift_context(p):
    B, T, C = p.shape
    g = p.reshape(B, T, C // 2, 2)
    prev = jnp.pad(g[:, :-1, :, 0], ((0, 0), (1, 0), (0, 0)))
    nxt = jnp.pad(g[:, 1:, :, 1], ((0, 0), (0, 1), (0, 0)))
    return jnp.stack([prev, nxt], axis=-1).reshape(B, T, C)

def shift_grid(p):
    B, T, C = p.shape
    rows = T // GRID_W
    g = p.reshape(B, rows, GRID_W, C // 4, 4)
    left = jnp.pad(g[:, :, :-1, :, 0], ((0, 0), (0, 0), (1, 0), (0, 0)))
    right = jnp.pad(g[:, :, 1:, :, 1], ((0, 0), (0, 0), (0, 1), (0, 0)))
    up = jnp.pad(g[:, :-1, :, :, 2], ((0, 0), (1, 0), (0, 0), (0, 0)))
    down = jnp.pad(g[:, 1:, :, :, 3], ((0, 0), (0, 1), (0, 0), (0, 0)))
    return jnp.stack([left, right, up, down], axis=-1).reshape(B, T, C)

def pool_branch(u, pool_w, pool_scale):
    B, T, _ = u.shape
    uf = u.astype(jnp.float32)
    cs = jnp.pad(jnp.cumsum(uf, axis=1), ((0, 0), (1, 0), (0, 0)))
    t = jnp.arange(T)
    outs = []
    for gi, win in enumerate(POOL_WINDOWS):
        sl = slice(gi * POOL_GROUP_DIM, (gi + 1) * POOL_GROUP_DIM)
        lo = jnp.clip(t - win // 2, 0, T)
        hi = jnp.clip(t + win // 2, 0, T)
        csg = cs[:, :, sl]
        s = jnp.take(csg, hi, axis=1) - jnp.take(csg, lo, axis=1)
        cnt = (hi - lo).astype(jnp.float32)[None, :, None]
        outs.append(s / cnt - uf[:, :, sl])
    pooled = jnp.stack(outs, axis=2)
    mixed = jnp.einsum('btgc,gcd->btgd', pooled, pool_w).reshape(B, T, POOL_WIDTH)
    return mixed * pool_scale

def wkv_scan(r, w, k, v, kk, a, s0, reverse):
    def step(S, inp):
        r_t, w_t, k_t, v_t, kk_t, a_t = inp
        sa = jnp.einsum('bhvk,bhk->bhv', S, -kk_t)
        S = (S * w_t[:, :, None, :]
             + sa[..., None] * (kk_t * a_t)[:, :, None, :]
             + v_t[..., None] * k_t[:, :, None, :])
        y = jnp.einsum('bhvk,bhk->bhv', S, r_t)
        return S, y
    xs = tuple(jnp.moveaxis(z, 1, 0) for z in (r, w, k, v, kk, a))
    S, ys = lax.scan(step, s0.astype(jnp.float32), xs, reverse=reverse)
    return jnp.moveaxis(ys, 0, 1), S

def rwkv_branch(p, shift_fn, s0_f, s0_b, lp):
    B, T, _ = p.shape
    pf = p.astype(jnp.float32)
    pm = pf + lp['shift_mu'] * (shift_fn(pf) - pf)

    def heads(z):
        return z.reshape(B, T, RWKV_HEADS, RWKV_HEAD_SIZE)

    r = pm[..., 0:RWKV_WIDTH]
    k = pm[..., RWKV_WIDTH:2 * RWKV_WIDTH]
    v = pm[..., 2 * RWKV_WIDTH:3 * RWKV_WIDTH]
    o = 3 * RWKV_WIDTH
    w_lo = (pm[..., o:o + DECAY_LORA], pm[..., o + DECAY_LORA:o + 2 * DECAY_LORA])
    o += 2 * DECAY_LORA
    a_lo = (pm[..., o:o + AAA_LORA], pm[..., o + AAA_LORA:o + 2 * AAA_LORA])
    o += 2 * AAA_LORA
    g = jax.nn.sigmoid(pm[..., o:o + GATE_LORA]) @ lp['gate_w2']

    kk = heads(k * lp['k_k'])
    kk = kk / jnp.maximum(jnp.sqrt(jnp.sum(kk * kk, axis=-1, keepdims=True)), 1e-12)
    rh, vh = heads(r), heads(v)
    ys, finals = [], []
    for d, (reverse, s0) in enumerate(((False, s0_f), (True, s0_b))):
        w = -jax.nn.softplus(-(lp['decay_w0'][d] + jnp.tanh(w_lo[d]) @ lp['decay_w2'][d])) - 0.5
        decay = jnp.exp(-jnp.exp(w))
        a = jax.nn.sigmoid(lp['iclr_a0'][d] + a_lo[d] @ lp['iclr_a2'][d])
        kd = heads(k * (1.0 + (a - 1.0) * lp['k_a']))
        yd, Sd = wkv_scan(rh, heads(decay), kd, vh, kk, heads(a), s0, reverse)
        yd = yd + jnp.sum(rh * kd * lp['r_k'], axis=-1, keepdims=True) * vh
        ys.append(yd)
        finals.append(Sd)
    y = ys[0] + ys[1]
    mu = jnp.mean(y, axis=-1, keepdims=True)
    var = jnp.mean((y - mu) ** 2, axis=-1, keepdims=True)
    y = ((y - mu) * lax.rsqrt(var + GN_EPS)).reshape(B, T, RWKV_WIDTH)
    y = (y * lp['ln_x_w'] + lp['ln_x_b']) * g
    return y, finals[0], finals[1]

def moe(h, lp):
    B, T, D = h.shape
    xt = h.reshape(B * T, D)
    logits = (xt @ lp['router_w'] + lp['router_b']).astype(jnp.float32)
    top_v, top_i = lax.top_k(logits, TOP_K)
    top_w = jax.nn.softmax(top_v, axis=-1)
    combine = jnp.sum(jax.nn.one_hot(top_i, N_EXPERTS, dtype=jnp.float32) * top_w[..., None], axis=1)
    out = jnp.zeros((B * T, D), jnp.float32)
    for e in range(N_EXPERTS):
        gu = xt @ lp['expert_w_gu'][e] + lp['expert_b_gu'][e]
        glu = jnp.minimum(gu[:, :D_FF], SWIGLU_LIMIT)
        lin = jnp.clip(gu[:, D_FF:], -SWIGLU_LIMIT, SWIGLU_LIMIT)
        act = glu * jax.nn.sigmoid(SWIGLU_ALPHA * glu) * (lin + 1.0)
        out = out + combine[:, e:e + 1] * (act @ lp['expert_w_down'][e] + lp['expert_b_down'][e])
    return out.astype(h.dtype).reshape(B, T, D)

def trunk_layer(x, mod, shift_fn, s0_f, s0_b, lp):
    shift1, scale1, gate1, shift2, scale2, gate2 = mod
    hn = rmsnorm(x, lp['norm_mix_w']) * (1.0 + scale1) + shift1
    proj = hn @ lp['w_in']
    merge = jax.nn.sigmoid(proj[..., OFF_MERGE:] + lp['b_merge'])
    y_pool = pool_branch(proj[..., :OFF_R], lp['pool_w'], lp['pool_scale']) @ lp['w_pool_out']
    y_rwkv, sf, sb = rwkv_branch(proj[..., OFF_R:OFF_MERGE], shift_fn, s0_f, s0_b, lp)
    y_rwkv = y_rwkv @ lp['w_rwkv_out']
    mixed = (merge[..., :D_MODEL] * y_pool + merge[..., D_MODEL:] * y_rwkv) @ lp['w_o']
    x = (x + gate1 * mixed).astype(x.dtype)
    hn2 = rmsnorm(x, lp['norm_ffn_w']) * (1.0 + scale2) + shift2
    x = (x + gate2 * moe(hn2, lp)).astype(x.dtype)
    return x, sf, sb

def setup_inputs(seed: int = 0) -> dict:
    key = jax.random.key(seed)
    ks = iter(jax.random.split(key, 48))

    def nrm(shape, s):
        return jax.random.normal(next(ks), shape, jnp.float32) * s

    D, L, H, N, E = D_MODEL, DEPTH, RWKV_HEADS, RWKV_HEAD_SIZE, N_EXPERTS
    return {
        'x_prompt': nrm((BATCH, SEQ, D), 1.0),
        'x_sample': nrm((DEC_BATCH, DEC_SEQ, D), 1.0),
        'state_fwd': nrm((DEC_BATCH, L, H, N, N), 0.3),
        'state_bwd': nrm((DEC_BATCH, L, H, N, N), 0.3),
        'c': nrm((DEC_BATCH, D), 1.0),
        'c_ctx': nrm((D,), 1.0),
        'w_mod': nrm((L, D, N_MOD * D), 0.5 * D ** -0.5),
        'b_mod': nrm((L, N_MOD * D), 0.02),
        'norm_mix_w': 1.0 + nrm((L, D), 0.1),
        'w_in': nrm((L, D, IN_COLS), D ** -0.5),
        'b_merge': nrm((L, 2 * D), 0.1),
        'pool_w': nrm((L, POOL_GROUPS, POOL_GROUP_DIM, POOL_GROUP_DIM), POOL_GROUP_DIM ** -0.5),
        'pool_scale': 1.0 + nrm((L, POOL_WIDTH), 0.1),
        'w_pool_out': nrm((L, POOL_WIDTH, D), POOL_WIDTH ** -0.5),
        'shift_mu': jax.random.uniform(next(ks), (L, SHIFT_COLS), jnp.float32),
        'decay_w0': nrm((L, 2, RWKV_WIDTH), 0.5),
        'decay_w2': nrm((L, 2, DECAY_LORA, RWKV_WIDTH), 0.5 * DECAY_LORA ** -0.5),
        'iclr_a0': nrm((L, 2, RWKV_WIDTH), 0.5),
        'iclr_a2': nrm((L, 2, AAA_LORA, RWKV_WIDTH), 0.5 * AAA_LORA ** -0.5),
        'gate_w2': nrm((L, GATE_LORA, RWKV_WIDTH), GATE_LORA ** -0.5),
        'k_k': 0.85 + nrm((L, RWKV_WIDTH), 0.05),
        'k_a': 1.0 + nrm((L, RWKV_WIDTH), 0.05),
        'r_k': nrm((L, H, N), 0.1),
        'ln_x_w': 1.0 + nrm((L, RWKV_WIDTH), 0.1),
        'ln_x_b': nrm((L, RWKV_WIDTH), 0.02),
        'w_rwkv_out': nrm((L, RWKV_WIDTH, D), RWKV_WIDTH ** -0.5),
        'w_o': nrm((L, D, D), D ** -0.5),
        'norm_ffn_w': 1.0 + nrm((L, D), 0.1),
        'router_w': nrm((L, D, E), D ** -0.5),
        'router_b': nrm((L, E), 0.01),
        'expert_w_gu': nrm((L, E, D, 2 * D_FF), D ** -0.5),
        'expert_b_gu': nrm((L, E, 2 * D_FF), 0.01),
        'expert_w_down': nrm((L, E, D_FF, D), D_FF ** -0.5),
        'expert_b_down': nrm((L, E, D), 0.01),
        'norm_final_w': 1.0 + nrm((D,), 0.1),
    }

def reference(x_prompt, x_sample, state_fwd, state_bwd, c, c_ctx, w_mod, b_mod, norm_mix_w, w_in, b_merge,
              pool_w, pool_scale, w_pool_out, shift_mu, decay_w0, decay_w2, iclr_a0, iclr_a2, gate_w2,
              k_k, k_a, r_k, ln_x_w, ln_x_b, w_rwkv_out, w_o, norm_ffn_w, router_w, router_b,
              expert_w_gu, expert_b_gu, expert_w_down, expert_b_down, norm_final_w):
    xp, xs = x_prompt, x_sample
    zeros = jnp.zeros((xp.shape[0], RWKV_HEADS, RWKV_HEAD_SIZE, RWKV_HEAD_SIZE), jnp.float32)
    new_f, new_b = [], []
    for l in range(DEPTH):
        lp = {
            'norm_mix_w': norm_mix_w[l], 'w_in': w_in[l], 'b_merge': b_merge[l],
            'pool_w': pool_w[l], 'pool_scale': pool_scale[l], 'w_pool_out': w_pool_out[l],
            'shift_mu': shift_mu[l], 'decay_w0': decay_w0[l], 'decay_w2': decay_w2[l],
            'iclr_a0': iclr_a0[l], 'iclr_a2': iclr_a2[l], 'gate_w2': gate_w2[l],
            'k_k': k_k[l], 'k_a': k_a[l], 'r_k': r_k[l], 'ln_x_w': ln_x_w[l], 'ln_x_b': ln_x_b[l],
            'w_rwkv_out': w_rwkv_out[l], 'w_o': w_o[l], 'norm_ffn_w': norm_ffn_w[l],
            'router_w': router_w[l], 'router_b': router_b[l],
            'expert_w_gu': expert_w_gu[l], 'expert_b_gu': expert_b_gu[l],
            'expert_w_down': expert_w_down[l], 'expert_b_down': expert_b_down[l],
        }
        mod_ctx = modulation(c_ctx[None, :], w_mod[l], b_mod[l])
        mod_lat = modulation(c, w_mod[l], b_mod[l])
        xp, sf, sb = trunk_layer(xp, mod_ctx, shift_context, zeros, zeros, lp)
        new_f.append(sf)
        new_b.append(sb)
        xs, _, _ = trunk_layer(xs, mod_lat, shift_grid, state_fwd[:, l], state_bwd[:, l], lp)
    y_prompt = rmsnorm(xp, norm_final_w)
    y_sample = rmsnorm(xs, norm_final_w)
    new_state_fwd = jnp.stack(new_f, axis=1)
    new_state_bwd = jnp.stack(new_b, axis=1)
    return (y_prompt, y_sample, new_state_fwd, new_state_bwd)


_drawn_inputs = setup_inputs


def setup_inputs(seed=0):
    import zlib

    import numpy as np

    out = dict(_drawn_inputs(seed))
    spreads = {}
    factors = {'state_fwd': 8.0,
     'state_bwd': 6.411,
     'b_merge': 4.809,
     'pool_scale': 2.952,
     'r_k': 3.774,
     'ln_x_w': 3.356,
     'ln_x_b': 24.455,
     'router_b': 4.95,
     'expert_b_gu': 30.041,
     'expert_b_down': 37.241}
    for name, (base, spread) in spreads.items():
        noise = np.random.default_rng([zlib.crc32(name.encode()), seed]).standard_normal(out[name].shape)
        drawn = base * np.exp(spread * noise) if base else spread * noise
        out[name] = __import__('jax').numpy.asarray(drawn.astype(out[name].dtype))
    for name, factor in factors.items():
        out[name] = (out[name] * factor).astype(out[name].dtype)
    return out
```

```python
import concourse.bass as bass
from concourse import mybir
from contextlib import ExitStack

F32 = mybir.dt.float32
I32 = mybir.dt.int32
U32 = mybir.dt.uint32
ALU = mybir.AluOpType
ACT = mybir.ActivationFunctionType
AX = mybir.AxisListType

P = 128
D = 1024
T = 128
NS = 2
TT = NS * T
KT = D // P
POOLW = 512
RW = 512
NT = RW // P
HS = 64
GRID_W = 64
RCOLS = 3 * RW + 3 * P
RTILES = RCOLS // P
OFF_M = POOLW + RCOLS
WINDOWS = (2, 4, 8, 16)
NE = 32
FF = 1024
SLOTS = 64
EXTRA = 16
ITEMS = NE + EXTRA + 1
DECAY = 0.6065306597126334
LIMIT = 7.0
ALPHA = 1.702
RMS_EPS = 1e-6
GN_EPS = 1e-5 * HS

RING = 12
FRING = 8
CW = 2048
GU_CHUNKS = KT
DN_CHUNKS = 4


def front_chunks():
    out = [("w_mod", 256 * i, 256) for i in range(8)]
    out += [("w_in", POOLW + 256 * i, 256) for i in range(RTILES // 2)] + [("w_in", OFF_M - P, P)]
    out += [("w_in", 0, 256), ("w_in", 256, 256)]
    out += [("w_mod", 2048 + 256 * i, 256) for i in range(16)]
    out += [("w_in", OFF_M + 256 * i, 256) for i in range(8)]
    out += [("w_pool_out", 512 * i, 512) for i in range(2)]
    out += [("w_rwkv_out", 512 * i, 512) for i in range(2)]
    out += [("w_o", 256 * i, 256) for i in range(4)]
    return out


CHUNKS = front_chunks()
NF = len(CHUNKS)
C_MODA, C_RWKV, C_POOL, C_MODB, C_MERGE, C_POUT, C_ROUT, C_WO = 0, 8, 16, 18, 34, 42, 44, 46


def released(c):
    if c < C_RWKV:
        return "moda_mm", c + 1
    if c < C_POOL:
        return "proj_done", min(2 * (c - C_RWKV) + 2, RTILES)
    if c < C_MODB:
        return "pu_mm", c - C_POOL + 1
    if c < C_MERGE:
        return "modb_mm", c - C_MODB + 1
    if c < C_POUT:
        return "merge_mm", 2 * (c - C_MERGE) + 2
    if c < C_ROUT:
        return "pout_mm", 4 * (c - C_POUT) + 4
    if c < C_WO:
        return "rout_mm", 4 * (c - C_ROUT) + 4
    return "wo_mm", 2 * (c - C_WO) + 2


FRONT_USES = [len(range(s, NF, FRING)) for s in range(FRING)] + [0] * (RING - FRING)


def trunk_kernel(nc, A, O, scratch):
    ctx = ExitStack()
    sems = {}

    def S(name):
        if name not in sems:
            sems[name] = ctx.enter_context(nc.semaphore(name))
        return sems[name]

    def sb(name, shape, dt=F32):
        return ctx.enter_context(nc.sbuf_tensor(name, shape, dt))

    ring = sb("ring", [P, RING, CW])

    ident = sb("ident", [P, P])
    ones = sb("ones", [P, P])
    upp = sb("upp", [P, P])
    mqr = sb("mqr", [P, 2, 2, P])
    lvl = sb("lvl", [P, 7, 2, P])
    bmean = sb("bmean", [P, P])
    rowlo = sb("rowlo", [P, 1])
    iotai = sb("iotai", [P, P], I32)
    iota2 = sb("iota2", [P, P])
    eidx = sb("eidx", [P, P])
    iota3 = sb("iota3", [P, 3])
    thr3 = sb("thr3", [P, 3])
    par4 = sb("par4", [P, 4])
    par2 = sb("par2", [P, 2])

    rows_a = sb("rows_a", [96, P])
    rows_b = sb("rows_b", [55, P])
    prm = sb("prm", [P, 96])
    prb = sb("prb", [P, 55])
    cvec = sb("cvec", [P, NS, KT])
    csig = sb("csig", [P, NS, KT])
    mu = sb("mu", [P, 7, RTILES])
    kam = sb("kam", [P, NT])
    epsr = sb("epsr", [P, 1])
    epsg = sb("epsg", [P, 1])
    moda = sb("moda", [P, 2, KT, NS])
    modb = sb("modb", [P, 4, KT, NS])
    gcol = sb("gcol", [P, 2, NS, KT])
    grow = sb("grow", [2 * NS * KT, P])

    x = sb("x", [P, NS, D])
    stat = sb("stat", [P, 8])
    hnT = sb("hnT", [P, KT, TT])
    pr = sb("pr", [P, RTILES, TT])
    raw = sb("raw", [P, 4, TT])
    kk = sb("kk", [P, NT, TT])
    qr = sb("qr", [P, 2, NS, NT, 2, T])
    bt = sb("bt", [P, 2, NS, NT, T])
    kt_ = sb("kt_", [P, 2, NS, NT, T])
    vt = sb("vt", [P, NS, RW])
    s0t = sb("s0t", [P, 2 * NT, HS])
    pms = sb("pms", [P, 2 * NT])
    fin = sb("fin", [P, 2, NT])
    gate = sb("gate", [P, NT, TT])
    corr = sb("corr", [P, NT, TT])
    pmT = sb("pmT", [P, 4, TT])

    early = qr[:].rearrange("p d s c k t -> p (d s c k t)")
    w2, a2, gw2 = early[:, 0:512], early[:, 512:1024], early[:, 1024:1536]
    poolw = early[:, 1536:2048].rearrange("p (g c) -> p g c", g=4)
    w0row = early[0:1, 2048:3072].rearrange("p (d c) -> p d c", d=2)
    s0raw = early[0:HS, 3072:4096].rearrange("p (d q c) -> p d q c", d=2, q=NT)
    em = kt_[:].rearrange("p d s c t -> p (d s c t)")
    pband = em[:, 0:512].rearrange("p (g t) -> p g t", g=4)
    tri = em[:, 512:1024].rearrange("p (d k t) -> p d k t", d=2, k=2)
    bdm = em[:, 1024:1280].rearrange("p (b t) -> p b t", b=2)
    low = em[:, 1280:1408]
    bones = em[:, 1408:1536]
    rawf = raw[:].rearrange("p c t -> p (c t)")
    so = rawf[:, 0:512].rearrange("p (c k) -> p c k", c=2 * NT)
    zs = rawf[:, 512:1024].rearrange("p (d i v) -> p d i v", d=2, i=4)
    us = pr[:, 8:12, :].rearrange("p c t -> p (c t)").rearrange("p (g i v) -> p g i v", g=4, i=4)

    sig = ring[:, 8, :].rearrange("p (d s c) -> p d s c", d=2, s=NS)
    aa = ring[:, 9, :].rearrange("p (d c t) -> p d c t", d=2, c=NT)
    kd = ring[:, 10, :].rearrange("p (d c t) -> p d c t", d=2, c=NT)
    utok = ring[:, 11, 0:1024].rearrange("p (s c) -> p s c", s=NS)
    pooled = ring[:, 11, 1024:2048].rearrange("p (g t) -> p g t", g=4)
    work = ring[:, 8:12, :].rearrange("p g (k i t) -> p g k i t", k=4, i=4)
    W_M, W_X, W_AT, W_XT = 0, 1, 2, 3


    def kqm(g):
        return ring[:, 8 + g, 0:1024].rearrange("p (i k t) -> p i k t", i=4, k=2)

    xn = ring[:, 8, :].rearrange("p (s c) -> p s c", s=NS)
    junk = ring[:, 9, :].rearrange("p (s c) -> p s c", s=NS)
    bfin = raw[:].rearrange("p c t -> p (c t)").rearrange("p (d q t) -> p d q t", d=2, q=NT)
    bkt = pr[:, 0:8, :].rearrange("p c t -> p (c t)").rearrange("p (j d c) -> p j d c", j=2, d=2)

    area = qr[:].rearrange("p d s c k t -> p (d s c k t)")
    merge = area.rearrange("p (m t) -> p m t", m=16)
    x2t = bt[:].rearrange("p d s c t -> p (d s c t)").rearrange("p (s c) -> p s c", s=NS)
    xn2 = x2t
    ms = kt_[:].rearrange("p d s c t -> p (d s c t)").rearrange("p (m t) -> p m t", m=KT)
    gbc = pr[:, 0:8, :].rearrange("p m t -> p (m t)").rearrange("p (s c) -> p s c", s=NS)
    bgu = area[0:NE, 0:2048]
    bdn = area[0:NE, 2048:3072]
    rtw = sb("rtw", [P, KT, NE])
    rtb = sb("rtb", [1, NE])
    wbuf = area[:, 3072:4096]
    xg = gate[:].rearrange("p c t -> p (c t)")[:, 0:512].rearrange("p (k s) -> p k s", k=KT)
    gsb = gate[:].rearrange("p c t -> p (c t)")[:, 512:1024]
    sgb = corr[:].rearrange("p c t -> p (c t)")[:, 0:512]
    lcb = corr[:].rearrange("p c t -> p (c t)")[:, 512:1024]
    act_ = pmT[:].rearrange("p c t -> p (c t)")[:, 0:512]
    actT = pmT[:].rearrange("p c t -> p (c t)")[:, 512:1024].rearrange("p (j h s) -> p j h s", j=4, h=2)
    ysb = kk[:].rearrange("p c t -> p (c t)")[:, 0:512]
    pwt = kk[:].rearrange("p c t -> p (c t)")[:, 512:768].rearrange("p (i t) -> p i t", i=NS)
    p2 = vt[:, 0, 0:256].rearrange("p (i s) -> p i s", i=NS)
    pw = vt[:, 0, 256:512].rearrange("p (i s) -> p i s", i=NS)
    sele = vt[0:NE, 1, 0:SLOTS]
    lg = sb("lg", [P, NS, NE])
    top8 = sb("top8", [P, NS, 8])
    idx8 = sb("idx8", [P, NS, 8], U32)
    idxf = sb("idxf", [P, NS, 8])
    tw = sb("tw", [P, NS, 4])
    twn = sb("twn", [P, NS, 4])
    sel = sb("sel", [P, NS, NE])
    comb = sb("comb", [P, NS, NE])
    oh = sb("oh", [P, NE])
    rank = sb("rank", [P, NS, NE])
    combT = sb("combT", [NE, TT])
    cnt = sb("cnt", [NE, 8])
    fl = sb("fl", [NE, 3])
    posc = sb("posc", [NE, 3])
    oh16 = sb("oh16", [NE, 3, EXTRA])
    e16 = sb("e16", [NE, 2, EXTRA])
    item = sb("item", [1, ITEMS + 1], I32)
    base = sb("base", [P, ITEMS])
    fstat = sb("fstat", [P, 4])

    banks = [ctx.enter_context(nc.psum_tensor(f"bank{i}", [P, 512], F32)) for i in range(8)]

    def ring_in(c):
        _, _, n = CHUNKS[c]
        rt = min(KT, CW // n)
        return ring[:, c % FRING, 0:rt * n].rearrange("p (k n) -> p k n", k=rt)

    def arrived(eng, c):
        eng.wait_ge(S(f"slot{c % FRING}_full"), 16 * (c // FRING + 1))

    rwv = {n: A[n] for n in ("w_in", "w_mod", "w_pool_out", "w_rwkv_out", "w_o")}

    XB = [(0, 1), (2, 3)]
    PB = [banks[0], banks[5], banks[6], banks[7]]
    CB = [4, 0, 6, 7]
    block = ctx.enter_context(nc.Block())

    @block.sync
    def _(sp):
        sp.dma_start(x[:, 0, :], A["x_prompt"][0]).then_inc(S("x_in"), 16)
        sp.dma_start(x[:, 1, :], A["x_sample"][0]).then_inc(S("x_in"), 16)

        def rows(dst, at, ap, n, s):
            sp.dma_start(dst[at:at + n, :], ap).then_inc(S(s), 16)

        def r128(ap):
            return ap.rearrange("(n p) -> n p", p=P)

        rows(rows_a, 0, r128(A["c_ctx"]), 8, "rows_a_in")
        rows(rows_a, 8, r128(A["c"][0]), 8, "rows_a_in")
        rows(rows_a, 16, r128(A["b_mod"][0]), 48, "rows_a_in")
        rows(rows_a, 64, r128(A["norm_mix_w"][0]), 8, "rows_a_in")
        rows(rows_a, 72, r128(A["norm_ffn_w"][0]), 8, "rows_a_in")
        rows(rows_a, 80, r128(A["b_merge"][0]), 16, "rows_a_in")

        def chunk(c):
            name, c0, n = CHUNKS[c]
            if c >= FRING:
                name_, count = released(c - FRING)
                sp.wait_ge(S(name_), count)
            src = rwv[name][0].rearrange("(k p) n -> p k n", p=P)[:, :, c0:c0 + n]
            sp.dma_start(ring_in(c), src).then_inc(S(f"slot{c % FRING}_full"), 16)

        for c in range(2):
            chunk(c)
        rows(rows_b, 0, r128(A["shift_mu"][0]), 15, "rows_b_in")
        rows(rows_b, 15, r128(A["pool_scale"][0]), 4, "rows_b_in")
        for d in range(2):
            rows(rows_b, 19 + 4 * d, r128(A["iclr_a0"][0, d]), 4, "rows_b_in")
        rows(rows_b, 27, r128(A["k_k"][0]), 4, "rows_b_in")
        rows(rows_b, 31, r128(A["k_a"][0]), 4, "rows_b_in")
        rows(rows_b, 35, A["r_k"][0].rearrange("(n a) c -> n (a c)", a=2), 4, "rows_b_in")
        rows(rows_b, 39, r128(A["ln_x_w"][0]), 4, "rows_b_in")
        rows(rows_b, 43, r128(A["ln_x_b"][0]), 4, "rows_b_in")
        rows(rows_b, 47, r128(A["norm_final_w"]), 8, "rows_b_in")
        for c in range(2, 8):
            chunk(c)
        sp.dma_start(w2, A["decay_w2"][0].rearrange("d l c -> (d l) c")).then_inc(S("lora_in"), 16)
        sp.dma_start(a2, A["iclr_a2"][0].rearrange("d l c -> (d l) c")).then_inc(S("lora_in"), 16)
        sp.dma_start(gw2, A["gate_w2"][0]).then_inc(S("lora_in"), 16)
        sp.dma_start(w0row, A["decay_w0"]).then_inc(S("lora_in"), 16)
        sp.dma_start(poolw, A["pool_w"][0].rearrange("g c d -> c g d")).then_inc(S("poolw_in"), 16)
        for d, n in enumerate(("state_fwd", "state_bwd")):
            for q in range(NT):
                sp.dma_start(s0raw[:, d, q, :].rearrange("v (h k) -> v h k", h=2),
                             A[n][0, 0, 2 * q:2 * q + 2].rearrange("h v k -> v h k")).then_inc(S("state_in"), 16)
        sp.dma_start(rtw[:], A["router_w"][0].rearrange("(k p) e -> p k e", p=P)).then_inc(S("router_in"), 16)
        sp.dma_start(rtb[:], A["router_b"]).then_inc(S("router_in"), 16)
        for c in range(8, NF):
            chunk(c)

        def expert_chunks(e, uses):
            for j in range(RING):
                uses(j)
                if j < GU_CHUNKS:
                    src, dst = A["expert_w_gu"][0][bass.ds(e, 1), j * P:(j + 1) * P, :], ring[:, j, :]
                    src = src.rearrange("o p n -> (o p) n")
                else:
                    r = 2 * P * (j - GU_CHUNKS)
                    src = A["expert_w_down"][0][bass.ds(e, 1), r:r + 2 * P, :].rearrange("o (i p) n -> p (o i) n", i=2)
                    dst = ring[:, j, :].rearrange("p (i n) -> p i n", i=2)
                sp.dma_start(dst, src).then_inc(S(f"slot{j}_full"), 16)

        def first(j):
            if j < FRING:
                name, count = released(max(c for c in range(NF) if c % FRING == j))
                sp.wait_ge(S(name), count)
            elif j == FRING:
                sp.wait_ge(S("y_mm"), 4)

        expert_chunks(0, first)
        sp.wait_ge(S("items_ready"), 1)
        n_items = sp.value_load(item[0:1, ITEMS:ITEMS + 1], min_val=NE, max_val=NE + EXTRA)
        with sp.Fori(1, n_items) as it:
            e = sp.value_load(item[0:1, bass.ds(it, 1)], min_val=0, max_val=NE - 1)
            def again(j):
                sp.wait_ge(S("chunk_used"), it * RING + (j + 1 - RING))

            expert_chunks(e, again)
        sp.wait_ge(S("stored"), 96)

    @block.gpsimd
    def _(pool):
        g = nc.gpsimd
        n = [0]

        def step(ins):
            n[0] += 1
            ins.then_inc(S("pool_step"), 1)
            pool.wait_ge(S("pool_step"), n[0])

        def signal(ins, name, count):
            ins.then_inc(S(name), 1)
            pool.wait_ge(S(name), count)

        def keep(dst, src, pattern, op, fill, b=0, cm=1):
            step(g.affine_select(out=dst, in_=src, compare_op=op, fill=fill, base=b, pattern=pattern,
                                 channel_multiplier=cm))

        step(g.memset(ident[:], 0.0))
        step(g.memset(ones[:], 1.0))
        keep(ident[:], ident[:], [[-1, P]], ALU.not_equal, 1.0)
        step(g.memset(epsr[:], RMS_EPS))
        step(g.memset(epsg[:], GN_EPS))
        signal(g.memset(rowlo[:], 0.0), "ident_ready", 1)
        keep(low, ones[:], [[-1, P]], ALU.is_gt, 0.0)
        keep(upp[:], ones[:], [[1, P]], ALU.is_gt, 0.0, cm=-1)
        keep(mqr[:, 0, 0, :], ones[:], [[1, P]], ALU.is_gt, 0.0, cm=-1)
        keep(mqr[:, 0, 1, :], ones[:], [[1, P]], ALU.is_ge, 0.0, cm=-1)
        keep(mqr[:, 1, 0, :], ones[:], [[-1, P]], ALU.is_gt, 0.0)
        keep(mqr[:, 1, 1, :], ones[:], [[-1, P]], ALU.is_ge, 0.0)
        step(g.memset(rowlo[0:HS, :], 1.0))
        step(g.memset(bones, 0.0))
        step(g.memset(bmean[:], 0.0))
        for h in range(2):
            step(g.memset(bones[h * HS:(h + 1) * HS, h * HS:(h + 1) * HS], 1.0))
            step(g.memset(bmean[h * HS:(h + 1) * HS, h * HS:(h + 1) * HS], 1.0 / HS))
        for i, w in enumerate(WINDOWS):
            keep(pband[:, i, :], ones[:], [[-1, P]], ALU.is_ge, 0.0, b=w // 2)
            keep(pband[:, i, :], pband[:, i, :], [[1, P]], ALU.is_gt, 0.0, b=w // 2, cm=-1)
        signal(g.memset(base[:], 0.0), "masks_ready", 1)
        for i in range(1, 7):
            m = 2 ** i
            if i >= 3:
                pool.wait_ge(S("bd_used"), i - 1)
            b = bdm[:, i % 2, :]
            bv = b.rearrange("p (n m) -> p n m", m=m)
            keep(bv, ones[:].rearrange("p (n m) -> p n m", m=m), [[-m, P // m], [0, m]], ALU.is_ge, 0.0)
            signal(g.affine_select(out=bv, in_=bv, compare_op=ALU.is_gt, fill=0.0, base=m,
                                   pattern=[[m, P // m], [0, m]], channel_multiplier=-1), "bd_ready", i)
        step(g.iota(iotai[:], [[0, 2], [1, SLOTS]], base=0, channel_multiplier=0))
        step(g.tensor_copy(iota2[:], iotai[:]))
        step(g.iota(iotai[:], [[0, P]], base=0, channel_multiplier=1))
        step(g.tensor_copy(eidx[:], iotai[:]))
        step(g.tensor_copy(iota3[:], iota2[:, 0:3]))
        step(g.iota(item[:, 0:NE], [[1, NE]], base=0, channel_multiplier=0))
        step(g.memset(item[:, NE:ITEMS + 1], 0))
        signal(g.tensor_scalar(thr3[:], iota2[:, 0:3], float(SLOTS), float(SLOTS), ALU.mult, ALU.add), "lists_ready", 1)

        pool.wait_ge(S("grow_ready"), 1)
        pool.dma_start(scratch.rearrange("g s (k p) -> (g s k) p", p=P), grow[:]).then_inc(S("gates_out"), 16)
        pool.wait_ge(S("gates_out"), 16)
        pool.wait_ge(S("y_mm"), 4)
        for gi in range(2):
            if gi:
                pool.wait_ge(S("wo_used"), 8)
            for s in range(NS):
                pool.dma_start(gbc[:, s, :], scratch[gi, s:s + 1, :].to_broadcast([P, D])).then_inc(S("gbc_in"), 16)
            if gi:
                pool.dma_start(bgu, A["expert_b_gu"][0]).then_inc(S("bgu_in"), 16)
                pool.dma_start(bdn, A["expert_b_down"][0]).then_inc(S("bdn_in"), 16)
                pool.dma_start(wbuf, A["norm_final_w"].rearrange("(a n) -> a n", a=1).to_broadcast([P, D])).then_inc(S("wfin_in"), 16)

    @block.tensor
    def _(pe):
        mm = nc.tensor.matmul
        tr = nc.tensor.transpose

        pe.wait_ge(S("ident_ready"), 1)
        pe.wait_ge(S("rows_a_in"), 96)
        tr(banks[0][:, 0:96], rows_a[:], ident[0:96, 0:96]).then_inc(S("prmT_done"), 1)
        for s in range(NS):
            pe.wait_ge(S("xn_ready"), s + 1)
            for k in range(KT):
                b = banks[1 + k // 2]
                last = tr(b[:, (k % 2) * TT + s * T:(k % 2) * TT + (s + 1) * T], xn[:, s, k * P:(k + 1) * P], ident[:])
        last.then_inc(S("xnT_done"), 1)

        def mod_chunks(c0, bank, n_ct, done):
            for i in range(n_ct // 2):
                arrived(pe, c0 + i)
                w = ring_in(c0 + i)
                for h in range(2):
                    ct = 2 * i + h
                    for k in range(KT):
                        last = mm(bank[:, 2 * ct:2 * ct + 2], w[:, k, h * P:(h + 1) * P], cvec[:, :, k],
                                  start=(k == 0), stop=(k == KT - 1))
                last.then_inc(S(done), 1)

        pe.wait_ge(S("cvec_ready"), 1)
        mod_chunks(C_MODA, banks[5], 16, "moda_mm")
        pe.wait_ge(S("rows_b_in"), 160)
        tr(banks[0][:, 128:183], rows_b[:], ident[0:55, 0:55]).then_inc(S("prbT_done"), 1)

        pe.wait_ge(S("hn_ready"), 2)
        pe.wait_ge(S("prb_ready"), 1)
        for ct in range(RTILES):
            c = C_RWKV + ct // 2
            arrived(pe, c)
            w = ring_in(c)
            if ct >= 4:
                pe.wait_ge(S("raw_copied"), ct - 3)
            o = (ct % 2) * P if ct < RTILES - 1 else 0
            for k in range(KT):
                last = mm(PB[ct % 4][:, 0:TT], w[:, k, o:o + P], hnT[:, k, :], start=(k == 0), stop=(k == KT - 1))
            last.then_inc(S("proj_done"), 1)

        for c in range(2):
            arrived(pe, C_POOL + c)
            w = ring_in(C_POOL + c)
            for s in range(NS):
                for k in range(KT):
                    last = mm(banks[2 + s][:, 256 * c:256 * c + 256], hnT[:, k, s * T:(s + 1) * T], w[:, k, :],
                              start=(k == 0), stop=(k == KT - 1))
            last.then_inc(S("pu_mm"), 1)

        pe.wait_ge(S("masks_ready"), 1)
        mm(banks[4][:, :], ones[:], pband.rearrange("p g t -> p (g t)"), start=True, stop=True).then_inc(S("pcnt_done"), 1)

        pe.wait_ge(S("lora_in"), 64)
        pe.wait_ge(S("raw_copied"), RTILES)
        pe.wait_ge(S("th_ready"), 1)
        for d in range(2):
            for s in range(NS):
                b = PB[2 * d + s]
                mm(b[:, :], pr[d * HS:(d + 1) * HS, 12, s * T:(s + 1) * T], w2[d * HS:(d + 1) * HS, :], start=True, stop=False)
                mm(b[:, :], ones[0:1, :], w0row[0:1, d, :], start=False, stop=True).then_inc(S("z_done"), 1)
        pe.wait_ge(S("utok_ready"), 2)
        pe.wait_ge(S("pband_ready"), 1)
        for gi in range(4):
            for s in range(NS):
                last = mm(banks[2 + gi // 2][:, (gi % 2) * TT + s * T:(gi % 2) * TT + (s + 1) * T],
                          utok[:, s, gi * P:(gi + 1) * P], pband[:, gi, :], start=True, stop=True)
        last.then_inc(S("pooled_done"), 1)
        pe.wait_ge(S("sig_ready"), 4)
        for d in range(2):
            for q in range(NT):
                last = mm(PB[2 * d + q // 2][:, (q % 2) * TT:(q % 2 + 1) * TT], a2[d * HS:(d + 1) * HS, q * P:(q + 1) * P],
                          pr[d * HS:(d + 1) * HS, 13, :], start=True, stop=True)
                if q % 2:
                    last.then_inc(S("a_done"), 1)
        pe.wait_ge(S("pooled_ready"), 2)
        pe.wait_ge(S("poolw_in"), 16)
        pe.wait_ge(S("pband_ready"), 1)
        MB = [banks[1], banks[4]]
        for gi in range(4):
            last = mm(MB[gi // 2][:, (gi % 2) * TT:(gi % 2 + 1) * TT], poolw[:, gi, :], pooled[:, gi, :], start=True, stop=True)
        last.then_inc(S("mixed_done"), 1)
        for q in range(NT):
            last = mm(banks[2 + q // 2][:, (q % 2) * TT:(q % 2 + 1) * TT], gw2[:, q * P:(q + 1) * P], pr[:, 14, :], start=True, stop=True)
        last.then_inc(S("gate_done"), 1)
        pe.wait_ge(S("a_ready"), 4)
        pe.wait_ge(S("ksq_ready"), 1)
        for q in range(NT):
            last = mm(PB[q // 2][:, (q % 2) * TT:(q % 2 + 1) * TT], bones, raw[:, q, :], start=True, stop=True)
        last.then_inc(S("norm_done"), 1)
        for s in range(NS):
            for q in range(NT):
                last = tr(banks[6 + s][:, q * P:(q + 1) * P], pr[:, 8 + q, s * T:(s + 1) * T], ident[:])
        last.then_inc(S("vt_done"), 1)
        pe.wait_ge(S("state_in"), 128)
        pe.wait_ge(S("mixed_ready"), 2)
        for d in range(2):
            for q in range(NT):
                i = d * NT + q
                last = tr(banks[1][:, i * HS:(i + 1) * HS], s0raw[:, d, q, :], ident[0:HS, 0:HS])
        last.then_inc(S("s0_done"), 1)
        pe.wait_ge(S("gate_ready"), 2)
        pe.wait_ge(S("rkk_ready"), 1)
        for q in range(NT):
            last = mm(banks[2 + q // 2][:, (q % 2) * TT:(q % 2 + 1) * TT], bones, raw[:, q, :], start=True, stop=True)
        last.then_inc(S("rk_done"), 1)
        pe.wait_ge(S("tri_ready"), 1)
        pe.wait_ge(S("kk_ready"), 1)
        pe.wait_ge(S("vt_ready"), 2)
        for i in range(8):
            d, s, t2 = i // 4, (i // 2) % 2, i % 2
            if i >= 4:
                pe.wait_ge(S("cum_used"), i - 3)
            for q in range(2):
                last = mm(banks[CB[i % 4]][:, q * 256:(q + 1) * 256], sig[:, d, s, (2 * t2 + q) * P:(2 * t2 + q + 1) * P],
                          tri[:, d, :, :].rearrange("p k t -> p (k t)"), start=True, stop=True)
            last.then_inc(S("cum_done"), 1)

        mod_chunks(C_MODB, banks[5], 32, "modb_mm")
        pe.wait_ge(S("gcol_ready"), 1)
        tr(banks[5][0:32, 128:256], gcol[:].rearrange("p g s k -> p (g s k)"), ident[:]).then_inc(S("grow_done"), 1)

        for j in range(2):
            for d in range(2):
                pe.wait_ge(S("bf_ready"), 2 * j + d + 1)
                if 2 * j + d >= 2:
                    pe.wait_ge(S("bk_ready"), 2 * j + d - 1)
                b = banks[2 + d]
                for q in range(NT):
                    last = tr(b[:, q * P:(q + 1) * P], bfin[:, d, q, :], ident[:])
                last.then_inc(S("bk_done"), 1)

        for s in range(NS):
            pe.wait_ge(S("scan_ops_ready"), s + 1)
            pe.wait_ge(S("grow_ready"), 1)
            for g in range(4):
                d, tp = g // 2, g % 2
                if g >= 2:
                    pe.wait_ge(S("a_evac"), 4 * s + g - 1)
                elif s == 1:
                    pe.wait_ge(S("y_evac"), 2)
                    pe.wait_ge(S("state_copied"), 1)
                elif g == 0:
                    pe.wait_ge(S("bk_ready"), 4)
                ba, bat = banks[2 * (g % 2)], banks[2 * (g % 2) + 1]
                for i in range(4):
                    h, q = i // 2, 2 * tp + i % 2
                    r = slice(h * HS, (h + 1) * HS)
                    b, c = (ba, bat)[h], (i % 2) * T
                    mm(b[:, c:c + T], qr[r, d, s, q, 0, :], bt[r, d, s, q, :], start=True, stop=True)
                    last = mm(b[:, 2 * T + c:3 * T + c], bt[r, d, s, q, :], qr[r, d, s, q, 0, :], start=True, stop=True)
                last.then_inc(S("a_mm"), 1)
            for l in range(1, 7):
                for g in range(4):
                    n = 24 * s + 4 * (l - 1) + g
                    if l == 1:
                        pe.wait_ge(S("a_evac"), 4 * s + g + 1)
                    else:
                        pe.wait_ge(S("x_upd"), n - 4 + 1)
                    if n >= 2:
                        pe.wait_ge(S("m_evac"), n - 1)
                    b = banks[4 + g % 2]
                    for i in range(4):
                        last = mm(b[:, i * T:(i + 1) * T], work[:, g, W_AT, i, :], work[:, g, W_X, i, :], start=True, stop=True)
                    last.then_inc(S("m_mm"), 1)
                for g in range(4):
                    n = 24 * s + 4 * (l - 1) + g
                    pe.wait_ge(S("m_evac"), n + 1)
                    if g >= 2:
                        pe.wait_ge(S("x_upd"), n - 2 + 1)
                    bx, bxt = XB[g % 2]
                    for i in range(4):
                        if l < 6:
                            mm(banks[bx][:, i * T:(i + 1) * T], work[:, g, W_XT, i, :], work[:, g, W_M, i, :], start=True, stop=True)
                        last = mm(banks[bxt][:, i * T:(i + 1) * T], work[:, g, W_M, i, :], work[:, g, W_XT, i, :], start=True, stop=True)
                    last.then_inc(S("x_mm"), 1)
            for tp in range(2):
                for d in range(2):
                    g = 2 * d + tp
                    n = 4 * s + 2 * tp + d
                    pe.wait_ge(S("x_upd"), 24 * s + 20 + g + 1)
                    if tp == 0 and d == 0:
                        pe.wait_ge(S("x_upd"), 24 * s + 24)
                    if n % 4:
                        pe.wait_ge(S("kq_evac"), n)
                    for i in range(4):
                        h, q = i // 2, 2 * tp + i % 2
                        r = slice(h * HS, (h + 1) * HS)
                        mm(banks[i // 2][:, (i % 2) * 256:(i % 2 + 1) * 256], kt_[r, d, s, q, :],
                           qr[r, d, s, q, :, :].rearrange("p k t -> p (k t)"), start=True, stop=True)
                        last = mm(banks[(2, 6)[h]][:, (i % 2) * T:(i % 2 + 1) * T], bt[r, d, s, q, :], qr[r, d, s, q, 1, :], start=True, stop=True)
                    last.then_inc(S("kq_mm"), 1)
                    pe.wait_ge(S("kq_evac"), n + 1)
                    for i in range(4):
                        h, q = i // 2, 2 * tp + i % 2
                        r = slice(h * HS, (h + 1) * HS)
                        o = banks[(3, 7)[h]][:, (i % 2) * HS:(i % 2 + 1) * HS]
                        last = mm(o, kqm(g)[:, i, 0, :], vt[:, s, q * P + h * HS:q * P + (h + 1) * HS],
                                  start=True, stop=(s == 0))
                        if s == 1:
                            last = mm(o, qr[r, d, s, q, 0, :], s0t[r, d * NT + q, :], start=False, stop=True)
                    last.then_inc(S("z_mm"), 1)
                    pe.wait_ge(S("z_evac"), n + 1)
                    if n:
                        pe.wait_ge(S("u_evac"), n)
                    for i in range(4):
                        last = mm(banks[4][:, i * HS:(i + 1) * HS], work[:, g, W_XT, i, :], zs[:, d, i, :], start=True, stop=True)
                    last.then_inc(S("u_mm"), 1)
                pe.wait_ge(S("u_evac"), 4 * s + 2 * tp + 2)
                if s or tp:
                    pe.wait_ge(S("y_evac"), 2 * s + tp)
                for qi in range(2):
                    q = 2 * tp + qi
                    for h in range(2):
                        i = 2 * h + qi
                        r = slice(h * HS, (h + 1) * HS)
                        o = banks[5][r, qi * T:(qi + 1) * T]
                        for d in range(2):
                            g = 2 * d + tp
                            mm(o, vt[:, s, q * P + h * HS:q * P + (h + 1) * HS], kqm(g)[:, i, 1, :], start=(d == 0), stop=False)
                            last = mm(o, us[:, g, i, :], work[:, g, W_AT, i, :], start=False, stop=(d == 1 and s == 0))
                        if s == 1:
                            for d in range(2):
                                last = mm(o, s0t[r, d * NT + q, :], qr[r, d, s, q, 1, :], start=False, stop=(d == 1))
                last.then_inc(S("y_mm"), 1)
            if s == 0:
                for d in range(2):
                    for q in range(NT):
                        g, qi = 2 * d + q // 2, q % 2
                        for h in range(2):
                            i = 2 * h + qi
                            r = slice(h * HS, (h + 1) * HS)
                            o = banks[6][r, (d * NT + q) * HS:(d * NT + q + 1) * HS]
                            mm(o, us[:, g, i, :], bkt[:, 0, d, q * P + h * HS:q * P + (h + 1) * HS], start=True, stop=False)
                            last = mm(o, vt[:, s, q * P + h * HS:q * P + (h + 1) * HS], bkt[:, 1, d, q * P + h * HS:q * P + (h + 1) * HS],
                                      start=False, stop=True)
                last.then_inc(S("state_mm"), 1)
        for m in range(16):
            c = C_MERGE + m // 2
            arrived(pe, c)
            if m >= 4:
                pe.wait_ge(S("merge_ready"), m - 3)
            for k in range(KT):
                last = mm(banks[m % 4][:, 0:TT], ring_in(c)[:, k, (m % 2) * P:(m % 2 + 1) * P], hnT[:, k, :],
                          start=(k == 0), stop=(k == KT - 1))
            last.then_inc(S("merge_mm"), 1)
            if m == 7:
                pe.wait_ge(S("y_evac"), 4)
                pe.wait_ge(S("state_copied"), 1)
                for q in range(NT):
                    last = mm(banks[(4, 6)[q // 2]][:, (q % 2) * TT:(q % 2 + 1) * TT], bmean[:], kk[:, q, :], start=True, stop=True)
                last.then_inc(S("mean_mm"), 1)
        pe.wait_ge(S("ysq_ready"), 1)
        for q in range(NT):
            last = mm(banks[(4, 6)[q // 2]][:, (q % 2) * TT:(q % 2 + 1) * TT], bmean[:], raw[:, q, :], start=True, stop=True)
        last.then_inc(S("var_mm"), 1)

        def branch(c0, src, bb, used, done):
            for m in range(KT):
                c = c0 + m // 4
                arrived(pe, c)
                if m >= 2:
                    pe.wait_ge(S(used), m - 1)
                for k in range(4):
                    last = mm(banks[bb + m % 2][:, 0:TT], ring_in(c)[:, k, (m % 4) * P:(m % 4 + 1) * P], src[:, k, :],
                              start=(k == 0), stop=(k == 3))
                last.then_inc(S(done), 1)

        pe.wait_ge(S("merge_ready"), 16)
        branch(C_POUT, pmT, 0, "pout_used", "pout_mm")
        pe.wait_ge(S("yn_ready"), 1)
        branch(C_ROUT, kk, 2, "rout_used", "rout_mm")

        pe.wait_ge(S("rout_used"), KT)
        for c in range(4):
            arrived(pe, C_WO + c)
            for s in range(NS):
                n = 2 * c + s
                if n >= 4:
                    pe.wait_ge(S("wo_used"), n - 3)
                for k in range(KT):
                    last = mm(banks[(0, 1, 5, 4)[n % 4]][:, 0:256], ms[:, k, s * T:(s + 1) * T], ring_in(C_WO + c)[:, k, :],
                              start=(k == 0), stop=(k == KT - 1))
                last.then_inc(S("wo_mm"), 1)

        for s in range(NS):
            pe.wait_ge(S("xn2_ready"), s + 1)
            for k in range(KT):
                last = tr(banks[k // 2][:, (k % 2) * TT + s * T:(k % 2) * TT + (s + 1) * T], xn2[:, s, k * P:(k + 1) * P], ident[:])
        last.then_inc(S("xn2T_done"), 1)
        pe.wait_ge(S("hn2_ready"), 2)
        pe.wait_ge(S("router_in"), 32)
        for s in range(NS):
            for k in range(KT):
                mm(banks[5][:, s * NE:(s + 1) * NE], hnT[:, k, s * T:(s + 1) * T], rtw[:, k, :], start=(k == 0), stop=False)
            last = mm(banks[5][:, s * NE:(s + 1) * NE], ones[0:1, :], rtb[:], start=False, stop=True)
        last.then_inc(S("logits_mm"), 1)
        for s in range(NS):
            for k in range(KT):
                last = tr(banks[2 * s + k // 4][:, (k % 4) * P:(k % 4 + 1) * P], hnT[:, k, s * T:(s + 1) * T], ident[:])
        last.then_inc(S("x2_mm"), 1)
        pe.wait_ge(S("sel_done"), 1)
        mm(banks[6][:, 0:NE], upp[:], sel[:, 0, :], start=True, stop=True)
        mm(banks[6][:, NE:2 * NE], upp[:], sel[:, 1, :], start=True, stop=False)
        mm(banks[6][:, NE:2 * NE], ones[:], sel[:, 0, :], start=False, stop=True)
        for s in range(NS):
            last = mm(banks[6][0:NE, 64:65], sel[:, s, :], ones[:, 0:1], start=(s == 0), stop=(s == 1))
        last.then_inc(S("rank_mm"), 1)
        for s in range(NS):
            last = tr(banks[7][0:NE, s * T:(s + 1) * T], comb[:, s, :], ident[:])
        last.then_inc(S("combT_mm"), 1)
        pe.wait_ge(S("extra_ready"), 1)
        mm(banks[6][0:NE, 65:66], upp[0:NE, 0:NE], cnt[:, 1:2], start=True, stop=True)
        mm(banks[6][:, 66:67], ones[0:NE, :], cnt[:, 1:2], start=True, stop=True).then_inc(S("pos_mm"), 1)
        pe.wait_ge(S("e16_ready"), 1)
        mm(banks[6][:, 96:96 + EXTRA], eidx[0:NE, :], e16[:, 0, :], start=True, stop=True)
        mm(banks[6][:, 128:128 + EXTRA], ones[0:NE, :], e16[:, 1, :], start=True, stop=True).then_inc(S("list_mm"), 1)

        def gather():
            for k in range(KT):
                for s in range(NS):
                    last = mm(banks[6][:, k * SLOTS:(k + 1) * SLOTS], x2t[:, s, k * P:(k + 1) * P], p2[:, s, 0:SLOTS],
                              start=(s == 0), stop=(s == NS - 1))
            last.then_inc(S("gathered"), 1)

        pe.wait_ge(S("items_ready"), 1)
        n_items = pe.value_load(item[0:1, ITEMS:ITEMS + 1], min_val=NE, max_val=NE + EXTRA)
        pe.wait_ge(S("x2_ready"), 4)
        pe.wait_ge(S("combT_ready"), 1)
        pe.wait_ge(S("bdn_in"), 16)
        for s in range(NS):
            for h in range(2):
                mm(banks[2 * s + h][:, :], combT[:, s * T:(s + 1) * T], bdn[:, h * 512:(h + 1) * 512], start=True, stop=True)
        pe.wait_ge(S("sel_ready"), 1)
        gather()
        pe.wait_ge(S("bgu_in"), 16)
        with pe.Fori(0, n_items) as it:
            G, L = banks[4], banks[5]
            pe.wait_ge(S("xg_ready"), it + 1)
            pe.wait_ge(S("sele_ready"), it + 1)
            for h in range(2):
                r = slice(h * SLOTS, (h + 1) * SLOTS)
                mm(G[r, :], sele, bgu[:, h * 512:(h + 1) * 512], start=True, stop=False)
                mm(L[r, :], sele, bgu[:, FF + h * 512:FF + (h + 1) * 512], start=True, stop=False)
            for j in range(GU_CHUNKS):
                pe.wait_ge(S(f"slot{j}_full"), it * 16 + 16 * (FRONT_USES[j] + 1))
                for b, o in ((G, 0), (L, FF)):
                    for h in range(2):
                        last = mm(b[h * SLOTS:(h + 1) * SLOTS, :], xg[:, j, :], ring[:, j, o + h * 512:o + (h + 1) * 512],
                                  start=False, stop=(j == GU_CHUNKS - 1))
                last.then_inc(S("chunk_used"), 1)
            pe.wait_ge(S("sel_ready"), it + 2)
            gather()
            pe.wait_ge(S("pw_ready"), it + 1)
            for s in range(NS):
                last = tr(banks[7][:, s * T:(s + 1) * T], pw[:, s, :], ident[:])
            last.then_inc(S("pwt_done"), 1)
            pe.wait_ge(S("act_ready"), it + 1)
            for j in range(4):
                last = tr(L[:, j * P:(j + 1) * P], act_[:, j * P:(j + 1) * P], ident[:])
            last.then_inc(S("actT_done"), 1)
            pe.wait_ge(S("actT_ready"), it + 1)
            for j in range(DN_CHUNKS):
                pe.wait_ge(S(f"slot{GU_CHUNKS + j}_full"), it * 16 + 16 * (FRONT_USES[GU_CHUNKS + j] + 1))
                for i in range(2):
                    c = 2 * j + i
                    for h in range(2):
                        last = mm(G[h * SLOTS:(h + 1) * SLOTS, :], actT[:, c % 4, c // 4, :],
                                  ring[:, GU_CHUNKS + j, i * D + h * 512:i * D + (h + 1) * 512],
                                  start=(c == 0), stop=(c == 7))
                last.then_inc(S("chunk_used"), 1)
            pe.wait_ge(S("pwt_ready"), it + 1)
            pe.wait_ge(S("ysb_ready"), it + 1)
            for s in range(NS):
                for h in range(2):
                    r = slice(h * SLOTS, (h + 1) * SLOTS)
                    last = mm(banks[2 * s + h][:, :], pwt[r, s, :], ysb[r, :], start=False, stop=True, skip_group_check=True)
            last.then_inc(S("scattered"), 1)

    @block.scalar
    def _(act):
        af = nc.scalar.activation

        act.wait_ge(S("x_in"), 32)
        act.wait_ge(S("ident_ready"), 1)
        for s in range(NS):
            af(junk[:, s, :], x[:, s, :], ACT.Square, accum_out=stat[:, s:s + 1]).then_inc(S("sq_done"), 1)
        act.wait_ge(S("sq_done"), 2)
        af(stat[:, 2:4], stat[:, 0:2], ACT.Sqrt, bias=epsr[:], scale=1.0 / D).then_inc(S("rms1_ready"), 1)
        act.wait_ge(S("prm_ready"), 1)
        af(csig[:].rearrange("p s k -> p (s k)"), prm[:, 0:16], ACT.Sigmoid).then_inc(S("csig_ready"), 1)
        act.wait_ge(S("xnT_done"), 1)
        act.wait_ge(S("moda_ready"), 1)
        for k in range(4):
            for s in range(NS):
                o = (k % 2) * TT + s * T
                last = af(hnT[:, k, s * T:(s + 1) * T], banks[1 + k // 2][:, o:o + T], ACT.Identity,
                          bias=moda[:, 0, k, s:s + 1], scale=moda[:, 1, k, s:s + 1])
        last.then_inc(S("hn_ready"), 1)
        for ct in range(RTILES):
            act.wait_ge(S("proj_done"), ct + 1)
            if ct >= 4:
                act.wait_ge(S("mix_done"), ct - 3)
            af(raw[:, ct % 4, :], PB[ct % 4][:, 0:TT], ACT.Copy).then_inc(S("raw_copied"), 1)
        act.wait_ge(S("mix_done"), RTILES)
        af(pr[:, 12, :], pr[:, 12, :], ACT.Tanh)
        af(pr[:, 14, :], pr[:, 14, :], ACT.Sigmoid).then_inc(S("th_ready"), 1)
        for n in range(4):
            act.wait_ge(S("z_done"), n + 1)
            af(sig[:, n // 2, n % 2, :], PB[n][:, :], ACT.Sigmoid).then_inc(S("sig_ready"), 1)
        for j in range(4):
            d = j // 2
            act.wait_ge(S("a_done"), j + 1)
            for q in range(2 * (j % 2), 2 * (j % 2) + 2):
                last = af(aa[:, d, q, :], PB[j][:, (q % 2) * TT:(q % 2 + 1) * TT], ACT.Sigmoid,
                          bias=prb[:, 19 + 4 * d + q:20 + 4 * d + q])
            last.then_inc(S("a_ready"), 1)
        act.wait_ge(S("gate_done"), 1)
        for j in range(2):
            af(gate[:, 2 * j:2 * j + 2, :].rearrange("p c t -> p (c t)"), banks[2 + j][:, :], ACT.Copy).then_inc(S("gate_ready"), 1)
        act.wait_ge(S("norm_done"), 1)
        for j in range(2):
            af(raw[:, 2 * j:2 * j + 2, :].rearrange("p c t -> p (c t)"), PB[j][:, :], ACT.Sqrt).then_inc(S("nrm_ready"), 1)
        for i in range(8):
            d, s, t2 = i // 4, (i // 2) % 2, i % 2
            act.wait_ge(S("cum_done"), i + 1)
            ps = banks[CB[i % 4]][:].rearrange("p (q k t) -> p q k t", q=2, k=2)
            af(qr[:, d, s, 2 * t2:2 * t2 + 2, :, :].rearrange("p q k t -> p (q k t)"), banks[CB[i % 4]][:, :], ACT.Exp, scale=-DECAY)
            if s == 1:
                t0 = 0 if d == 0 else T - 1
                af(pms[:, d * NT + 2 * t2:d * NT + 2 * t2 + 2], ps[:, :, 0, t0], ACT.Exp, scale=DECAY)
            af(bt[:, d, s, 2 * t2:2 * t2 + 2, :], ps[:, :, 1, :], ACT.Exp, scale=DECAY).then_inc(S("cum_used"), 1)
        for n in range(8):
            s, tp, d = n // 4, (n // 2) % 2, n % 2
            g = 2 * d + tp
            act.wait_ge(S("z_mm"), n + 1)
            for h in range(2):
                last = af(zs[:, d, 2 * h:2 * h + 2, :].rearrange("p i v -> p (i v)"), banks[(3, 7)[h]][:, 0:2 * HS], ACT.Copy, scale=-1.0)
            last.then_inc(S("z_evac"), 1)
            act.wait_ge(S("u_mm"), n + 1)
            af(us[:, g, :, :].rearrange("p i v -> p (i v)"), banks[4][:, 0:4 * HS], ACT.Copy).then_inc(S("u_evac"), 1)
            if n == 3:
                act.wait_ge(S("state_mm"), 1)
                af(so.rearrange("p c k -> p (c k)"), banks[6][:, :], ACT.Copy).then_inc(S("state_copied"), 1)
                act.wait_ge(S("state_copied"), 1)
                for dd in range(2):
                    for h in range(2):
                        act.dma_start(O[2 + dd][0, 0].rearrange("(q h) v k -> h v q k", h=2)[h],
                                      so[h * HS:(h + 1) * HS, dd * NT:(dd + 1) * NT, :]).then_inc(S("stored"), 16)
        for m in range(16):
            act.wait_ge(S("merge_mm"), m + 1)
            af(merge[:, m, :], banks[m % 4][:, 0:TT], ACT.Sigmoid, bias=prm[:, 80 + m:81 + m]).then_inc(S("merge_ready"), 1)
        act.wait_ge(S("var_mm"), 1)
        for j in range(2):
            af(raw[:, 2 * j:2 * j + 2, :].rearrange("p c t -> p (c t)"), banks[(4, 6)[j]][:, :], ACT.Sqrt, bias=epsg[:]).then_inc(S("gstd_ready"), 1)
        act.wait_ge(S("wo_used"), 8)
        for s in range(NS):
            af(x2t[:, s, :], x[:, s, :], ACT.Square, accum_out=stat[:, 4 + s:5 + s]).then_inc(S("sq_done"), 1)
        act.wait_ge(S("sq_done"), 4)
        af(stat[:, 6:8], stat[:, 4:6], ACT.Sqrt, bias=epsr[:], scale=1.0 / D).then_inc(S("rms2_ready"), 1)
        act.wait_ge(S("xn2T_done"), 1)
        act.wait_ge(S("gcol_ready"), 1)
        for k in range(4):
            for s in range(NS):
                o = (k % 2) * TT + s * T
                last = af(hnT[:, k, s * T:(s + 1) * T], banks[k // 2][:, o:o + T], ACT.Identity,
                          bias=modb[:, 1, k, s:s + 1], scale=modb[:, 2, k, s:s + 1])
        last.then_inc(S("hn2_ready"), 1)
        act.wait_ge(S("x2_mm"), 1)
        for j in range(2):
            af(x2t[:, 0, j * 512:(j + 1) * 512], banks[j][:, :], ACT.Copy).then_inc(S("x2_ready"), 1)
        act.wait_ge(S("top_ready"), 1)
        for s in range(NS):
            last = af(tw[:, s, :], top8[:, s, 0:4], ACT.Exp, bias=fstat[:, s:s + 1])
        last.then_inc(S("exp_ready"), 1)
        act.wait_ge(S("combT_mm"), 1)
        af(combT[:], banks[7][0:NE, 0:TT], ACT.Copy).then_inc(S("combT_ready"), 1)

        act.wait_ge(S("items_ready"), 1)
        n_items = act.value_load(item[0:1, ITEMS:ITEMS + 1], min_val=NE, max_val=NE + EXTRA)

        def gathered_out(n):
            act.wait_ge(S("gathered"), n)
            af(xg.rearrange("p k s -> p (k s)"), banks[6][:, :], ACT.Copy).then_inc(S("xg_ready"), 1)

        gathered_out(1)
        with act.Fori(0, n_items) as it:
            act.wait_ge(S("g_ready"), it + 1)
            af(sgb, gsb, ACT.Sigmoid, scale=ALPHA).then_inc(S("sg_ready"), 1)
            gathered_out(it + 2)
            act.wait_ge(S("pwt_done"), it + 1)
            af(pwt.rearrange("p s t -> p (s t)"), banks[7][:, 0:TT], ACT.Copy).then_inc(S("pwt_ready"), 1)
            act.wait_ge(S("chunk_used"), it * RING + RING)
            af(ysb, banks[4][:, :], ACT.Copy).then_inc(S("ysb_ready"), 1)

        act.wait_ge(S("res_ready"), 1)
        for s in range(NS):
            af(hnT[:, 4 * s:4 * s + 4, :].rearrange("p k t -> p (k t)"), x[:, s, :], ACT.Square, accum_out=fstat[:, s:s + 1]).then_inc(S("sq_done"), 1)
        act.wait_ge(S("sq_done"), 6)
        af(fstat[:, 2:4], fstat[:, 0:2], ACT.Sqrt, bias=epsr[:], scale=1.0 / D).then_inc(S("rms3_ready"), 1)
        for s in range(NS):
            act.wait_ge(S("out_ready"), s + 1)
            act.dma_start(O[s][0], x[:, s, :]).then_inc(S("stored"), 16)

    @block.vector
    def _(dve):
        v = nc.vector
        MUL, ADD, SUB = ALU.mult, ALU.add, ALU.subtract
        n = [0]

        def step(ins):
            n[0] += 1
            ins.then_inc(S("dve_step"), 1)

        def sync():
            dve.wait_ge(S("dve_step"), n[0])

        def own(ins):
            step(ins)
            sync()

        def last_of(name, count):
            dve.wait_ge(S(name), count)

        def bc(ap, m):
            return ap.unsqueeze(1).to_broadcast([P, m, ap.shape[-1]])

        def col(ap, m):
            return ap.unsqueeze(2).to_broadcast([P, ap.shape[-1], m])

        dve.wait_ge(S("prmT_done"), 1)
        v.tensor_copy(prm[:], banks[0][:, 0:96]).then_inc(S("prm_ready"), 1)
        dve.wait_ge(S("rms1_ready"), 1)
        own(v.reciprocal(stat[:, 0:2], stat[:, 2:4]))
        for s in range(NS):
            v.tensor_scalar(xn[:, s, :], x[:, s, :], stat[:, s:s + 1], None, MUL).then_inc(S("xn_ready"), 1)
        last_of("prm_ready", 1)
        dve.wait_ge(S("csig_ready"), 1)
        v.tensor_tensor(cvec[:].rearrange("p s k -> p (s k)"), prm[:, 0:16], csig[:].rearrange("p s k -> p (s k)"), MUL).then_inc(S("cvec_ready"), 1)
        own(v.reduce_sum(par4[:], ident[:].rearrange("p (n j) -> p j n", j=4), axis=AX.X))
        own(v.tensor_tensor(par2[:], par4[:, 0:2], par4[:, 2:4], ADD))
        dve.wait_ge(S("prbT_done"), 1)
        own(v.tensor_copy(prb[:], banks[0][:, 128:183]))
        m15 = prb[:, 0:RTILES]
        step(v.tensor_scalar(mu[:, 0, :], m15, -1.0, 1.0, MUL, ADD))
        for j in range(2):
            step(v.tensor_scalar(mu[:, 1 + j, :], m15, par2[:, j:j + 1], None, MUL))
        for j in range(4):
            step(v.tensor_scalar(mu[:, 3 + j, :], m15, par4[:, j:j + 1], None, MUL))
        v.tensor_scalar(kam[:], prb[:, 31:35], -1.0, 1.0, MUL, ADD).then_inc(S("prb_ready"), 1)
        dve.wait_ge(S("moda_mm"), 8)
        own(v.tensor_tensor(moda[:].rearrange("p g k s -> p (g k) s"), banks[5][:, 0:32].rearrange("p (g s) -> p g s", s=NS),
                            col(prm[:, 16:32], NS), ADD))
        v.scalar_tensor_tensor(moda[:, 1, :, :], moda[:, 1, :, :], 1.0, col(prm[:, 64:72], NS), ADD, MUL).then_inc(S("moda_ready"), 1)
        last_of("moda_ready", 1)
        dve.wait_ge(S("xnT_done"), 1)
        for k in range(4, KT):
            for s in range(NS):
                o = (k % 2) * TT + s * T
                last = v.tensor_scalar(hnT[:, k, s * T:(s + 1) * T], banks[1 + k // 2][:, o:o + T], moda[:, 1, k, s:s + 1],
                                       moda[:, 0, k, s:s + 1], MUL, ADD)
        last.then_inc(S("hn_ready"), 1)
        dve.wait_ge(S("masks_ready"), 1)
        prev = ident[:]
        for i in range(7):
            m = 2 ** (i + 1)
            if m < P:
                dve.wait_ge(S("bd_ready"), i + 1)
                cur = bdm[:, (i + 1) % 2, :]
            else:
                cur = ones[:]
            own(v.tensor_tensor(lvl[:, i, 0, :], cur, prev, SUB))
            step(v.tensor_tensor(lvl[:, i, 1, :], lvl[:, i, 0, :], upp[:], MUL))
            v.tensor_tensor(lvl[:, i, 0, :], lvl[:, i, 0, :], low, MUL).then_inc(S("bd_used"), 1)
            prev = cur
        step(v.tensor_scalar(tri[:, 0, :, :], mqr[:, 0, :, :], rowlo[:], None, SUB))
        v.tensor_scalar(tri[:, 1, :, :], mqr[:, 1, :, :], rowlo[:], -1.0, ADD, ADD).then_inc(S("tri_ready"), 1)

        last_of("prb_ready", 1)
        sync()
        for ct in range(RTILES):
            dve.wait_ge(S("raw_copied"), ct + 1)
            r_ = raw[:, ct % 4, :]
            o_ = pr[:, ct, :]
            own(v.tensor_scalar(o_, r_, mu[:, 0, ct:ct + 1], None, MUL))

            def add(dst, src, j):
                return v.scalar_tensor_tensor(dst, src, mu[:, j, ct:ct + 1], dst, MUL, ADD)

            og, rg = o_[:, T:TT].rearrange("p (r c) -> p r c", c=GRID_W), r_[:, T:TT].rearrange("p (r c) -> p r c", c=GRID_W)
            step(add(o_[:, 1:T], r_[:, 0:T - 1], 1))
            own(add(og[:, :, 1:], rg[:, :, :-1], 3))
            step(add(o_[:, 0:T - 1], r_[:, 1:T], 2))
            own(add(og[:, :, :-1], rg[:, :, 1:], 4))
            own(add(og[:, 1:, :], rg[:, :-1, :], 5))
            add(og[:, :-1, :], rg[:, 1:, :], 6).then_inc(S("mix_done"), 1)
        last_of("mix_done", RTILES)

        dve.wait_ge(S("pcnt_done"), 1)
        cbuf = corr[:].rearrange("p c t -> p (c t)")[:, 0:512]
        pbf = pband.rearrange("p g t -> p (g t)")
        own(v.reciprocal(cbuf, banks[4][:, :]))
        own(v.tensor_tensor(pbf, pbf, cbuf, MUL))
        v.tensor_tensor(pband, pband, bc(ident[:], 4), SUB).then_inc(S("pband_ready"), 1)
        dve.wait_ge(S("pu_mm"), 2)
        for s in range(NS):
            v.tensor_copy(utok[:, s, :], banks[2 + s][:, :]).then_inc(S("utok_ready"), 1)
        for q in range(NT):
            step(v.tensor_scalar(kk[:, q, :], pr[:, 4 + q, :], prb[:, 27 + q:28 + q], None, MUL))
        sync()
        v.tensor_tensor(raw[:], kk[:], kk[:], MUL).then_inc(S("ksq_ready"), 1)
        dve.wait_ge(S("pooled_done"), 1)
        for j in range(2):
            v.tensor_copy(pooled[:, 2 * j:2 * j + 2, :].rearrange("p g t -> p (g t)"), banks[2 + j][:, :]).then_inc(S("pooled_ready"), 1)
        dve.wait_ge(S("mixed_done"), 1)
        for j in range(2):
            for g in (2 * j, 2 * j + 1):
                last = v.tensor_scalar(pmT[:, g, :], banks[(1, 4)[j]][:, (g % 2) * TT:(g % 2 + 1) * TT], prb[:, 15 + g:16 + g], None, MUL)
            last.then_inc(S("mixed_ready"), 1)
        dve.wait_ge(S("a_ready"), 4)
        for d in range(2):
            for q in range(NT):
                step(v.tensor_scalar(kd[:, d, q, :], aa[:, d, q, :], prb[:, 31 + q:32 + q], kam[:, q:q + 1], MUL, ADD))
        sync()
        for d in range(2):
            step(v.tensor_tensor(kd[:, d, :, :], kd[:, d, :, :], pr[:, 4:8, :], MUL))
        dve.wait_ge(S("vt_done"), 1)
        for s in range(NS):
            v.tensor_copy(vt[:, s, :], banks[6 + s][:, :]).then_inc(S("vt_ready"), 1)
        dve.wait_ge(S("nrm_ready"), 2)
        own(v.tensor_scalar(raw[:], raw[:], 1e-12, None, ALU.max))
        own(v.reciprocal(raw[:], raw[:]))
        v.tensor_tensor(kk[:], kk[:], raw[:], MUL).then_inc(S("kk_ready"), 1)
        last_of("kk_ready", 1)
        own(v.tensor_tensor(raw[:], kd[:, 0, :, :], kd[:, 1, :, :], ADD))
        own(v.tensor_tensor(raw[:], raw[:], pr[:, 0:4, :], MUL))
        for q in range(NT):
            last = v.tensor_scalar(raw[:, q, :], raw[:, q, :], prb[:, 35 + q:36 + q], None, MUL)
        last.then_inc(S("rkk_ready"), 1)
        dve.wait_ge(S("rk_done"), 1)
        for j in range(2):
            step(v.tensor_tensor(corr[:, 2 * j:2 * j + 2, :].rearrange("p c t -> p (c t)"), pr[:, 8 + 2 * j:10 + 2 * j, :].rearrange("p c t -> p (c t)"),
                                 banks[2 + j][:, :], MUL))

        dve.wait_ge(S("cum_used"), 8)
        dve.wait_ge(S("s0_done"), 1)
        own(v.tensor_tensor(s0t[:], banks[1][:].rearrange("p (i v) -> p i v", v=HS), col(pms[:], HS), MUL))
        step(v.tensor_copy(fin[:, 0, :], qr[:, 0, 0, :, 1, T - 1]))
        own(v.tensor_copy(fin[:, 1, :], qr[:, 1, 0, :, 1, 0]))
        for s in range(NS):
            ts = slice(s * T, (s + 1) * T)
            for d in range(2):
                step(v.tensor_tensor(qr[:, d, s, :, 0, :], qr[:, d, s, :, 0, :], kk[:, :, ts], MUL))
                step(v.tensor_tensor(qr[:, d, s, :, 1, :], qr[:, d, s, :, 1, :], pr[:, 0:4, ts], MUL))
                step(v.tensor_tensor(kt_[:, d, s, :, :], bt[:, d, s, :, :], kd[:, d, :, ts], MUL))
                own(v.tensor_tensor(bt[:, d, s, :, :], bt[:, d, s, :, :], aa[:, d, :, ts], MUL))
                last = v.tensor_tensor(bt[:, d, s, :, :], bt[:, d, s, :, :], kk[:, :, ts], MUL)
                if d == 0:
                    step(last)
            last.then_inc(S("scan_ops_ready"), 1)
            last_of("scan_ops_ready", s + 1)
        dve.wait_ge(S("modb_mm"), 16)
        own(v.tensor_tensor(modb[:].rearrange("p g k s -> p (g k) s"), banks[5][:, 0:64].rearrange("p (g s) -> p g s", s=NS),
                            col(prm[:, 32:64], NS), ADD))
        step(v.scalar_tensor_tensor(modb[:, 2, :, :], modb[:, 2, :, :], 1.0, col(prm[:, 72:80], NS), ADD, MUL))
        for gi, m in enumerate((0, 3)):
            last = v.tensor_copy(gcol[:, gi, :, :], modb[:, m, :, :].rearrange("p k s -> p s k"))
            if gi == 0:
                step(last)
        last.then_inc(S("gcol_ready"), 1)
        dve.wait_ge(S("grow_done"), 1)
        v.tensor_copy(grow[:], banks[5][0:32, 128:256]).then_inc(S("grow_ready"), 1)
        for j, src in enumerate((bt, kt_)):
            for d in range(2):
                if j:
                    dve.wait_ge(S("bk_done"), d + 1)
                v.tensor_tensor(bfin[:, d, :, :], src[:, d, 0, :, :], col(fin[:, d, :], T), MUL).then_inc(S("bf_ready"), 1)
            for d in range(2):
                dve.wait_ge(S("bk_done"), 2 * j + d + 1)
                v.tensor_copy(bkt[:, j, d, :], banks[2 + d][:, :]).then_inc(S("bk_ready"), 1)

        def b4(i):
            return banks[i][:].rearrange("p (i t) -> p i t", i=4)

        for s in range(NS):
            for g in range(4):
                d = g // 2
                ba, bat = 2 * (g % 2), 2 * (g % 2) + 1
                dve.wait_ge(S("a_mm"), 4 * s + g + 1)
                for h, b in enumerate((ba, bat)):
                    hs = slice(2 * h, 2 * h + 2)
                    step(v.tensor_tensor(work[:, g, W_M, hs, :], b4(b)[:, 0:2, :], bc(lvl[:, 0, d, :], 2), MUL))
                    step(v.tensor_tensor(work[:, g, W_AT, hs, :], b4(b)[:, 2:4, :], bc(mqr[:, d, 0, :], 2), MUL))
                sync()
                step(v.tensor_tensor(work[:, g, W_X, :, :], bc(ident[:], 4), work[:, g, W_M, :, :], SUB))
                own(v.tensor_tensor(work[:, g, W_XT, :, :], work[:, g, W_AT, :, :], bc(lvl[:, 0, 1 - d, :], 4), MUL))
                v.tensor_tensor(work[:, g, W_XT, :, :], bc(ident[:], 4), work[:, g, W_XT, :, :], SUB).then_inc(S("a_evac"), 1)
            last_of("a_evac", 4 * s + 4)
            for l in range(1, 7):
                for g in range(4):
                    dve.wait_ge(S("m_mm"), 24 * s + 4 * (l - 1) + g + 1)
                    v.tensor_tensor(work[:, g, W_M, :, :], b4(4 + g % 2), bc(lvl[:, l, g // 2, :], 4), MUL).then_inc(S("m_evac"), 1)
                for g in range(4):
                    dve.wait_ge(S("x_mm"), 24 * s + 4 * (l - 1) + g + 1)
                    bx, bxt = XB[g % 2]
                    if l < 6:
                        step(v.tensor_tensor(work[:, g, W_X, :, :], work[:, g, W_X, :, :], b4(bx), SUB))
                    v.tensor_tensor(work[:, g, W_XT, :, :], work[:, g, W_XT, :, :], b4(bxt), SUB).then_inc(S("x_upd"), 1)
                last_of("x_upd", 24 * s + 4 * l)
            for tp in range(2):
                for d in range(2):
                    g = 2 * d + tp
                    dve.wait_ge(S("kq_mm"), 4 * s + 2 * tp + d + 1)
                    for j in range(2):
                        step(v.tensor_tensor(kqm(g)[:, 2 * j:2 * j + 2, :, :].rearrange("p i k t -> p i (k t)"),
                                             banks[j][:].rearrange("p (i c) -> p i c", i=2),
                                             bc(mqr[:, d, :, :].rearrange("p k t -> p (k t)"), 2), MUL))
                    for h in range(2):
                        last = v.tensor_tensor(work[:, g, W_AT, 2 * h:2 * h + 2, :], b4((2, 6)[h])[:, 0:2, :], bc(mqr[:, d, 1, :], 2), MUL)
                    last.then_inc(S("kq_evac"), 1)
                dve.wait_ge(S("y_mm"), 2 * s + tp + 1)
                v.tensor_tensor(kk[:, 2 * tp:2 * tp + 2, s * T:(s + 1) * T], banks[5][:, 0:2 * T].rearrange("p (q t) -> p q t", q=2),
                                corr[:, 2 * tp:2 * tp + 2, s * T:(s + 1) * T], ADD).then_inc(S("y_evac"), 1)

        last_of("y_evac", 4)
        dve.wait_ge(S("mean_mm"), 1)

        def pair(ap, j):
            return ap[:, 2 * j:2 * j + 2, :].rearrange("p c t -> p (c t)")

        for j in range(2):
            step(v.tensor_tensor(pair(kk, j), pair(kk, j), banks[(4, 6)[j]][:, :], SUB))
        sync()
        dve.wait_ge(S("stored"), 64)
        v.tensor_tensor(raw[:], kk[:], kk[:], MUL).then_inc(S("ysq_ready"), 1)
        dve.wait_ge(S("gstd_ready"), 2)
        own(v.reciprocal(raw[:], raw[:]))
        own(v.tensor_tensor(kk[:], kk[:], raw[:], MUL))
        for q in range(NT):
            step(v.tensor_scalar(kk[:, q, :], kk[:, q, :], prb[:, 39 + q:40 + q], prb[:, 43 + q:44 + q], MUL, ADD))
        sync()
        v.tensor_tensor(kk[:], kk[:], gate[:], MUL).then_inc(S("yn_ready"), 1)
        for m in range(KT):
            dve.wait_ge(S("pout_mm"), m + 1)
            v.tensor_tensor(ms[:, m, :], merge[:, m, :], banks[m % 2][:, 0:TT], MUL).then_inc(S("pout_used"), 1)
        last_of("yn_ready", 1)
        last_of("pout_used", KT)
        for m in range(KT):
            dve.wait_ge(S("rout_mm"), m + 1)
            own(v.tensor_tensor(gate[:, m % 4, :], merge[:, KT + m, :], banks[2 + m % 2][:, 0:TT], MUL))
            v.tensor_tensor(ms[:, m, :], ms[:, m, :], gate[:, m % 4, :], ADD).then_inc(S("rout_used"), 1)
        dve.wait_ge(S("gbc_in"), 32)
        for c in range(4):
            for s in range(NS):
                i = 2 * c + s
                dve.wait_ge(S("wo_mm"), i + 1)
                cs = slice(256 * c, 256 * c + 256)
                own(v.tensor_tensor(corr[:, i % 4, :], banks[(0, 1, 5, 4)[i % 4]][:, 0:256], gbc[:, s, cs], MUL))
                v.tensor_tensor(x[:, s, cs], x[:, s, cs], corr[:, i % 4, :], ADD).then_inc(S("wo_used"), 1)
        last_of("wo_used", 8)
        dve.wait_ge(S("rms2_ready"), 1)
        own(v.reciprocal(stat[:, 4:6], stat[:, 6:8]))
        for s in range(NS):
            v.tensor_scalar(xn2[:, s, :], x[:, s, :], stat[:, 4 + s:5 + s], None, MUL).then_inc(S("xn2_ready"), 1)
        dve.wait_ge(S("xn2T_done"), 1)
        last_of("gcol_ready", 1)
        for k in range(4, KT):
            for s in range(NS):
                o = (k % 2) * TT + s * T
                last = v.tensor_scalar(hnT[:, k, s * T:(s + 1) * T], banks[k // 2][:, o:o + T], modb[:, 2, k, s:s + 1],
                                       modb[:, 1, k, s:s + 1], MUL, ADD)
        last.then_inc(S("hn2_ready"), 1)

        dve.wait_ge(S("logits_mm"), 1)
        own(v.tensor_copy(lg[:].rearrange("p s e -> p (s e)"), banks[5][:, 0:NS * NE]))
        for s in range(NS):
            own(v.max(top8[:, s, :], lg[:, s, :]))
            own(v.max_index(idx8[:, s, :], top8[:, s, :], lg[:, s, :]))
        step(v.tensor_copy(idxf[:], idx8[:]))
        v.tensor_scalar(fstat[:, 0:2], top8[:, :, 0], -1.0, None, MUL).then_inc(S("top_ready"), 1)
        dve.wait_ge(S("x2_mm"), 1)
        for j in range(2):
            v.tensor_copy(x2t[:, 1, j * 512:(j + 1) * 512], banks[2 + j][:, :]).then_inc(S("x2_ready"), 1)
        dve.wait_ge(S("exp_ready"), 1)
        own(v.reduce_sum(fstat[:, 2:4], tw[:], axis=AX.X))
        own(v.reciprocal(fstat[:, 2:4], fstat[:, 2:4]))
        for s in range(NS):
            own(v.tensor_scalar(twn[:, s, :], tw[:, s, :], fstat[:, 2 + s:3 + s], None, MUL))
        dve.wait_ge(S("lists_ready"), 1)
        for s in range(NS):
            for j in range(4):
                d0, d1 = (sel[:, s, :], comb[:, s, :]) if j == 0 else (oh[:], lg[:, s, :])
                step(v.tensor_scalar(d0, iota2[:, 0:NE], idxf[:, s, j:j + 1], None, ALU.is_equal))
                own(v.tensor_scalar(d1, iota2[:, 0:NE], idxf[:, s, j:j + 1], twn[:, s, j:j + 1], ALU.is_equal, MUL))
                if j:
                    step(v.tensor_tensor(sel[:, s, :], sel[:, s, :], oh[:], ADD))
                    own(v.tensor_tensor(comb[:, s, :], comb[:, s, :], lg[:, s, :], ADD))
        v.tensor_copy(oh[:], sel[:, 0, :]).then_inc(S("sel_done"), 1)
        dve.wait_ge(S("rank_mm"), 1)
        own(v.scalar_tensor_tensor(rank[:], banks[6][:, 0:2 * NE].rearrange("p (s e) -> p s e", s=NS), 1.0, sel[:], ADD, MUL))
        step(v.tensor_scalar(rank[:], rank[:], -1.0, None, ADD))
        own(v.tensor_copy(cnt[:, 0:1], banks[6][0:NE, 64:65]))
        own(v.tensor_scalar(fl[:], thr3[0:NE, :], cnt[:, 0:1], None, ALU.is_lt))
        v.reduce_sum(cnt[:, 1:2], fl[:], axis=AX.X).then_inc(S("extra_ready"), 1)
        dve.wait_ge(S("pos_mm"), 1)
        own(v.tensor_copy(cnt[:, 2:3], banks[6][0:NE, 65:66]))
        own(v.tensor_scalar(posc[:], iota3[0:NE, :], cnt[:, 2:3], None, ADD))
        for c in range(3):
            own(v.tensor_scalar(oh16[:, c, :], iota2[0:NE, 0:EXTRA], posc[:, c:c + 1], fl[:, c:c + 1], ALU.is_equal, MUL))
        step(v.tensor_tensor(e16[:, 0, :], oh16[:, 0, :], oh16[:, 1, :], ADD))
        own(v.scalar_tensor_tensor(e16[:, 1, :], oh16[:, 1, :], 2.0, oh16[:, 0, :], MUL, ADD))
        step(v.tensor_tensor(e16[:, 0, :], e16[:, 0, :], oh16[:, 2, :], ADD))
        own(v.scalar_tensor_tensor(e16[:, 1, :], oh16[:, 2, :], 3.0, e16[:, 1, :], MUL, ADD))
        v.tensor_scalar(e16[:, 1, :], e16[:, 1, :], float(SLOTS), None, MUL).then_inc(S("e16_ready"), 1)
        dve.wait_ge(S("list_mm"), 1)
        step(v.tensor_copy(item[0:1, NE:NE + EXTRA], banks[6][0:1, 96:96 + EXTRA]))
        step(v.tensor_copy(base[:, NE:NE + EXTRA], banks[6][:, 128:128 + EXTRA]))
        own(v.tensor_scalar(item[0:1, ITEMS:ITEMS + 1], banks[6][0:1, 66:67], float(NE), None, ADD))

        def choose(n, e):
            for s in range(NS):
                last = v.tensor_scalar(p2[:, s, :], iota2[:], base[:, bass.ds(n, 1)], rank[:, s, bass.ds(e, 1)], ADD, ALU.is_equal)
            last.then_inc(S("sel_ready"), 1)

        def expert_row(e):
            v.tensor_copy(sele, ident[0:NE, bass.ds(e, 1)].to_broadcast([NE, SLOTS])).then_inc(S("sele_ready"), 1)

        v.tensor_copy(oh[:], sel[:, 0, :]).then_inc(S("items_ready"), 1)
        dve.wait_ge(S("items_ready"), 1)
        n_items = dve.value_load(item[0:1, ITEMS:ITEMS + 1], min_val=NE, max_val=NE + EXTRA)
        dve.wait_ge(S("combT_mm"), 1)
        choose(0, 0)
        expert_row(0)
        with dve.Fori(0, n_items) as it:
            e = dve.value_load(item[0:1, bass.ds(it, 1)], min_val=0, max_val=NE - 1)
            nxt = dve.value_load(item[0:1, bass.ds(it + 1, 1)], min_val=0, max_val=NE - 1)
            dve.wait_ge(S("sel_ready"), it + 1)
            for s in range(NS):
                last = v.tensor_scalar(pw[:, s, :], p2[:, s, :], comb[:, s, bass.ds(e, 1)], None, MUL)
            last.then_inc(S("pw_ready"), 1)
            dve.wait_ge(S("pw_ready"), it + 1)
            dve.wait_ge(S("gathered"), it + 1)
            choose(it + 1, nxt)
            dve.wait_ge(S("chunk_used"), it * RING + GU_CHUNKS)
            v.tensor_scalar(gsb, banks[4][:, :], LIMIT, None, ALU.min).then_inc(S("g_ready"), 1)
            v.tensor_scalar(lcb, banks[5][:, :], LIMIT, -LIMIT, ALU.min, ALU.max).then_inc(S("lin_done"), 1)
            expert_row(nxt)
            dve.wait_ge(S("lin_done"), it + 1)
            v.scalar_tensor_tensor(lcb, lcb, 1.0, gsb, ADD, MUL).then_inc(S("gl_done"), 1)
            dve.wait_ge(S("gl_done"), it + 1)
            dve.wait_ge(S("sg_ready"), it + 1)
            v.tensor_tensor(act_, lcb, sgb, MUL).then_inc(S("act_ready"), 1)
            dve.wait_ge(S("actT_done"), it + 1)
            v.tensor_copy(actT.rearrange("p j h s -> p (j h s)"), banks[5][:, :]).then_inc(S("actT_ready"), 1)

        dve.wait_ge(S("scattered"), n_items)
        dve.wait_ge(S("gbc_in"), 64)
        dve.wait_ge(S("wfin_in"), 16)
        for s in range(NS):
            for h in range(2):
                cs = slice(512 * h, 512 * h + 512)
                step(v.tensor_tensor(gbc[:, s, cs], gbc[:, s, cs], banks[2 * s + h][:, :], MUL))
        sync()
        v.tensor_tensor(x[:], x[:], gbc, ADD).then_inc(S("res_ready"), 1)
        last_of("res_ready", 1)
        dve.wait_ge(S("rms3_ready"), 1)
        own(v.reciprocal(fstat[:, 2:4], fstat[:, 2:4]))
        for s in range(NS):
            v.scalar_tensor_tensor(x[:, s, :], x[:, s, :], fstat[:, 2 + s:3 + s], wbuf, MUL, MUL).then_inc(S("out_ready"), 1)

    return ctx


_INS = ['x_prompt', 'x_sample', 'state_fwd', 'state_bwd', 'c', 'c_ctx', 'w_mod', 'b_mod', 'norm_mix_w', 'w_in', 'b_merge',
        'pool_w', 'pool_scale', 'w_pool_out', 'shift_mu', 'decay_w0', 'decay_w2', 'iclr_a0', 'iclr_a2', 'gate_w2',
        'k_k', 'k_a', 'r_k', 'ln_x_w', 'ln_x_b', 'w_rwkv_out', 'w_o', 'norm_ffn_w', 'router_w', 'router_b',
        'expert_w_gu', 'expert_b_gu', 'expert_w_down', 'expert_b_down', 'norm_final_w']
_OUTS = [(1, 128, 1024), (1, 128, 1024), (1, 1, 8, 64, 64), (1, 1, 8, 64, 64)]


def kernel(**inputs):
    import numpy as np
    import concourse.bacc as bacc
    from concourse.bass_utils import run_bass_kernel_spmd

    nc = bacc.Bacc("TRN2", target_bir_lowering=False, num_devices=1)
    arrays, A = {}, {}
    for name in _INS:
        a = np.ascontiguousarray(inputs[name])
        arrays[f"in_{name}"] = a
        A[name] = nc.dram_tensor(f"in_{name}", a.shape, mybir.dt.from_np(a.dtype), kind="ExternalInput").ap()
    outs = [nc.dram_tensor(f"out_{i}", s, F32, kind="ExternalOutput").ap() for i, s in enumerate(_OUTS)]
    scratch = nc.dram_tensor("gate_rows", (2, NS, D), F32, kind="Internal").ap()
    ctx = trunk_kernel(nc, A, outs, scratch)
    ctx.close()
    r = run_bass_kernel_spmd(nc, [arrays], core_ids=[0])
    return tuple(r.results[0][f"out_{i}"] for i in range(4))
```

```python
import concourse.bass as bass
from concourse import mybir
from contextlib import ExitStack

F32 = mybir.dt.float32
I32 = mybir.dt.int32
U32 = mybir.dt.uint32
ALU = mybir.AluOpType
ACT = mybir.ActivationFunctionType
AX = mybir.AxisListType

P = 128
D = 1024
T = 128
NS = 2
TT = NS * T
KT = D // P
POOLW = 512
RW = 512
NT = RW // P
HS = 64
GRID_W = 64
RCOLS = 3 * RW + 3 * P
RTILES = RCOLS // P
OFF_M = POOLW + RCOLS
WINDOWS = (2, 4, 8, 16)
NE = 32
FF = 1024
SLOTS = 64
EXTRA = 16
ITEMS = NE + EXTRA + 1
DECAY = 0.6065306597126334
LIMIT = 7.0
ALPHA = 1.702
RMS_EPS = 1e-6
GN_EPS = 1e-5 * HS

RING = 12
FRING = 8
CW = 2048
GU_CHUNKS = KT
DN_CHUNKS = 4


def front_chunks():
    out = [("w_mod", 256 * i, 256) for i in range(8)]
    out += [("w_in", POOLW + 256 * i, 256) for i in range(RTILES // 2)] + [("w_in", OFF_M - P, P)]
    out += [("w_in", 0, 256), ("w_in", 256, 256)]
    out += [("w_mod", 2048 + 256 * i, 256) for i in range(16)]
    out += [("w_in", OFF_M + 256 * i, 256) for i in range(8)]
    out += [("w_pool_out", 512 * i, 512) for i in range(2)]
    out += [("w_rwkv_out", 512 * i, 512) for i in range(2)]
    out += [("w_o", 256 * i, 256) for i in range(4)]
    return out


MG = 4
MW = 256

CHUNKS = front_chunks()
NF = len(CHUNKS)
C_MODA, C_RWKV, C_POOL, C_MODB, C_MERGE, C_POUT, C_ROUT, C_WO = 0, 8, 16, 18, 34, 42, 44, 46


def released(c):
    if c < C_RWKV:
        return "moda_mm", c // MG + 1
    if c < C_POOL:
        return "proj_done", min(2 * (c - C_RWKV) + 2, RTILES)
    if c < C_MODB:
        return "pu_mm", c - C_POOL + 1
    if c < C_MERGE:
        return "modb_mm", (c - C_MODB) // MG + 1
    if c < C_POUT:
        return "merge_mm", 2 * (c - C_MERGE) + 2
    if c < C_ROUT:
        return "pout_mm", 4 * (c - C_POUT) + 4
    if c < C_WO:
        return "rout_mm", 4 * (c - C_ROUT) + 4
    return "wo_mm", 2 * (c - C_WO) + 2


def slot_of(c):
    return c % FRING if c < C_POUT else (c + 2) % FRING


def freed(c):
    if c < C_POUT:
        return released(c - FRING)
    if c < C_WO:
        return released(c - FRING + 2)
    return (("kq_mm", 4), ("kq_mm", 8), ("rout_used", KT), ("rout_used", KT))[c - C_WO]


USE = [sum(slot_of(b) == slot_of(c) for b in range(c + 1)) for c in range(NF)]
FRONT_USES = [sum(slot_of(c) == s for c in range(NF)) for s in range(RING)]


def trunk_kernel(nc, A, O, scratch):
    ctx = ExitStack()
    sems = {}

    def S(name):
        if name not in sems:
            sems[name] = ctx.enter_context(nc.semaphore(name))
        return sems[name]

    def sb(name, shape, dt=F32):
        return ctx.enter_context(nc.sbuf_tensor(name, shape, dt))

    ring = sb("ring", [P, RING, CW])

    ident = sb("ident", [P, P])
    ones = sb("ones", [P, P])
    upp = sb("upp", [P, P])
    mqr = sb("mqr", [P, 2, 2, P])
    lvl = sb("lvl", [P, 7, 2, P])
    bmean = sb("bmean", [P, P])
    rowlo = sb("rowlo", [P, 1])
    iotai = sb("iotai", [P, P], I32)
    iota2 = sb("iota2", [P, P])
    eidx = sb("eidx", [P, P])
    iota3 = sb("iota3", [P, 3])
    thr3 = sb("thr3", [P, 3])
    par4 = sb("par4", [P, 4])
    par2 = sb("par2", [P, 2])

    rows_a = sb("rows_a", [96, P])
    rows_b = sb("rows_b", [55, P])
    prm = sb("prm", [P, 96])
    prb = sb("prb", [P, 55])
    cpad = sb("cpad", [P, KT, 32])
    csig = sb("csig", [P, NS, KT])
    mu = sb("mu", [P, 7, RTILES])
    kam = sb("kam", [P, NT])
    epsr = sb("epsr", [P, 1])
    epsg = sb("epsg", [P, 1])
    moda = sb("moda", [P, 2, KT, NS])
    modb = sb("modb", [P, 4, KT, NS])
    modt = sb("modt", [P, 4, KT, NS])
    hm = sb("hm", [P, 2])
    gcol = sb("gcol", [P, 2, NS, KT])
    grow = rows_a[0:2 * NS * KT, :]

    x = sb("x", [P, NS, D])
    stat = sb("stat", [P, 8])
    hnT = sb("hnT", [P, KT, TT])
    pr = sb("pr", [P, RTILES, TT])
    raw = sb("raw", [P, 4, TT])
    kk = sb("kk", [P, NT, TT])
    qr = sb("qr", [P, 2, NS, NT, 2, T])
    bt = sb("bt", [P, 2, NS, NT, T])
    kt_ = sb("kt_", [P, 2, NS, NT, T])
    vt = sb("vt", [P, NS, RW])
    s0t = sb("s0t", [P, 2 * NT, 2, HS])
    pms = sb("pms", [P, 2 * NT])
    fin = sb("fin", [P, 2, NT])
    gate = sb("gate", [P, NT, TT])
    corr = sb("corr", [P, NT, TT])
    pmT = sb("pmT", [P, 4, TT])

    early = qr[:].rearrange("p d s c k t -> p (d s c k t)")
    w2, a2, gw2 = early[:, 0:512], early[:, 512:1024], early[:, 1024:1536]
    poolw = early[:, 1536:2048].rearrange("p (g c) -> p g c", g=4)
    w0row = early[0:1, 2048:3072].rearrange("p (d c) -> p d c", d=2)
    s0raw = early[0:HS, 3072:4096].rearrange("p (d q c) -> p d q c", d=2, q=NT)
    em = kt_[:].rearrange("p d s c t -> p (d s c t)")
    pband = em[:, 0:512].rearrange("p (g t) -> p g t", g=4)
    tri = em[:, 512:1024].rearrange("p (d k t) -> p d k t", d=2, k=2)
    bdm = em[:, 1024:1280].rearrange("p (b t) -> p b t", b=2)
    low = em[:, 1280:1408]
    bones = em[:, 1408:1536]
    rawf = raw[:].rearrange("p c t -> p (c t)")
    so = rawf[:, 0:512].rearrange("p (c k) -> p c k", c=2 * NT)
    zs = rawf[:, 512:1024].rearrange("p (d q h v) -> p d q h v", d=2, q=2, h=2)
    us = pr[:, 8:12, :].rearrange("p c t -> p (c t)").rearrange("p (g q h v) -> p g q h v", g=4, q=2, h=2)
    btm = [w.rearrange("p (d q h t) -> p d q h t", d=2, q=NT, h=2)
           for w in (ring[:, 0, :], hnT[:].rearrange("p k t -> p (k t)"))]
    ktm = ring[:, 1, :].rearrange("p (d q h t) -> p d q h t", d=2, q=NT, h=2)
    mrow_a = corr[:].rearrange("p c t -> p (c t)")[:, 0:2 * MW].rearrange("p (g n) -> p g n", g=2)

    sig = ring[:, 8, :].rearrange("p (d s c) -> p d s c", d=2, s=NS)
    aa = ring[:, 9, :].rearrange("p (d c t) -> p d c t", d=2, c=NT)
    kd = ring[:, 10, :].rearrange("p (d c t) -> p d c t", d=2, c=NT)
    mrow_b = bt[:].rearrange("p d s c t -> p (d s c t)")[:, 0:4 * MW].rearrange("p (g n) -> p g n", g=4)
    utok = ring[:, 11, 0:1024].rearrange("p (s c) -> p s c", s=NS)
    pooled = ring[:, 11, 1024:2048].rearrange("p (g t) -> p g t", g=4)
    work = ring[:, 8:12, :].rearrange("p g (k i t) -> p g k i t", k=4, i=4)
    W_M, W_X, W_AT, W_XT = 0, 1, 2, 3


    def kqm(g):
        return ring[:, 8 + g, 0:1024].rearrange("p (i k t) -> p i k t", i=4, k=2)

    xn = ring[:, 8, :].rearrange("p (s c) -> p s c", s=NS)
    junk = ring[:, 9, :].rearrange("p (s c) -> p s c", s=NS)
    bfin = raw[:].rearrange("p c t -> p (c t)").rearrange("p (d q t) -> p d q t", d=2, q=NT)
    bkt = pr[:, 0:8, :].rearrange("p c t -> p (c t)").rearrange("p (j d c) -> p j d c", j=2, d=2)

    area = qr[:].rearrange("p d s c k t -> p (d s c k t)")
    merge = ring[:, 2:4, :].rearrange("p g (m t) -> p (g m) t", m=KT)
    x2t = bt[:].rearrange("p d s c t -> p (d s c t)").rearrange("p (s c) -> p s c", s=NS)
    xn2 = x2t
    ms = kt_[:].rearrange("p d s c t -> p (d s c t)").rearrange("p (m t) -> p m t", m=KT)
    gbc = pr[:, 0:8, :].rearrange("p m t -> p (m t)").rearrange("p (s c) -> p s c", s=NS)
    bgu = area[0:NE, 0:2048]
    bdn = area[0:NE, 2048:3072]
    rtw = sb("rtw", [P, KT, NE])
    rtb = sb("rtb", [1, NE])
    wbuf = area[:, 3072:4096]
    xg = gate[:].rearrange("p c t -> p (c t)")[:, 0:512].rearrange("p (k s) -> p k s", k=KT)
    gsb = gate[:].rearrange("p c t -> p (c t)")[:, 512:1024]
    sgb = corr[:].rearrange("p c t -> p (c t)")[:, 0:512]
    lcb = corr[:].rearrange("p c t -> p (c t)")[:, 512:1024]
    act_ = pmT[:].rearrange("p c t -> p (c t)")[:, 0:512]
    actT = pmT[:].rearrange("p c t -> p (c t)")[:, 512:1024].rearrange("p (j h s) -> p j h s", j=4, h=2)
    ysb = kk[:].rearrange("p c t -> p (c t)")[:, 0:512]
    pwt = kk[:].rearrange("p c t -> p (c t)")[:, 512:768].rearrange("p (i t) -> p i t", i=NS)
    p2 = vt[:, 0, 0:256].rearrange("p (i s) -> p i s", i=NS)
    pw = vt[:, 0, 256:512].rearrange("p (i s) -> p i s", i=NS)
    sele = vt[0:NE, 1, 0:SLOTS]
    lg = sb("lg", [P, NS, NE])
    top8 = sb("top8", [P, NS, 8])
    idx8 = sb("idx8", [P, NS, 8], U32)
    idxf = sb("idxf", [P, NS, 8])
    tw = sb("tw", [P, NS, 4])
    twn = sb("twn", [P, NS, 4])
    sel = sb("sel", [P, NS, NE])
    comb = sb("comb", [P, NS, NE])
    oh = sb("oh", [P, NE])
    rank = sb("rank", [P, NS, NE])
    combT = vt[0:NE, 1, SLOTS:SLOTS + TT]
    cnt = sb("cnt", [NE, 8])
    fl = sb("fl", [NE, 3])
    posc = sb("posc", [NE, 3])
    oh16 = sb("oh16", [NE, 3, EXTRA])
    e16 = sb("e16", [NE, 2, EXTRA])
    item = sb("item", [1, ITEMS + 1], I32)
    base = sb("base", [P, ITEMS])
    fstat = sb("fstat", [P, 4])

    banks = [ctx.enter_context(nc.psum_tensor(f"bank{i}", [P, 512], F32)) for i in range(8)]

    def ring_in(c):
        _, _, n = CHUNKS[c]
        rt = min(KT, CW // n)
        return ring[:, slot_of(c), 0:rt * n].rearrange("p (k n) -> p k n", k=rt)

    def arrived(eng, c):
        eng.wait_ge(S(f"slot{slot_of(c)}_full"), 16 * USE[c])

    rwv = {n: A[n] for n in ("w_in", "w_mod", "w_pool_out", "w_rwkv_out", "w_o")}

    XB = [(0, 1), (2, 3)]
    PB = [banks[0], banks[5], banks[6], banks[7]]
    ZB = [0, 6, 1, 0]
    CB = [6, 2, 0]

    def unit_bank(u):
        return banks[5 + 2 * (u % 2)][:, 0:TT]

    FILL = [[("R", 0), ("R", 1), ("X", 0), ("X", 1)], [("R", 2)], [("R", 3), ("X", 2)], [("X", 3), ("M", 0), ("M", 1)],
            [("M", m) for m in range(2, 5)], [("M", m) for m in range(5, 7)], [("M", m) for m in range(7, 9)],
            [("M", m) for m in range(9, 16)]]
    UNITS = [u for part in FILL for u in part]
    block = ctx.enter_context(nc.Block())

    @block.sync
    def _(sp):
        sp.dma_start(x[:, 0, :], A["x_prompt"][0]).then_inc(S("x_in"), 16)
        sp.dma_start(x[:, 1, :], A["x_sample"][0]).then_inc(S("x_in"), 16)

        def rows(dst, at, ap, n, s):
            sp.dma_start(dst[at:at + n, :], ap).then_inc(S(s), 16)

        def r128(ap):
            return ap.rearrange("(n p) -> n p", p=P)

        rows(rows_a, 0, r128(A["c_ctx"]), 8, "rows_a_in")
        rows(rows_a, 8, r128(A["c"][0]), 8, "rows_a_in")
        rows(rows_a, 16, r128(A["b_mod"][0]), 48, "rows_a_in")
        rows(rows_a, 64, r128(A["norm_mix_w"][0]), 8, "rows_a_in")
        rows(rows_a, 72, r128(A["norm_ffn_w"][0]), 8, "rows_a_in")
        rows(rows_a, 80, r128(A["b_merge"][0]), 16, "rows_a_in")

        def chunk(c):
            name, c0, n = CHUNKS[c]
            if c >= FRING:
                name_, count = freed(c)
                sp.wait_ge(S(name_), count)
            src = rwv[name][0].rearrange("(k p) n -> p k n", p=P)[:, :, c0:c0 + n]
            sp.dma_start(ring_in(c), src).then_inc(S(f"slot{slot_of(c)}_full"), 16)

        for c in range(2):
            chunk(c)
        rows(rows_b, 0, r128(A["shift_mu"][0]), 15, "rows_b_in")
        rows(rows_b, 15, r128(A["pool_scale"][0]), 4, "rows_b_in")
        for d in range(2):
            rows(rows_b, 19 + 4 * d, r128(A["iclr_a0"][0, d]), 4, "rows_b_in")
        rows(rows_b, 27, r128(A["k_k"][0]), 4, "rows_b_in")
        rows(rows_b, 31, r128(A["k_a"][0]), 4, "rows_b_in")
        rows(rows_b, 35, A["r_k"][0].rearrange("(n a) c -> n (a c)", a=2), 4, "rows_b_in")
        rows(rows_b, 39, r128(A["ln_x_w"][0]), 4, "rows_b_in")
        rows(rows_b, 43, r128(A["ln_x_b"][0]), 4, "rows_b_in")
        rows(rows_b, 47, r128(A["norm_final_w"]), 8, "rows_b_in")
        for c in range(2, 8):
            chunk(c)
        sp.dma_start(w2, A["decay_w2"][0].rearrange("d l c -> (d l) c")).then_inc(S("lora_in"), 16)
        sp.dma_start(a2, A["iclr_a2"][0].rearrange("d l c -> (d l) c")).then_inc(S("lora_in"), 16)
        sp.dma_start(gw2, A["gate_w2"][0]).then_inc(S("lora_in"), 16)
        sp.dma_start(w0row, A["decay_w0"]).then_inc(S("lora_in"), 16)
        sp.dma_start(poolw, A["pool_w"][0].rearrange("g c d -> c g d")).then_inc(S("poolw_in"), 16)
        for d, n in enumerate(("state_fwd", "state_bwd")):
            for q in range(NT):
                sp.dma_start(s0raw[:, d, q, :].rearrange("v (h k) -> v h k", h=2),
                             A[n][0, 0, 2 * q:2 * q + 2].rearrange("h v k -> v h k")).then_inc(S("state_in"), 16)
        sp.dma_start(rtw[:], A["router_w"][0].rearrange("(k p) e -> p k e", p=P)).then_inc(S("router_in"), 16)
        sp.dma_start(rtb[:], A["router_b"]).then_inc(S("router_in"), 16)
        for c in range(8, C_WO + 2):
            chunk(c)

        def expert_chunk(e, j):
            if j < GU_CHUNKS:
                src, dst = A["expert_w_gu"][0][bass.ds(e, 1), j * P:(j + 1) * P, :], ring[:, j, :]
                src = src.rearrange("o p n -> (o p) n")
            else:
                r = 2 * P * (j - GU_CHUNKS)
                src = A["expert_w_down"][0][bass.ds(e, 1), r:r + 2 * P, :].rearrange("o (i p) n -> p (o i) n", i=2)
                dst = ring[:, j, :].rearrange("p (i n) -> p i n", i=2)
            sp.dma_start(dst, src).then_inc(S(f"slot{j}_full"), 16)

        sp.wait_ge(S("y_mm"), 4)
        for j in range(FRING, RING):
            expert_chunk(0, j)
        for c in range(C_WO + 2, NF):
            chunk(c)
        for c in range(NF - FRING, NF):
            name, count = released(c)
            sp.wait_ge(S(name), count)
            expert_chunk(0, slot_of(c))
        sp.wait_ge(S("items_ready"), 1)
        n_items = sp.value_load(item[0:1, ITEMS:ITEMS + 1], min_val=NE, max_val=NE + EXTRA)
        with sp.Fori(1, n_items) as it:
            e = sp.value_load(item[0:1, bass.ds(it, 1)], min_val=0, max_val=NE - 1)
            for j in range(RING):
                sp.wait_ge(S("chunk_used"), it * RING + (j + 1 - RING))
                expert_chunk(e, j)
        sp.wait_ge(S("stored"), 96)

    @block.gpsimd
    def _(pool):
        g = nc.gpsimd
        n = [0]

        def step(ins):
            n[0] += 1
            ins.then_inc(S("pool_step"), 1)
            pool.wait_ge(S("pool_step"), n[0])

        def signal(ins, name, count):
            ins.then_inc(S(name), 1)
            pool.wait_ge(S(name), count)

        def keep(dst, src, pattern, op, fill, b=0, cm=1):
            step(g.affine_select(out=dst, in_=src, compare_op=op, fill=fill, base=b, pattern=pattern,
                                 channel_multiplier=cm))

        step(g.memset(ident[:], 0.0))
        step(g.memset(ones[:], 1.0))
        keep(ident[:], ident[:], [[-1, P]], ALU.not_equal, 1.0)
        step(g.memset(epsr[:], RMS_EPS))
        step(g.memset(epsg[:], GN_EPS))
        step(g.memset(cpad[:], 0.0))
        signal(g.memset(rowlo[:], 0.0), "ident_ready", 1)
        keep(low, ones[:], [[-1, P]], ALU.is_gt, 0.0)
        keep(upp[:], ones[:], [[1, P]], ALU.is_gt, 0.0, cm=-1)
        keep(mqr[:, 0, 0, :], ones[:], [[1, P]], ALU.is_gt, 0.0, cm=-1)
        keep(mqr[:, 0, 1, :], ones[:], [[1, P]], ALU.is_ge, 0.0, cm=-1)
        keep(mqr[:, 1, 0, :], ones[:], [[-1, P]], ALU.is_gt, 0.0)
        keep(mqr[:, 1, 1, :], ones[:], [[-1, P]], ALU.is_ge, 0.0)
        step(g.memset(rowlo[0:HS, :], 1.0))
        step(g.memset(hm[:], 0.0))
        step(g.memset(s0t[:], 0.0))
        for h in range(2):
            step(g.memset(hm[h * HS:(h + 1) * HS, h:h + 1], 1.0))
        step(g.memset(bones, 0.0))
        step(g.memset(bmean[:], 0.0))
        for h in range(2):
            step(g.memset(bones[h * HS:(h + 1) * HS, h * HS:(h + 1) * HS], 1.0))
            step(g.memset(bmean[h * HS:(h + 1) * HS, h * HS:(h + 1) * HS], 1.0 / HS))
        for i, w in enumerate(WINDOWS):
            keep(pband[:, i, :], ones[:], [[-1, P]], ALU.is_ge, 0.0, b=w // 2)
            keep(pband[:, i, :], pband[:, i, :], [[1, P]], ALU.is_gt, 0.0, b=w // 2, cm=-1)
        signal(g.memset(base[:], 0.0), "masks_ready", 1)
        for i in range(1, 7):
            m = 2 ** i
            if i >= 3:
                pool.wait_ge(S("bd_used"), i - 1)
            b = bdm[:, i % 2, :]
            bv = b.rearrange("p (n m) -> p n m", m=m)
            keep(bv, ones[:].rearrange("p (n m) -> p n m", m=m), [[-m, P // m], [0, m]], ALU.is_ge, 0.0)
            signal(g.affine_select(out=bv, in_=bv, compare_op=ALU.is_gt, fill=0.0, base=m,
                                   pattern=[[m, P // m], [0, m]], channel_multiplier=-1), "bd_ready", i)
        step(g.iota(iotai[:], [[0, 2], [1, SLOTS]], base=0, channel_multiplier=0))
        step(g.tensor_copy(iota2[:], iotai[:]))
        step(g.iota(iotai[:], [[0, P]], base=0, channel_multiplier=1))
        step(g.tensor_copy(eidx[:], iotai[:]))
        step(g.tensor_copy(iota3[:], iota2[:, 0:3]))
        step(g.iota(item[:, 0:NE], [[1, NE]], base=0, channel_multiplier=0))
        step(g.memset(item[:, NE:ITEMS + 1], 0))
        signal(g.tensor_scalar(thr3[:], iota2[:, 0:3], float(SLOTS), float(SLOTS), ALU.mult, ALU.add), "lists_ready", 1)

        pool.wait_ge(S("grow_ready"), 1)
        pool.dma_start(scratch.rearrange("g s (k p) -> (g s k) p", p=P), grow).then_inc(S("gates_out"), 16)
        pool.wait_ge(S("gates_out"), 16)
        pool.wait_ge(S("y_mm"), 4)
        for gi in range(2):
            if gi:
                pool.wait_ge(S("wo_used"), 8)
            for s in range(NS):
                pool.dma_start(gbc[:, s, :], scratch[gi, s:s + 1, :].to_broadcast([P, D])).then_inc(S("gbc_in"), 16)
            if gi == 0:
                pool.dma_start(bgu, A["expert_b_gu"][0]).then_inc(S("bgu_in"), 16)
                pool.dma_start(bdn, A["expert_b_down"][0]).then_inc(S("bdn_in"), 16)
                pool.dma_start(wbuf, A["norm_final_w"].rearrange("(a n) -> a n", a=1).to_broadcast([P, D])).then_inc(S("wfin_in"), 16)

    @block.tensor
    def _(pe):
        mm = nc.tensor.matmul
        tr = nc.tensor.transpose

        pe.wait_ge(S("ident_ready"), 1)
        pe.wait_ge(S("rows_a_in"), 96)
        tr(banks[0][:, 0:96], rows_a[:], ident[0:96, 0:96]).then_inc(S("prmT_done"), 1)
        for s in range(NS):
            pe.wait_ge(S("xn_ready"), s + 1)
            for k in range(KT):
                b = banks[1 + k // 2]
                last = tr(b[:, (k % 2) * TT + s * T:(k % 2) * TT + (s + 1) * T], xn[:, s, k * P:(k + 1) * P], ident[:])
        last.then_inc(S("xnT_done"), 1)

        def mod_rows(c0, out, done):
            for j in range(MG):
                arrived(pe, c0 + j)
            for k in range(KT):
                for j in range(MG):
                    last = mm(out[32 * j:32 * (j + 1), :], cpad[:, k, :], ring_in(c0 + j)[:, k, :], start=(k == 0), stop=(k == KT - 1))
            last.then_inc(S(done), 1)

        def mod_turn(rows, out, done):
            for h in range(2):
                last = tr(out[:, h * P:(h + 1) * P], rows[:, h * P:(h + 1) * P], ident[:])
            last.then_inc(S(done), 1)

        pe.wait_ge(S("cpad_ready"), 1)
        for g in range(2):
            mod_rows(C_MODA + MG * g, unit_bank(g), "moda_mm")
        for g in range(2):
            pe.wait_ge(S("mrow_ready"), g + 1)
            mod_turn(mrow_a[:, g, :], banks[6][:, g * MW:(g + 1) * MW], "modat_mm")
        pe.wait_ge(S("rows_b_in"), 160)
        tr(banks[0][:, 128:183], rows_b[:], ident[0:55, 0:55]).then_inc(S("prbT_done"), 1)

        fills = [0]

        def fill(part):
            for kind, i in FILL[part]:
                u = fills[0]
                if u >= 2:
                    pe.wait_ge(S("fill_used"), u - 1)
                if kind == "R":
                    mod_rows(C_MODB + MG * i, unit_bank(u), "modb_mm")
                elif kind == "X":
                    pe.wait_ge(S("fill_used"), UNITS.index(("R", i)) + 1)
                    mod_turn(mrow_b[:, i, :], unit_bank(u), "modbt_mm")
                else:
                    c = C_MERGE + i // 2
                    arrived(pe, c)
                    for k in range(KT):
                        last = mm(unit_bank(u), ring_in(c)[:, k, (i % 2) * P:(i % 2 + 1) * P], hnT[:, k, :],
                                  start=(k == 0), stop=(k == KT - 1))
                    last.then_inc(S("merge_mm"), 1)
                fills[0] += 1

        pe.wait_ge(S("hn_ready"), 2)
        pe.wait_ge(S("prb_ready"), 1)
        for ct in range(RTILES):
            c = C_RWKV + ct // 2
            arrived(pe, c)
            w = ring_in(c)
            if ct >= 4:
                pe.wait_ge(S("raw_copied"), ct - 3)
            o = (ct % 2) * P if ct < RTILES - 1 else 0
            for k in range(KT):
                last = mm(PB[ct % 4][:, 0:TT], w[:, k, o:o + P], hnT[:, k, :], start=(k == 0), stop=(k == KT - 1))
            last.then_inc(S("proj_done"), 1)

        for c in range(2):
            arrived(pe, C_POOL + c)
            w = ring_in(C_POOL + c)
            for s in range(NS):
                for k in range(KT):
                    last = mm(banks[2 + s][:, 256 * c:256 * c + 256], hnT[:, k, s * T:(s + 1) * T], w[:, k, :],
                              start=(k == 0), stop=(k == KT - 1))
            last.then_inc(S("pu_mm"), 1)

        pe.wait_ge(S("masks_ready"), 1)
        mm(banks[4][:, :], ones[:], pband.rearrange("p g t -> p (g t)"), start=True, stop=True).then_inc(S("pcnt_done"), 1)

        pe.wait_ge(S("raw_copied"), RTILES)
        fill(0)
        pe.wait_ge(S("lora_in"), 64)
        pe.wait_ge(S("th_ready"), 1)
        for d in range(2):
            for s in range(NS):
                b = banks[ZB[2 * d + s]]
                if 2 * d + s == 3:
                    pe.wait_ge(S("sig_ready"), 1)
                mm(b[:, :], pr[d * HS:(d + 1) * HS, 12, s * T:(s + 1) * T], w2[d * HS:(d + 1) * HS, :], start=True, stop=False)
                mm(b[:, :], ones[0:1, :], w0row[0:1, d, :], start=False, stop=True).then_inc(S("z_done"), 1)
        fill(1)
        pe.wait_ge(S("utok_ready"), 2)
        pe.wait_ge(S("pband_ready"), 1)
        for gi in range(4):
            for s in range(NS):
                last = mm(banks[2 + gi // 2][:, (gi % 2) * TT + s * T:(gi % 2) * TT + (s + 1) * T],
                          utok[:, s, gi * P:(gi + 1) * P], pband[:, gi, :], start=True, stop=True)
        last.then_inc(S("pooled_done"), 1)
        pe.wait_ge(S("sig_ready"), 4)
        for d in range(2):
            for q in range(NT):
                if d == 1 and q == 2:
                    pe.wait_ge(S("a_ready"), 1)
                last = mm(banks[ZB[2 * d + q // 2]][:, (q % 2) * TT:(q % 2 + 1) * TT], a2[d * HS:(d + 1) * HS, q * P:(q + 1) * P],
                          pr[d * HS:(d + 1) * HS, 13, :], start=True, stop=True)
                if q % 2:
                    last.then_inc(S("a_done"), 1)
        fill(2)
        pe.wait_ge(S("pooled_ready"), 2)
        pe.wait_ge(S("poolw_in"), 16)
        pe.wait_ge(S("pband_ready"), 1)
        MB = [banks[4], banks[2]]
        for gi in range(4):
            last = mm(MB[gi // 2][:, (gi % 2) * TT:(gi % 2 + 1) * TT], poolw[:, gi, :], pooled[:, gi, :], start=True, stop=True)
        last.then_inc(S("mixed_done"), 1)
        pe.wait_ge(S("a_ready"), 4)
        for q in range(NT):
            last = mm(banks[(3, 0)[q // 2]][:, (q % 2) * TT:(q % 2 + 1) * TT], gw2[:, q * P:(q + 1) * P], pr[:, 14, :], start=True, stop=True)
        last.then_inc(S("gate_done"), 1)
        fill(3)
        pe.wait_ge(S("a_ready"), 4)
        pe.wait_ge(S("ksq_ready"), 1)
        for q in range(NT):
            last = mm(banks[(6, 1)[q // 2]][:, (q % 2) * TT:(q % 2 + 1) * TT], bones, raw[:, q, :], start=True, stop=True)
        last.then_inc(S("norm_done"), 1)
        pe.wait_ge(S("mixed_ready"), 2)
        pe.wait_ge(S("gate_ready"), 2)
        for s in range(NS):
            for q in range(NT):
                last = tr(banks[(2, 0)[s]][:, q * P:(q + 1) * P], pr[:, 8 + q, s * T:(s + 1) * T], ident[:])
        last.then_inc(S("vt_done"), 1)
        pe.wait_ge(S("state_in"), 128)
        for d in range(2):
            for q in range(NT):
                i = d * NT + q
                last = tr(banks[4][:, i * HS:(i + 1) * HS], s0raw[:, d, q, :], ident[0:HS, 0:HS])
        last.then_inc(S("s0_done"), 1)
        fill(4)
        pe.wait_ge(S("gate_ready"), 2)
        pe.wait_ge(S("rkk_ready"), 1)
        for q in range(NT):
            last = mm(banks[(3, 1)[q // 2]][:, (q % 2) * TT:(q % 2 + 1) * TT], bones, raw[:, q, :], start=True, stop=True)
        last.then_inc(S("rk_done"), 1)
        fill(5)
        pe.wait_ge(S("tri_ready"), 1)
        pe.wait_ge(S("kk_ready"), 1)
        pe.wait_ge(S("vt_ready"), 2)
        for i in range(8):
            d, s, t2 = i // 4, (i // 2) % 2, i % 2
            if i >= 3:
                pe.wait_ge(S("cum_used"), i - 2)
            for q in range(2):
                last = mm(banks[CB[i % 3]][:, q * 256:(q + 1) * 256], sig[:, d, s, (2 * t2 + q) * P:(2 * t2 + q + 1) * P],
                          tri[:, d, :, :].rearrange("p k t -> p (k t)"), start=True, stop=True)
            last.then_inc(S("cum_done"), 1)

        fill(6)
        fill(7)
        pe.wait_ge(S("gcol_ready"), 1)
        pe.wait_ge(S("fill_used"), len(UNITS))
        tr(banks[5][0:32, 128:256], gcol[:].rearrange("p g s k -> p (g s k)"), ident[:]).then_inc(S("grow_done"), 1)

        for j in range(2):
            for d in range(2):
                pe.wait_ge(S("bf_ready"), 2 * j + d + 1)
                if 2 * j + d >= 2:
                    pe.wait_ge(S("bk_ready"), 2 * j + d - 1)
                b = banks[(3, 1)[d]]
                for q in range(NT):
                    last = tr(b[:, q * P:(q + 1) * P], bfin[:, d, q, :], ident[:])
                last.then_inc(S("bk_done"), 1)

        for s in range(NS):
            pe.wait_ge(S("btm_ready"), s + 1)
            pe.wait_ge(S("grow_ready"), 1)
            for g in range(4):
                d, tp = g // 2, g % 2
                if g >= 2:
                    pe.wait_ge(S("a_evac"), 4 * s + g - 1)
                elif s == 1:
                    pe.wait_ge(S("y_evac"), 2)
                    pe.wait_ge(S("state_copied"), 1)
                elif g == 0:
                    pe.wait_ge(S("bk_ready"), 4)
                ba, bat = banks[2 * (g % 2)], banks[2 * (g % 2) + 1]
                for i in range(4):
                    h, q = i // 2, 2 * tp + i % 2
                    c = (i % 2) * T
                    b = (ba, bat)[h]
                    mm(b[:, c:c + T], qr[:, d, s, q, 0, :], btm[s][:, d, q, h, :], start=True, stop=True)
                    last = mm(b[:, 2 * T + c:3 * T + c], btm[s][:, d, q, h, :], qr[:, d, s, q, 0, :], start=True, stop=True)
                last.then_inc(S("a_mm"), 1)
            for l in range(1, 7):
                for g in range(4):
                    n = 24 * s + 4 * (l - 1) + g
                    if l == 1:
                        pe.wait_ge(S("a_evac"), 4 * s + g + 1)
                    else:
                        pe.wait_ge(S("x_upd"), n - 4 + 1)
                    if n >= 2:
                        pe.wait_ge(S("m_evac"), n - 1)
                    b = banks[4 + g % 2]
                    for i in range(4):
                        last = mm(b[:, i * T:(i + 1) * T], work[:, g, W_AT, i, :], work[:, g, W_X, i, :], start=True, stop=True)
                    last.then_inc(S("m_mm"), 1)
                for g in range(4):
                    n = 24 * s + 4 * (l - 1) + g
                    pe.wait_ge(S("m_evac"), n + 1)
                    if g >= 2:
                        pe.wait_ge(S("x_upd"), n - 2 + 1)
                    bx, bxt = XB[g % 2]
                    for i in range(4):
                        if l < 6:
                            mm(banks[bx][:, i * T:(i + 1) * T], work[:, g, W_XT, i, :], work[:, g, W_M, i, :], start=True, stop=True)
                        last = mm(banks[bxt][:, i * T:(i + 1) * T], work[:, g, W_M, i, :], work[:, g, W_XT, i, :], start=True, stop=True)
                    last.then_inc(S("x_mm"), 1)
            def kq(j):
                tp, d = j // 2, j % 2
                n = 4 * s + j
                if j >= 2:
                    pe.wait_ge(S("kq_evac"), n - 1)
                elif j == 0:
                    pe.wait_ge(S("x_upd"), 24 * s + 24)
                    pe.wait_ge(S("ktm_ready"), s + 1)
                for i in range(4):
                    h, q = i // 2, 2 * tp + i % 2
                    mm(banks[6 + j % 2][:, i * T:(i + 1) * T], btm[s][:, d, q, h, :], qr[:, d, s, q, 1, :], start=True, stop=True)
                for i in range(4):
                    h, q = i // 2, 2 * tp + i % 2
                    last = mm(banks[2 * (j % 2) + i // 2][:, (i % 2) * 256:(i % 2 + 1) * 256], ktm[:, d, q, h, :],
                              qr[:, d, s, q, :, :].rearrange("p k t -> p (k t)"), start=True, stop=True)
                last.then_inc(S("kq_mm"), 1)

            def z(j):
                tp, d = j // 2, j % 2
                g, n = 2 * d + tp, 4 * s + j
                pe.wait_ge(S("kq_evac"), n + 1)
                if n:
                    pe.wait_ge(S("z_evac"), n)
                for i in range(4):
                    q = 2 * tp + i % 2
                    o = banks[4][:, i * T:(i + 1) * T]
                    last = mm(o, kqm(g)[:, i, 0, :], vt[:, s, q * P:(q + 1) * P], start=True, stop=(s == 0))
                    if s == 1:
                        last = mm(o, qr[:, d, s, q, 0, :], s0t[:, d * NT + q, :, :].rearrange("p h v -> p (h v)"), start=False, stop=True)
                last.then_inc(S("z_mm"), 1)

            def u(j):
                tp, d = j // 2, j % 2
                g, n = 2 * d + tp, 4 * s + j
                pe.wait_ge(S("z_evac"), n + 1)
                if n:
                    pe.wait_ge(S("u_evac"), n)
                if n and d == 0:
                    pe.wait_ge(S("y_evac"), n // 2)
                for i in range(4):
                    last = mm(banks[5][:, i * T:(i + 1) * T], work[:, g, W_XT, i, :], zs[:, d, i % 2, :, :].rearrange("p h v -> p (h v)"),
                              start=True, stop=True)
                last.then_inc(S("u_mm"), 1)

            def y(tp):
                pe.wait_ge(S("u_evac"), 4 * s + 2 * tp + 2)
                for qi in range(2):
                    q = 2 * tp + qi
                    for d in range(2):
                        g = 2 * d + tp
                        for h in range(2):
                            i = 2 * h + qi
                            o = banks[5][h * HS:(h + 1) * HS, qi * T:(qi + 1) * T]
                            mm(o, vt[:, s, q * P + h * HS:q * P + (h + 1) * HS], kqm(g)[:, i, 1, :], start=(d == 0), stop=False)
                            last = mm(o, us[:, g, qi, h, :], work[:, g, W_AT, i, :], start=False, stop=(d == 1))
                    if s == 1:
                        for d in range(2):
                            last = mm(banks[5][:, qi * T:(qi + 1) * T], s0t[:, d * NT + q, :, :].rearrange("p h v -> p (h v)"),
                                      qr[:, d, s, q, 1, :], start=False, stop=True, skip_group_check=True)
                last.then_inc(S("y_mm"), 1)

            for unit, j in ((kq, 0), (kq, 1), (z, 0), (kq, 2), (u, 0), (z, 1), (kq, 3), (u, 1), (z, 2), (y, 0),
                            (z, 3), (u, 2), (u, 3), (y, 1)):
                unit(j)
            if s == 0:
                for d in range(2):
                    for q in range(NT):
                        o = banks[d][:, q * P:(q + 1) * P]
                        mm(o, us[:, 2 * d + q // 2, q % 2, :, :].rearrange("p h v -> p (h v)"), bkt[:, 0, d, q * P:(q + 1) * P],
                           start=True, stop=False)
                        last = mm(o, vt[:, s, q * P:(q + 1) * P], bkt[:, 1, d, q * P:(q + 1) * P], start=False, stop=True)
                last.then_inc(S("state_mm"), 1)
        pe.wait_ge(S("y_evac"), 4)
        for q in range(NT):
            last = mm(banks[(4, 6)[q // 2]][:, (q % 2) * TT:(q % 2 + 1) * TT], bmean[:], kk[:, q, :], start=True, stop=True)
        last.then_inc(S("mean_mm"), 1)
        def branch(c0, src, bb, used, done, tiles=range(KT)):
            for m in tiles:
                c = c0 + m // 4
                arrived(pe, c)
                if m >= 2:
                    pe.wait_ge(S(used), m - 1)
                for k in range(4):
                    last = mm(banks[bb + m % 2][:, 0:TT], ring_in(c)[:, k, (m % 4) * P:(m % 4 + 1) * P], src[:, k, :],
                              start=(k == 0), stop=(k == 3))
                last.then_inc(S(done), 1)

        branch(C_POUT, pmT, 0, "pout_used", "pout_mm", range(2))
        pe.wait_ge(S("ysq_ready"), 1)
        for q in range(NT):
            last = mm(banks[(4, 6)[q // 2]][:, (q % 2) * TT:(q % 2 + 1) * TT], bmean[:], raw[:, q, :], start=True, stop=True)
        last.then_inc(S("var_mm"), 1)
        branch(C_POUT, pmT, 0, "pout_used", "pout_mm", range(2, KT))
        pe.wait_ge(S("yn_ready"), 1)
        branch(C_ROUT, kk, 2, "rout_used", "rout_mm")

        pe.wait_ge(S("rout_used"), KT)
        for c in range(4):
            arrived(pe, C_WO + c)
            for s in range(NS):
                n = 2 * c + s
                if n >= 4:
                    pe.wait_ge(S("wo_used"), n - 3)
                for k in range(KT):
                    last = mm(banks[(0, 1, 5, 4)[n % 4]][:, 0:256], ms[:, k, s * T:(s + 1) * T], ring_in(C_WO + c)[:, k, :],
                              start=(k == 0), stop=(k == KT - 1))
                last.then_inc(S("wo_mm"), 1)

        for s in range(NS):
            pe.wait_ge(S("xn2_ready"), s + 1)
            for k in range(KT):
                last = tr(banks[k // 2][:, (k % 2) * TT + s * T:(k % 2) * TT + (s + 1) * T], xn2[:, s, k * P:(k + 1) * P], ident[:])
        last.then_inc(S("xn2T_done"), 1)
        pe.wait_ge(S("hn2_ready"), 2)
        pe.wait_ge(S("router_in"), 32)
        for s in range(NS):
            for k in range(KT):
                mm(banks[5][:, s * NE:(s + 1) * NE], hnT[:, k, s * T:(s + 1) * T], rtw[:, k, :], start=(k == 0), stop=False)
            last = mm(banks[5][:, s * NE:(s + 1) * NE], ones[0:1, :], rtb[:], start=False, stop=True)
        last.then_inc(S("logits_mm"), 1)
        for s in range(NS):
            for k in range(KT):
                last = tr(banks[2 * s + k // 4][:, (k % 4) * P:(k % 4 + 1) * P], hnT[:, k, s * T:(s + 1) * T], ident[:])
        last.then_inc(S("x2_mm"), 1)
        pe.wait_ge(S("sel_done"), 1)
        mm(banks[6][:, 0:NE], upp[:], sel[:, 0, :], start=True, stop=True)
        mm(banks[6][:, NE:2 * NE], upp[:], sel[:, 1, :], start=True, stop=False)
        mm(banks[6][:, NE:2 * NE], ones[:], sel[:, 0, :], start=False, stop=True)
        for s in range(NS):
            last = mm(banks[6][0:NE, 64:65], sel[:, s, :], ones[:, 0:1], start=(s == 0), stop=(s == 1))
        last.then_inc(S("rank_mm"), 1)
        for s in range(NS):
            last = tr(banks[7][0:NE, s * T:(s + 1) * T], comb[:, s, :], ident[:])
        last.then_inc(S("combT_mm"), 1)
        pe.wait_ge(S("extra_ready"), 1)
        mm(banks[6][0:NE, 65:66], upp[0:NE, 0:NE], cnt[:, 1:2], start=True, stop=True)
        mm(banks[6][:, 66:67], ones[0:NE, :], cnt[:, 1:2], start=True, stop=True).then_inc(S("pos_mm"), 1)
        pe.wait_ge(S("e16_ready"), 1)
        mm(banks[6][:, 96:96 + EXTRA], eidx[0:NE, :], e16[:, 0, :], start=True, stop=True)
        mm(banks[6][:, 128:128 + EXTRA], ones[0:NE, :], e16[:, 1, :], start=True, stop=True).then_inc(S("list_mm"), 1)

        def gather():
            for k in range(KT):
                for s in range(NS):
                    last = mm(banks[6][:, k * SLOTS:(k + 1) * SLOTS], x2t[:, s, k * P:(k + 1) * P], p2[:, s, 0:SLOTS],
                              start=(s == 0), stop=(s == NS - 1))
            last.then_inc(S("gathered"), 1)

        pe.wait_ge(S("items_ready"), 1)
        n_items = pe.value_load(item[0:1, ITEMS:ITEMS + 1], min_val=NE, max_val=NE + EXTRA)
        pe.wait_ge(S("x2_ready"), 4)
        pe.wait_ge(S("combT_ready"), 1)
        pe.wait_ge(S("bdn_in"), 16)
        for s in range(NS):
            for h in range(2):
                mm(banks[2 * s + h][:, :], combT[:, s * T:(s + 1) * T], bdn[:, h * 512:(h + 1) * 512], start=True, stop=True)
        pe.wait_ge(S("sel_ready"), 1)
        gather()
        pe.wait_ge(S("bgu_in"), 16)
        with pe.Fori(0, n_items) as it:
            G, L = banks[4], banks[5]
            pe.wait_ge(S("xg_ready"), it + 1)
            pe.wait_ge(S("sele_ready"), it + 1)
            for h in range(2):
                r = slice(h * SLOTS, (h + 1) * SLOTS)
                mm(G[r, :], sele, bgu[:, h * 512:(h + 1) * 512], start=True, stop=False)
                mm(L[r, :], sele, bgu[:, FF + h * 512:FF + (h + 1) * 512], start=True, stop=False)
            for j in range(GU_CHUNKS):
                pe.wait_ge(S(f"slot{j}_full"), it * 16 + 16 * (FRONT_USES[j] + 1))
                for b, o in ((G, 0), (L, FF)):
                    for h in range(2):
                        last = mm(b[h * SLOTS:(h + 1) * SLOTS, :], xg[:, j, :], ring[:, j, o + h * 512:o + (h + 1) * 512],
                                  start=False, stop=(j == GU_CHUNKS - 1))
                last.then_inc(S("chunk_used"), 1)
            pe.wait_ge(S("sel_ready"), it + 2)
            gather()
            pe.wait_ge(S("pw_ready"), it + 1)
            for s in range(NS):
                last = tr(banks[7][:, s * T:(s + 1) * T], pw[:, s, :], ident[:])
            last.then_inc(S("pwt_done"), 1)
            pe.wait_ge(S("act_ready"), it + 1)
            for j in range(4):
                last = tr(L[:, j * P:(j + 1) * P], act_[:, j * P:(j + 1) * P], ident[:])
            last.then_inc(S("actT_done"), 1)
            pe.wait_ge(S("actT_ready"), it + 1)
            for j in range(DN_CHUNKS):
                pe.wait_ge(S(f"slot{GU_CHUNKS + j}_full"), it * 16 + 16 * (FRONT_USES[GU_CHUNKS + j] + 1))
                for i in range(2):
                    c = 2 * j + i
                    for h in range(2):
                        last = mm(G[h * SLOTS:(h + 1) * SLOTS, :], actT[:, c % 4, c // 4, :],
                                  ring[:, GU_CHUNKS + j, i * D + h * 512:i * D + (h + 1) * 512],
                                  start=(c == 0), stop=(c == 7))
                last.then_inc(S("chunk_used"), 1)
            pe.wait_ge(S("pwt_ready"), it + 1)
            pe.wait_ge(S("ysb_ready"), it + 1)
            for s in range(NS):
                for h in range(2):
                    r = slice(h * SLOTS, (h + 1) * SLOTS)
                    last = mm(banks[2 * s + h][:, :], pwt[r, s, :], ysb[r, :], start=False, stop=True, skip_group_check=True)
            last.then_inc(S("scattered"), 1)

    @block.scalar
    def _(act):
        af = nc.scalar.activation

        act.wait_ge(S("x_in"), 32)
        act.wait_ge(S("ident_ready"), 1)
        for s in range(NS):
            af(junk[:, s, :], x[:, s, :], ACT.Square, accum_out=stat[:, s:s + 1]).then_inc(S("sq_done"), 1)
        act.wait_ge(S("sq_done"), 2)
        af(stat[:, 2:4], stat[:, 0:2], ACT.Sqrt, bias=epsr[:], scale=1.0 / D).then_inc(S("rms1_ready"), 1)
        act.wait_ge(S("prm_ready"), 1)
        af(csig[:].rearrange("p s k -> p (s k)"), prm[:, 0:16], ACT.Sigmoid).then_inc(S("csig_ready"), 1)
        for g in range(2):
            act.wait_ge(S("moda_mm"), g + 1)
            af(mrow_a[:, g, :], unit_bank(g), ACT.Copy).then_inc(S("mrow_ready"), 1)
        act.wait_ge(S("xnT_done"), 1)
        act.wait_ge(S("moda_ready"), 1)
        for k in range(4):
            for s in range(NS):
                o = (k % 2) * TT + s * T
                last = af(hnT[:, k, s * T:(s + 1) * T], banks[1 + k // 2][:, o:o + T], ACT.Identity,
                          bias=moda[:, 0, k, s:s + 1], scale=moda[:, 1, k, s:s + 1])
        last.then_inc(S("hn_ready"), 1)
        for ct in range(RTILES):
            act.wait_ge(S("proj_done"), ct + 1)
            if ct >= 4:
                act.wait_ge(S("mix_done"), ct - 3)
            af(raw[:, ct % 4, :], PB[ct % 4][:, 0:TT], ACT.Copy).then_inc(S("raw_copied"), 1)
        fills = [0]

        def fill(part):
            for kind, i in FILL[part]:
                o = unit_bank(fills[0])
                if kind == "R":
                    act.wait_ge(S("modb_mm"), i + 1)
                    last = af(mrow_b[:, i, :], o, ACT.Copy)
                elif kind == "X":
                    act.wait_ge(S("modbt_mm"), i + 1)
                    last = af(modt[:, i, :, :].rearrange("p (j h) s -> p h j s", h=2),
                              o.rearrange("p (h j s) -> p h j s", h=2, j=MG)[:, :, :, 0:NS], ACT.Copy)
                else:
                    act.wait_ge(S("merge_mm"), max(i + 1, 2))
                    last = af(merge[:, i, :], o, ACT.Sigmoid, bias=prm[:, 80 + i:81 + i])
                last.then_inc(S("fill_used"), 1)
                fills[0] += 1

        fill(0)
        act.wait_ge(S("mix_done"), RTILES)
        af(pr[:, 12, :], pr[:, 12, :], ACT.Tanh)
        af(pr[:, 14, :], pr[:, 14, :], ACT.Sigmoid).then_inc(S("th_ready"), 1)
        for n in range(4):
            act.wait_ge(S("z_done"), n + 1)
            af(sig[:, n // 2, n % 2, :], banks[ZB[n]][:, :], ACT.Sigmoid).then_inc(S("sig_ready"), 1)
        fill(1)
        for j in range(4):
            d = j // 2
            act.wait_ge(S("a_done"), j + 1)
            for q in range(2 * (j % 2), 2 * (j % 2) + 2):
                last = af(aa[:, d, q, :], banks[ZB[j]][:, (q % 2) * TT:(q % 2 + 1) * TT], ACT.Sigmoid,
                          bias=prb[:, 19 + 4 * d + q:20 + 4 * d + q])
            last.then_inc(S("a_ready"), 1)
        fill(2)
        act.wait_ge(S("gate_done"), 1)
        for j in range(2):
            af(gate[:, 2 * j:2 * j + 2, :].rearrange("p c t -> p (c t)"), banks[(3, 0)[j]][:, :], ACT.Copy).then_inc(S("gate_ready"), 1)
        fill(3)
        act.wait_ge(S("norm_done"), 1)
        for j in range(2):
            af(raw[:, 2 * j:2 * j + 2, :].rearrange("p c t -> p (c t)"), banks[(6, 1)[j]][:, :], ACT.Sqrt).then_inc(S("nrm_ready"), 1)
        fill(4)
        fill(5)
        for i in range(8):
            d, s, t2 = i // 4, (i // 2) % 2, i % 2
            act.wait_ge(S("cum_done"), i + 1)
            ps = banks[CB[i % 3]][:].rearrange("p (q k t) -> p q k t", q=2, k=2)
            af(qr[:, d, s, 2 * t2:2 * t2 + 2, :, :].rearrange("p q k t -> p (q k t)"), banks[CB[i % 3]][:, :], ACT.Exp, scale=-DECAY)
            if s == 1:
                t0 = 0 if d == 0 else T - 1
                af(pms[:, d * NT + 2 * t2:d * NT + 2 * t2 + 2], ps[:, :, 0, t0], ACT.Exp, scale=DECAY)
            af(bt[:, d, s, 2 * t2:2 * t2 + 2, :], ps[:, :, 1, :], ACT.Exp, scale=DECAY).then_inc(S("cum_used"), 1)
        fill(6)
        fill(7)

        def mask_heads(dst, src, s, name):
            for h in range(2):
                for d in range(2):
                    last = af(dst[:, d, :, h, :], src[:, d, s, :, :], ACT.Copy, scale=hm[:, h:h + 1])
            last.then_inc(S(name), 1)

        for s in range(NS):
            act.wait_ge(S("scan_ops_ready"), s + 1)
            mask_heads(btm[s], bt, s, "btm_ready")
            if s == 0:
                mask_heads(ktm, kt_, s, "ktm_ready")
        def own_unit_bank(ps, h):
            return ps[:, h * 2 * T:(h + 1) * 2 * T].rearrange("p (q c) -> p q c", q=2)[:, :, h * HS:(h + 1) * HS]

        def z_out(n):
            act.wait_ge(S("z_mm"), n + 1)
            if n >= 2:
                act.wait_ge(S("u_mm"), n - 1)
            for h in range(2):
                last = af(zs[:, n % 2, :, h, :], own_unit_bank(banks[4], h), ACT.Copy, scale=-1.0)
            last.then_inc(S("z_evac"), 1)

        def u_out(n):
            tp, d = (n // 2) % 2, n % 2
            act.wait_ge(S("u_mm"), n + 1)
            for h in range(2):
                last = af(us[:, 2 * d + tp, :, h, :], own_unit_bank(banks[5], h), ACT.Copy)
            last.then_inc(S("u_evac"), 1)

        for s in range(NS):
            for unit, j in ((z_out, 0), (u_out, 0), (z_out, 1), (u_out, 1), (z_out, 2), (z_out, 3), (u_out, 2), (u_out, 3)):
                unit(4 * s + j)
            if s == 0:
                act.wait_ge(S("kq_mm"), 4)
                mask_heads(ktm, kt_, 1, "ktm_ready")
                act.wait_ge(S("state_mm"), 1)
                for h in range(2):
                    r = slice(h * HS, (h + 1) * HS)
                    for dd in range(2):
                        last = af(so[r, dd * NT:(dd + 1) * NT, :], banks[dd][r, :].rearrange("p (q k) -> p q k", q=NT)[:, :, r], ACT.Copy)
                last.then_inc(S("state_copied"), 1)
                act.wait_ge(S("state_copied"), 1)
                for dd in range(2):
                    for h in range(2):
                        act.dma_start(O[2 + dd][0, 0].rearrange("(q h) v k -> h v q k", h=2)[h],
                                      so[h * HS:(h + 1) * HS, dd * NT:(dd + 1) * NT, :]).then_inc(S("stored"), 16)
        act.wait_ge(S("var_mm"), 1)
        for j in range(2):
            af(raw[:, 2 * j:2 * j + 2, :].rearrange("p c t -> p (c t)"), banks[(4, 6)[j]][:, :], ACT.Sqrt, bias=epsg[:]).then_inc(S("gstd_ready"), 1)
        act.wait_ge(S("wo_used"), 8)
        for s in range(NS):
            af(x2t[:, s, :], x[:, s, :], ACT.Square, accum_out=stat[:, 4 + s:5 + s]).then_inc(S("sq_done"), 1)
        act.wait_ge(S("sq_done"), 4)
        af(stat[:, 6:8], stat[:, 4:6], ACT.Sqrt, bias=epsr[:], scale=1.0 / D).then_inc(S("rms2_ready"), 1)
        act.wait_ge(S("xn2T_done"), 1)
        act.wait_ge(S("gcol_ready"), 1)
        for k in range(4):
            for s in range(NS):
                o = (k % 2) * TT + s * T
                last = af(hnT[:, k, s * T:(s + 1) * T], banks[k // 2][:, o:o + T], ACT.Identity,
                          bias=modb[:, 1, k, s:s + 1], scale=modb[:, 2, k, s:s + 1])
        last.then_inc(S("hn2_ready"), 1)
        act.wait_ge(S("x2_mm"), 1)
        for j in range(2):
            af(x2t[:, 0, j * 512:(j + 1) * 512], banks[j][:, :], ACT.Copy).then_inc(S("x2_ready"), 1)
        act.wait_ge(S("top_ready"), 1)
        for s in range(NS):
            last = af(tw[:, s, :], top8[:, s, 0:4], ACT.Exp, bias=fstat[:, s:s + 1])
        last.then_inc(S("exp_ready"), 1)
        act.wait_ge(S("combT_mm"), 1)
        af(combT, banks[7][0:NE, 0:TT], ACT.Copy).then_inc(S("combT_ready"), 1)

        act.wait_ge(S("items_ready"), 1)
        n_items = act.value_load(item[0:1, ITEMS:ITEMS + 1], min_val=NE, max_val=NE + EXTRA)

        def gathered_out(n):
            act.wait_ge(S("gathered"), n)
            af(xg.rearrange("p k s -> p (k s)"), banks[6][:, :], ACT.Copy).then_inc(S("xg_ready"), 1)

        gathered_out(1)
        with act.Fori(0, n_items) as it:
            act.wait_ge(S("g_ready"), it + 1)
            af(sgb, gsb, ACT.Sigmoid, scale=ALPHA).then_inc(S("sg_ready"), 1)
            gathered_out(it + 2)
            act.wait_ge(S("pwt_done"), it + 1)
            af(pwt.rearrange("p s t -> p (s t)"), banks[7][:, 0:TT], ACT.Copy).then_inc(S("pwt_ready"), 1)
            act.wait_ge(S("chunk_used"), it * RING + RING)
            af(ysb, banks[4][:, :], ACT.Copy).then_inc(S("ysb_ready"), 1)

        act.wait_ge(S("res_ready"), 1)
        for s in range(NS):
            af(hnT[:, 4 * s:4 * s + 4, :].rearrange("p k t -> p (k t)"), x[:, s, :], ACT.Square, accum_out=fstat[:, s:s + 1]).then_inc(S("sq_done"), 1)
        act.wait_ge(S("sq_done"), 6)
        af(fstat[:, 2:4], fstat[:, 0:2], ACT.Sqrt, bias=epsr[:], scale=1.0 / D).then_inc(S("rms3_ready"), 1)
        for s in range(NS):
            act.wait_ge(S("out_ready"), s + 1)
            act.dma_start(O[s][0], x[:, s, :]).then_inc(S("stored"), 16)

    @block.vector
    def _(dve):
        v = nc.vector
        MUL, ADD, SUB = ALU.mult, ALU.add, ALU.subtract
        n = [0]

        def step(ins):
            n[0] += 1
            ins.then_inc(S("dve_step"), 1)

        def sync():
            dve.wait_ge(S("dve_step"), n[0])

        def own(ins):
            step(ins)
            sync()

        def last_of(name, count):
            dve.wait_ge(S(name), count)

        def bc(ap, m):
            return ap.unsqueeze(1).to_broadcast([P, m, ap.shape[-1]])

        def col(ap, m):
            return ap.unsqueeze(2).to_broadcast([P, ap.shape[-1], m])

        dve.wait_ge(S("prmT_done"), 1)
        v.tensor_copy(prm[:], banks[0][:, 0:96]).then_inc(S("prm_ready"), 1)
        dve.wait_ge(S("rms1_ready"), 1)
        own(v.reciprocal(stat[:, 0:2], stat[:, 2:4]))
        for s in range(NS):
            v.tensor_scalar(xn[:, s, :], x[:, s, :], stat[:, s:s + 1], None, MUL).then_inc(S("xn_ready"), 1)
        last_of("prm_ready", 1)
        dve.wait_ge(S("csig_ready"), 1)
        v.tensor_tensor(cpad[:, :, 0:NS].rearrange("p k s -> p s k"), prm[:, 0:16].rearrange("p (s k) -> p s k", s=NS), csig[:], MUL).then_inc(S("cpad_ready"), 1)
        own(v.reduce_sum(par4[:], ident[:].rearrange("p (n j) -> p j n", j=4), axis=AX.X))
        own(v.tensor_tensor(par2[:], par4[:, 0:2], par4[:, 2:4], ADD))
        dve.wait_ge(S("prbT_done"), 1)
        own(v.tensor_copy(prb[:], banks[0][:, 128:183]))
        m15 = prb[:, 0:RTILES]
        step(v.tensor_scalar(mu[:, 0, :], m15, -1.0, 1.0, MUL, ADD))
        for j in range(2):
            step(v.tensor_scalar(mu[:, 1 + j, :], m15, par2[:, j:j + 1], None, MUL))
        for j in range(4):
            step(v.tensor_scalar(mu[:, 3 + j, :], m15, par4[:, j:j + 1], None, MUL))
        v.tensor_scalar(kam[:], prb[:, 31:35], -1.0, 1.0, MUL, ADD).then_inc(S("prb_ready"), 1)
        dve.wait_ge(S("modat_mm"), 2)
        for g in range(2):
            step(v.tensor_tensor(moda[:, g, :, :].rearrange("p (j h) s -> p h j s", h=2),
                                 banks[6][:, g * MW:(g + 1) * MW].rearrange("p (h j s) -> p h j s", h=2, j=MG)[:, :, :, 0:NS],
                                 prm[:, 16 + KT * g:16 + KT * (g + 1)].rearrange("p (j h) -> p h j", h=2).unsqueeze(3).to_broadcast([P, 2, MG, NS]), ADD))
        sync()
        v.scalar_tensor_tensor(moda[:, 1, :, :], moda[:, 1, :, :], 1.0, col(prm[:, 64:72], NS), ADD, MUL).then_inc(S("moda_ready"), 1)
        last_of("moda_ready", 1)
        dve.wait_ge(S("xnT_done"), 1)
        for k in range(4, KT):
            for s in range(NS):
                o = (k % 2) * TT + s * T
                last = v.tensor_scalar(hnT[:, k, s * T:(s + 1) * T], banks[1 + k // 2][:, o:o + T], moda[:, 1, k, s:s + 1],
                                       moda[:, 0, k, s:s + 1], MUL, ADD)
        last.then_inc(S("hn_ready"), 1)
        dve.wait_ge(S("masks_ready"), 1)
        prev = ident[:]
        for i in range(7):
            m = 2 ** (i + 1)
            if m < P:
                dve.wait_ge(S("bd_ready"), i + 1)
                cur = bdm[:, (i + 1) % 2, :]
            else:
                cur = ones[:]
            own(v.tensor_tensor(lvl[:, i, 0, :], cur, prev, SUB))
            step(v.tensor_tensor(lvl[:, i, 1, :], lvl[:, i, 0, :], upp[:], MUL))
            v.tensor_tensor(lvl[:, i, 0, :], lvl[:, i, 0, :], low, MUL).then_inc(S("bd_used"), 1)
            prev = cur
        step(v.tensor_scalar(tri[:, 0, :, :], mqr[:, 0, :, :], rowlo[:], None, SUB))
        v.tensor_scalar(tri[:, 1, :, :], mqr[:, 1, :, :], rowlo[:], -1.0, ADD, ADD).then_inc(S("tri_ready"), 1)

        last_of("prb_ready", 1)
        sync()
        for ct in range(RTILES):
            dve.wait_ge(S("raw_copied"), ct + 1)
            r_ = raw[:, ct % 4, :]
            o_ = pr[:, ct, :]
            own(v.tensor_scalar(o_, r_, mu[:, 0, ct:ct + 1], None, MUL))

            def add(dst, src, j):
                return v.scalar_tensor_tensor(dst, src, mu[:, j, ct:ct + 1], dst, MUL, ADD)

            og, rg = o_[:, T:TT].rearrange("p (r c) -> p r c", c=GRID_W), r_[:, T:TT].rearrange("p (r c) -> p r c", c=GRID_W)
            step(add(o_[:, 1:T], r_[:, 0:T - 1], 1))
            own(add(og[:, :, 1:], rg[:, :, :-1], 3))
            step(add(o_[:, 0:T - 1], r_[:, 1:T], 2))
            own(add(og[:, :, :-1], rg[:, :, 1:], 4))
            own(add(og[:, 1:, :], rg[:, :-1, :], 5))
            add(og[:, :-1, :], rg[:, 1:, :], 6).then_inc(S("mix_done"), 1)
        last_of("mix_done", RTILES)

        dve.wait_ge(S("pcnt_done"), 1)
        cbuf = corr[:].rearrange("p c t -> p (c t)")[:, 0:512]
        pbf = pband.rearrange("p g t -> p (g t)")
        own(v.reciprocal(cbuf, banks[4][:, :]))
        own(v.tensor_tensor(pbf, pbf, cbuf, MUL))
        v.tensor_tensor(pband, pband, bc(ident[:], 4), SUB).then_inc(S("pband_ready"), 1)
        dve.wait_ge(S("pu_mm"), 2)
        for s in range(NS):
            v.tensor_copy(utok[:, s, :], banks[2 + s][:, :]).then_inc(S("utok_ready"), 1)
        for q in range(NT):
            step(v.tensor_scalar(kk[:, q, :], pr[:, 4 + q, :], prb[:, 27 + q:28 + q], None, MUL))
        sync()
        v.tensor_tensor(raw[:], kk[:], kk[:], MUL).then_inc(S("ksq_ready"), 1)
        dve.wait_ge(S("pooled_done"), 1)
        for j in range(2):
            v.tensor_copy(pooled[:, 2 * j:2 * j + 2, :].rearrange("p g t -> p (g t)"), banks[2 + j][:, :]).then_inc(S("pooled_ready"), 1)
        dve.wait_ge(S("mixed_done"), 1)
        for j in range(2):
            for g in (2 * j, 2 * j + 1):
                last = v.tensor_scalar(pmT[:, g, :], banks[(4, 2)[j]][:, (g % 2) * TT:(g % 2 + 1) * TT], prb[:, 15 + g:16 + g], None, MUL)
            last.then_inc(S("mixed_ready"), 1)
        dve.wait_ge(S("a_ready"), 4)
        for d in range(2):
            for q in range(NT):
                step(v.tensor_scalar(kd[:, d, q, :], aa[:, d, q, :], prb[:, 31 + q:32 + q], kam[:, q:q + 1], MUL, ADD))
        sync()
        for d in range(2):
            step(v.tensor_tensor(kd[:, d, :, :], kd[:, d, :, :], pr[:, 4:8, :], MUL))
        dve.wait_ge(S("vt_done"), 1)
        for s in range(NS):
            v.tensor_copy(vt[:, s, :], banks[(2, 0)[s]][:, :]).then_inc(S("vt_ready"), 1)
        dve.wait_ge(S("nrm_ready"), 2)
        own(v.tensor_scalar(raw[:], raw[:], 1e-12, None, ALU.max))
        own(v.reciprocal(raw[:], raw[:]))
        v.tensor_tensor(kk[:], kk[:], raw[:], MUL).then_inc(S("kk_ready"), 1)
        last_of("kk_ready", 1)
        own(v.tensor_tensor(raw[:], kd[:, 0, :, :], kd[:, 1, :, :], ADD))
        own(v.tensor_tensor(raw[:], raw[:], pr[:, 0:4, :], MUL))
        for q in range(NT):
            last = v.tensor_scalar(raw[:, q, :], raw[:, q, :], prb[:, 35 + q:36 + q], None, MUL)
        last.then_inc(S("rkk_ready"), 1)
        dve.wait_ge(S("rk_done"), 1)
        for j in range(2):
            step(v.tensor_tensor(corr[:, 2 * j:2 * j + 2, :].rearrange("p c t -> p (c t)"), pr[:, 8 + 2 * j:10 + 2 * j, :].rearrange("p c t -> p (c t)"),
                                 banks[(3, 1)[j]][:, :], MUL))

        dve.wait_ge(S("cum_used"), 8)
        dve.wait_ge(S("s0_done"), 1)
        for h in range(2):
            r = slice(h * HS, (h + 1) * HS)
            step(v.tensor_tensor(s0t[r, :, h, :], banks[4][r, :].rearrange("p (i v) -> p i v", v=HS),
                                 pms[r, :].unsqueeze(2).to_broadcast([HS, 2 * NT, HS]), MUL))
        step(v.tensor_copy(fin[:, 0, :], qr[:, 0, 0, :, 1, T - 1]))
        own(v.tensor_copy(fin[:, 1, :], qr[:, 1, 0, :, 1, 0]))
        for s in range(NS):
            ts = slice(s * T, (s + 1) * T)
            for d in range(2):
                step(v.tensor_tensor(qr[:, d, s, :, 0, :], qr[:, d, s, :, 0, :], kk[:, :, ts], MUL))
                step(v.tensor_tensor(qr[:, d, s, :, 1, :], qr[:, d, s, :, 1, :], pr[:, 0:4, ts], MUL))
                step(v.tensor_tensor(kt_[:, d, s, :, :], bt[:, d, s, :, :], kd[:, d, :, ts], MUL))
                own(v.tensor_tensor(bt[:, d, s, :, :], bt[:, d, s, :, :], aa[:, d, :, ts], MUL))
                last = v.tensor_tensor(bt[:, d, s, :, :], bt[:, d, s, :, :], kk[:, :, ts], MUL)
                if d == 0:
                    step(last)
            last.then_inc(S("scan_ops_ready"), 1)
            last_of("scan_ops_ready", s + 1)
        dve.wait_ge(S("fill_used"), UNITS.index(("X", 3)) + 1)
        own(v.tensor_tensor(modb[:].rearrange("p g k s -> p (g k) s"), modt[:].rearrange("p g k s -> p (g k) s"),
                            col(prm[:, 32:64], NS), ADD))
        step(v.scalar_tensor_tensor(modb[:, 2, :, :], modb[:, 2, :, :], 1.0, col(prm[:, 72:80], NS), ADD, MUL))
        for gi, m in enumerate((0, 3)):
            last = v.tensor_copy(gcol[:, gi, :, :], modb[:, m, :, :].rearrange("p k s -> p s k"))
            if gi == 0:
                step(last)
        last.then_inc(S("gcol_ready"), 1)
        dve.wait_ge(S("grow_done"), 1)
        v.tensor_copy(grow, banks[5][0:32, 128:256]).then_inc(S("grow_ready"), 1)
        for j, src in enumerate((bt, kt_)):
            for d in range(2):
                if j:
                    dve.wait_ge(S("bk_done"), d + 1)
                v.tensor_tensor(bfin[:, d, :, :], src[:, d, 0, :, :], col(fin[:, d, :], T), MUL).then_inc(S("bf_ready"), 1)
            for d in range(2):
                dve.wait_ge(S("bk_done"), 2 * j + d + 1)
                v.tensor_copy(bkt[:, j, d, :], banks[(3, 1)[d]][:, :]).then_inc(S("bk_ready"), 1)

        def b4(i):
            return banks[i][:].rearrange("p (i t) -> p i t", i=4)

        for s in range(NS):
            for g in range(4):
                d = g // 2
                ba, bat = 2 * (g % 2), 2 * (g % 2) + 1
                dve.wait_ge(S("a_mm"), 4 * s + g + 1)
                for h, b in enumerate((ba, bat)):
                    hs = slice(2 * h, 2 * h + 2)
                    step(v.tensor_tensor(work[:, g, W_M, hs, :], b4(b)[:, 0:2, :], bc(lvl[:, 0, d, :], 2), MUL))
                    step(v.tensor_tensor(work[:, g, W_AT, hs, :], b4(b)[:, 2:4, :], bc(mqr[:, d, 0, :], 2), MUL))
                sync()
                step(v.tensor_tensor(work[:, g, W_X, :, :], bc(ident[:], 4), work[:, g, W_M, :, :], SUB))
                own(v.tensor_tensor(work[:, g, W_XT, :, :], work[:, g, W_AT, :, :], bc(lvl[:, 0, 1 - d, :], 4), MUL))
                v.tensor_tensor(work[:, g, W_XT, :, :], bc(ident[:], 4), work[:, g, W_XT, :, :], SUB).then_inc(S("a_evac"), 1)
            last_of("a_evac", 4 * s + 4)
            for l in range(1, 7):
                for g in range(4):
                    dve.wait_ge(S("m_mm"), 24 * s + 4 * (l - 1) + g + 1)
                    v.tensor_tensor(work[:, g, W_M, :, :], b4(4 + g % 2), bc(lvl[:, l, g // 2, :], 4), MUL).then_inc(S("m_evac"), 1)
                for g in range(4):
                    dve.wait_ge(S("x_mm"), 24 * s + 4 * (l - 1) + g + 1)
                    bx, bxt = XB[g % 2]
                    if l < 6:
                        step(v.tensor_tensor(work[:, g, W_X, :, :], work[:, g, W_X, :, :], b4(bx), SUB))
                    v.tensor_tensor(work[:, g, W_XT, :, :], work[:, g, W_XT, :, :], b4(bxt), SUB).then_inc(S("x_upd"), 1)
                last_of("x_upd", 24 * s + 4 * l)
            def kq_out(j):
                tp, d = j // 2, j % 2
                g = 2 * d + tp
                dve.wait_ge(S("kq_mm"), 4 * s + j + 1)
                for i in range(2):
                    step(v.tensor_tensor(kqm(g)[:, 2 * i:2 * i + 2, :, :].rearrange("p i k t -> p i (k t)"),
                                         banks[2 * (j % 2) + i][:].rearrange("p (i c) -> p i c", i=2),
                                         bc(mqr[:, d, :, :].rearrange("p k t -> p (k t)"), 2), MUL))
                v.tensor_tensor(work[:, g, W_AT, :, :], b4(6 + j % 2), bc(mqr[:, d, 1, :], 4), MUL).then_inc(S("kq_evac"), 1)

            def y_out(tp):
                dve.wait_ge(S("y_mm"), 2 * s + tp + 1)
                v.tensor_tensor(kk[:, 2 * tp:2 * tp + 2, s * T:(s + 1) * T], banks[5][:, 0:2 * T].rearrange("p (q t) -> p q t", q=2),
                                corr[:, 2 * tp:2 * tp + 2, s * T:(s + 1) * T], ADD).then_inc(S("y_evac"), 1)

            for unit, j in ((kq_out, 0), (kq_out, 1), (kq_out, 2), (kq_out, 3), (y_out, 0), (y_out, 1)):
                unit(j)

        last_of("y_evac", 4)
        dve.wait_ge(S("mean_mm"), 1)

        def pair(ap, j):
            return ap[:, 2 * j:2 * j + 2, :].rearrange("p c t -> p (c t)")

        for j in range(2):
            step(v.tensor_tensor(pair(kk, j), pair(kk, j), banks[(4, 6)[j]][:, :], SUB))
        sync()
        dve.wait_ge(S("stored"), 64)
        v.tensor_tensor(raw[:], kk[:], kk[:], MUL).then_inc(S("ysq_ready"), 1)
        dve.wait_ge(S("gstd_ready"), 2)
        own(v.reciprocal(raw[:], raw[:]))
        own(v.tensor_tensor(kk[:], kk[:], raw[:], MUL))
        for q in range(NT):
            step(v.tensor_scalar(kk[:, q, :], kk[:, q, :], prb[:, 39 + q:40 + q], prb[:, 43 + q:44 + q], MUL, ADD))
        sync()
        v.tensor_tensor(kk[:], kk[:], gate[:], MUL).then_inc(S("yn_ready"), 1)
        for m in range(KT):
            dve.wait_ge(S("pout_mm"), m + 1)
            v.tensor_tensor(ms[:, m, :], merge[:, m, :], banks[m % 2][:, 0:TT], MUL).then_inc(S("pout_used"), 1)
        last_of("yn_ready", 1)
        last_of("pout_used", KT)
        for m in range(KT):
            dve.wait_ge(S("rout_mm"), m + 1)
            own(v.tensor_tensor(gate[:, m % 4, :], merge[:, KT + m, :], banks[2 + m % 2][:, 0:TT], MUL))
            v.tensor_tensor(ms[:, m, :], ms[:, m, :], gate[:, m % 4, :], ADD).then_inc(S("rout_used"), 1)
        dve.wait_ge(S("gbc_in"), 32)
        for c in range(4):
            for s in range(NS):
                i = 2 * c + s
                dve.wait_ge(S("wo_mm"), i + 1)
                cs = slice(256 * c, 256 * c + 256)
                own(v.tensor_tensor(corr[:, i % 4, :], banks[(0, 1, 5, 4)[i % 4]][:, 0:256], gbc[:, s, cs], MUL))
                v.tensor_tensor(x[:, s, cs], x[:, s, cs], corr[:, i % 4, :], ADD).then_inc(S("wo_used"), 1)
        last_of("wo_used", 8)
        dve.wait_ge(S("rms2_ready"), 1)
        own(v.reciprocal(stat[:, 4:6], stat[:, 6:8]))
        for s in range(NS):
            v.tensor_scalar(xn2[:, s, :], x[:, s, :], stat[:, 4 + s:5 + s], None, MUL).then_inc(S("xn2_ready"), 1)
        dve.wait_ge(S("xn2T_done"), 1)
        last_of("gcol_ready", 1)
        for k in range(4, KT):
            for s in range(NS):
                o = (k % 2) * TT + s * T
                last = v.tensor_scalar(hnT[:, k, s * T:(s + 1) * T], banks[k // 2][:, o:o + T], modb[:, 2, k, s:s + 1],
                                       modb[:, 1, k, s:s + 1], MUL, ADD)
        last.then_inc(S("hn2_ready"), 1)

        dve.wait_ge(S("logits_mm"), 1)
        own(v.tensor_copy(lg[:].rearrange("p s e -> p (s e)"), banks[5][:, 0:NS * NE]))
        for s in range(NS):
            own(v.max(top8[:, s, :], lg[:, s, :]))
            own(v.max_index(idx8[:, s, :], top8[:, s, :], lg[:, s, :]))
        step(v.tensor_copy(idxf[:], idx8[:]))
        v.tensor_scalar(fstat[:, 0:2], top8[:, :, 0], -1.0, None, MUL).then_inc(S("top_ready"), 1)
        dve.wait_ge(S("x2_mm"), 1)
        for j in range(2):
            v.tensor_copy(x2t[:, 1, j * 512:(j + 1) * 512], banks[2 + j][:, :]).then_inc(S("x2_ready"), 1)
        dve.wait_ge(S("exp_ready"), 1)
        own(v.reduce_sum(fstat[:, 2:4], tw[:], axis=AX.X))
        own(v.reciprocal(fstat[:, 2:4], fstat[:, 2:4]))
        for s in range(NS):
            own(v.tensor_scalar(twn[:, s, :], tw[:, s, :], fstat[:, 2 + s:3 + s], None, MUL))
        dve.wait_ge(S("lists_ready"), 1)
        for s in range(NS):
            for j in range(4):
                d0, d1 = (sel[:, s, :], comb[:, s, :]) if j == 0 else (oh[:], lg[:, s, :])
                step(v.tensor_scalar(d0, iota2[:, 0:NE], idxf[:, s, j:j + 1], None, ALU.is_equal))
                own(v.tensor_scalar(d1, iota2[:, 0:NE], idxf[:, s, j:j + 1], twn[:, s, j:j + 1], ALU.is_equal, MUL))
                if j:
                    step(v.tensor_tensor(sel[:, s, :], sel[:, s, :], oh[:], ADD))
                    own(v.tensor_tensor(comb[:, s, :], comb[:, s, :], lg[:, s, :], ADD))
        v.tensor_copy(oh[:], sel[:, 0, :]).then_inc(S("sel_done"), 1)
        dve.wait_ge(S("rank_mm"), 1)
        own(v.scalar_tensor_tensor(rank[:], banks[6][:, 0:2 * NE].rearrange("p (s e) -> p s e", s=NS), 1.0, sel[:], ADD, MUL))
        step(v.tensor_scalar(rank[:], rank[:], -1.0, None, ADD))
        own(v.tensor_copy(cnt[:, 0:1], banks[6][0:NE, 64:65]))
        own(v.tensor_scalar(fl[:], thr3[0:NE, :], cnt[:, 0:1], None, ALU.is_lt))
        v.reduce_sum(cnt[:, 1:2], fl[:], axis=AX.X).then_inc(S("extra_ready"), 1)
        dve.wait_ge(S("pos_mm"), 1)
        own(v.tensor_copy(cnt[:, 2:3], banks[6][0:NE, 65:66]))
        own(v.tensor_scalar(posc[:], iota3[0:NE, :], cnt[:, 2:3], None, ADD))
        for c in range(3):
            own(v.tensor_scalar(oh16[:, c, :], iota2[0:NE, 0:EXTRA], posc[:, c:c + 1], fl[:, c:c + 1], ALU.is_equal, MUL))
        step(v.tensor_tensor(e16[:, 0, :], oh16[:, 0, :], oh16[:, 1, :], ADD))
        own(v.scalar_tensor_tensor(e16[:, 1, :], oh16[:, 1, :], 2.0, oh16[:, 0, :], MUL, ADD))
        step(v.tensor_tensor(e16[:, 0, :], e16[:, 0, :], oh16[:, 2, :], ADD))
        own(v.scalar_tensor_tensor(e16[:, 1, :], oh16[:, 2, :], 3.0, e16[:, 1, :], MUL, ADD))
        v.tensor_scalar(e16[:, 1, :], e16[:, 1, :], float(SLOTS), None, MUL).then_inc(S("e16_ready"), 1)
        dve.wait_ge(S("list_mm"), 1)
        step(v.tensor_copy(item[0:1, NE:NE + EXTRA], banks[6][0:1, 96:96 + EXTRA]))
        step(v.tensor_copy(base[:, NE:NE + EXTRA], banks[6][:, 128:128 + EXTRA]))
        own(v.tensor_scalar(item[0:1, ITEMS:ITEMS + 1], banks[6][0:1, 66:67], float(NE), None, ADD))

        def choose(n, e):
            for s in range(NS):
                last = v.tensor_scalar(p2[:, s, :], iota2[:], base[:, bass.ds(n, 1)], rank[:, s, bass.ds(e, 1)], ADD, ALU.is_equal)
            last.then_inc(S("sel_ready"), 1)

        def expert_row(e):
            v.tensor_copy(sele, ident[0:NE, bass.ds(e, 1)].to_broadcast([NE, SLOTS])).then_inc(S("sele_ready"), 1)

        v.tensor_copy(oh[:], sel[:, 0, :]).then_inc(S("items_ready"), 1)
        dve.wait_ge(S("items_ready"), 1)
        n_items = dve.value_load(item[0:1, ITEMS:ITEMS + 1], min_val=NE, max_val=NE + EXTRA)
        dve.wait_ge(S("combT_mm"), 1)
        choose(0, 0)
        expert_row(0)
        with dve.Fori(0, n_items) as it:
            e = dve.value_load(item[0:1, bass.ds(it, 1)], min_val=0, max_val=NE - 1)
            nxt = dve.value_load(item[0:1, bass.ds(it + 1, 1)], min_val=0, max_val=NE - 1)
            dve.wait_ge(S("sel_ready"), it + 1)
            for s in range(NS):
                last = v.tensor_scalar(pw[:, s, :], p2[:, s, :], comb[:, s, bass.ds(e, 1)], None, MUL)
            last.then_inc(S("pw_ready"), 1)
            dve.wait_ge(S("pw_ready"), it + 1)
            dve.wait_ge(S("gathered"), it + 1)
            choose(it + 1, nxt)
            dve.wait_ge(S("chunk_used"), it * RING + GU_CHUNKS)
            v.tensor_scalar(gsb, banks[4][:, :], LIMIT, None, ALU.min).then_inc(S("g_ready"), 1)
            v.tensor_scalar(lcb, banks[5][:, :], LIMIT, -LIMIT, ALU.min, ALU.max).then_inc(S("lin_done"), 1)
            expert_row(nxt)
            dve.wait_ge(S("lin_done"), it + 1)
            v.scalar_tensor_tensor(lcb, lcb, 1.0, gsb, ADD, MUL).then_inc(S("gl_done"), 1)
            dve.wait_ge(S("gl_done"), it + 1)
            dve.wait_ge(S("sg_ready"), it + 1)
            v.tensor_tensor(act_, lcb, sgb, MUL).then_inc(S("act_ready"), 1)
            dve.wait_ge(S("actT_done"), it + 1)
            v.tensor_copy(actT.rearrange("p j h s -> p (j h s)"), banks[5][:, :]).then_inc(S("actT_ready"), 1)

        dve.wait_ge(S("scattered"), n_items)
        dve.wait_ge(S("gbc_in"), 64)
        dve.wait_ge(S("wfin_in"), 16)
        for s in range(NS):
            for h in range(2):
                cs = slice(512 * h, 512 * h + 512)
                step(v.tensor_tensor(gbc[:, s, cs], gbc[:, s, cs], banks[2 * s + h][:, :], MUL))
        sync()
        v.tensor_tensor(x[:], x[:], gbc, ADD).then_inc(S("res_ready"), 1)
        last_of("res_ready", 1)
        dve.wait_ge(S("rms3_ready"), 1)
        own(v.reciprocal(fstat[:, 2:4], fstat[:, 2:4]))
        for s in range(NS):
            v.scalar_tensor_tensor(x[:, s, :], x[:, s, :], fstat[:, 2 + s:3 + s], wbuf, MUL, MUL).then_inc(S("out_ready"), 1)

    return ctx


_INS = ['x_prompt', 'x_sample', 'state_fwd', 'state_bwd', 'c', 'c_ctx', 'w_mod', 'b_mod', 'norm_mix_w', 'w_in', 'b_merge',
        'pool_w', 'pool_scale', 'w_pool_out', 'shift_mu', 'decay_w0', 'decay_w2', 'iclr_a0', 'iclr_a2', 'gate_w2',
        'k_k', 'k_a', 'r_k', 'ln_x_w', 'ln_x_b', 'w_rwkv_out', 'w_o', 'norm_ffn_w', 'router_w', 'router_b',
        'expert_w_gu', 'expert_b_gu', 'expert_w_down', 'expert_b_down', 'norm_final_w']
_OUTS = [(1, 128, 1024), (1, 128, 1024), (1, 1, 8, 64, 64), (1, 1, 8, 64, 64)]


def kernel(**inputs):
    import numpy as np
    import concourse.bacc as bacc
    from concourse.bass_utils import run_bass_kernel_spmd

    nc = bacc.Bacc("TRN2", target_bir_lowering=False, num_devices=1)
    arrays, A = {}, {}
    for name in _INS:
        a = np.ascontiguousarray(inputs[name])
        arrays[f"in_{name}"] = a
        A[name] = nc.dram_tensor(f"in_{name}", a.shape, mybir.dt.from_np(a.dtype), kind="ExternalInput").ap()
    outs = [nc.dram_tensor(f"out_{i}", s, F32, kind="ExternalOutput").ap() for i, s in enumerate(_OUTS)]
    scratch = nc.dram_tensor("gate_rows", (2, NS, D), F32, kind="Internal").ap()
    ctx = trunk_kernel(nc, A, outs, scratch)
    ctx.close()
    r = run_bass_kernel_spmd(nc, [arrays], core_ids=[0])
    return tuple(r.results[0][f"out_{i}"] for i in range(4))
```

```python
import concourse.bass as bass
from concourse import mybir
from contextlib import ExitStack

F32 = mybir.dt.float32
I32 = mybir.dt.int32
U32 = mybir.dt.uint32
ALU = mybir.AluOpType
ACT = mybir.ActivationFunctionType
AX = mybir.AxisListType

P = 128
D = 1024
T = 128
NS = 2
TT = NS * T
KT = D // P
POOLW = 512
RW = 512
NT = RW // P
HS = 64
GRID_W = 64
RCOLS = 3 * RW + 3 * P
RTILES = RCOLS // P
OFF_M = POOLW + RCOLS
WINDOWS = (2, 4, 8, 16)
NE = 32
FF = 1024
SLOTS = 64
EXTRA = 16
ITEMS = NE + EXTRA + 1
DECAY = 0.6065306597126334
LIMIT = 7.0
ALPHA = 1.702
RMS_EPS = 1e-6
GN_EPS = 1e-5 * HS

RING = 12
FRING = 8
CW = 2048
GU_CHUNKS = KT
DN_CHUNKS = 4


MC = 4
MG = 4
MW = D // MG


def front_chunks():
    out = [("w_mod", D * g, D, 2 * r) for g in range(2) for r in range(MC)]
    out += [("w_in", POOLW + 256 * i, 256, 0) for i in range(RTILES // 2)] + [("w_in", OFF_M - P, P, 0)]
    out += [("w_in", 0, 256, 0), ("w_in", 256, 256, 0)]
    out += [("w_mod", D * g, D, 2 * r) for g in range(2, 6) for r in range(MC)]
    out += [("w_in", OFF_M + 256 * i, 256, 0) for i in range(8)]
    out += [("w_pool_out", 512 * i, 512, 0) for i in range(2)]
    out += [("w_rwkv_out", 512 * i, 512, 0) for i in range(2)]
    out += [("w_o", 256 * i, 256, 0) for i in range(4)]
    return out


CHUNKS = front_chunks()
NF = len(CHUNKS)
C_MODA, C_RWKV, C_POOL, C_MODB, C_MERGE, C_POUT, C_ROUT, C_WO = 0, 8, 16, 18, 34, 42, 44, 46


def released(c):
    if c < C_RWKV:
        return "moda_mm", c + 1
    if c < C_POOL:
        return "proj_done", min(2 * (c - C_RWKV) + 2, RTILES)
    if c < C_MODB:
        return "pu_mm", c - C_POOL + 1
    if c < C_MERGE:
        return "modb_mm", c - C_MODB + 1
    if c < C_POUT:
        return "merge_mm", 2 * (c - C_MERGE) + 2
    if c < C_ROUT:
        return "pout_mm", 4 * (c - C_POUT) + 4
    if c < C_WO:
        return "rout_mm", 4 * (c - C_ROUT) + 4
    return "wo_mm", 2 * (c - C_WO) + 2


def slot_of(c):
    return c % FRING if c < C_POUT else (6, 7, 0, 1, 4, 5, 2, 3)[c - C_POUT]


def freed(c):
    if c < C_POUT:
        return released(c - FRING)
    if c < C_WO:
        return released(C_MERGE + (c - C_POUT) + 4)
    return (("kq_mm", 4), ("kq_mm", 8), ("rout_used", KT), ("rout_used", KT))[c - C_WO]


USE = [sum(slot_of(b) == slot_of(c) for b in range(c + 1)) for c in range(NF)]
FRONT_USES = [sum(slot_of(c) == s for c in range(NF)) for s in range(RING)]


def trunk_kernel(nc, A, O, scratch):
    ctx = ExitStack()
    sems = {}

    def S(name):
        if name not in sems:
            sems[name] = ctx.enter_context(nc.semaphore(name))
        return sems[name]

    def sb(name, shape, dt=F32):
        return ctx.enter_context(nc.sbuf_tensor(name, shape, dt))

    ring = sb("ring", [P, RING, CW])

    ident = sb("ident", [P, P])
    ones = sb("ones", [P, P])
    upp = sb("upp", [P, P])
    mqr = sb("mqr", [P, 2, 2, P])
    lvl = sb("lvl", [P, 7, 2, P])
    bmean = sb("bmean", [P, P])
    rowlo = sb("rowlo", [P, 1])
    iotai = sb("iotai", [P, P], I32)
    iota2 = sb("iota2", [P, P])
    eidx = sb("eidx", [P, P])
    iota3 = sb("iota3", [P, 3])
    thr3 = sb("thr3", [P, 3])
    par4 = sb("par4", [P, 4])
    par2 = sb("par2", [P, 2])

    rows_a = sb("rows_a", [96, P])
    rows_b = sb("rows_b", [55, P])
    prm = sb("prm", [P, 96])
    prb = sb("prb", [P, 55])
    cpad = sb("cpad", [P, KT, 32])
    csig = sb("csig", [P, NS, KT])
    mu = sb("mu", [P, 7, RTILES])
    kam = sb("kam", [P, NT])
    hsum = sb("hsum", [P, NT, 8])
    epsr = sb("epsr", [P, 1])
    epsg = sb("epsg", [P, 1])
    moda = sb("moda", [P, 2, KT, NS])
    modb = sb("modb", [P, 4, KT, NS])
    modt = sb("modt", [P, 4, KT, NS])
    hm = sb("hm", [P, 2])
    gcol = sb("gcol", [P, 2, NS, KT])
    grow = rows_a[0:2 * NS * KT, :]

    x = sb("x", [P, NS, D])
    stat = sb("stat", [P, 8])
    hnT = sb("hnT", [P, KT, TT])
    pr = sb("pr", [P, RTILES, TT])
    raw = sb("raw", [P, 4, TT])
    kk = sb("kk", [P, NT, TT])
    qr = sb("qr", [P, 2, NS, NT, 2, T])
    bt = sb("bt", [P, 2, NS, NT, T])
    kt_ = sb("kt_", [P, 2, NS, NT, T])
    vt = sb("vt", [P, NS, RW])
    s0t = sb("s0t", [P, 2 * NT, 2, HS])
    pms = sb("pms", [P, 2 * NT])
    fin = sb("fin", [P, 2, NT])
    gate = sb("gate", [P, NT, TT])
    corr = sb("corr", [P, NT, TT])
    pmT = sb("pmT", [P, 4, TT])

    early = qr[:].rearrange("p d s c k t -> p (d s c k t)")
    em = kt_[:].rearrange("p d s c t -> p (d s c t)")
    btf = bt[:].rearrange("p d s c t -> p (d s c t)")
    w2 = [early[:, 0:512], em[:, 1536:2048]]
    a2 = [early[:, 512:1024], btf[:, 1024:1536]]
    gw2 = early[:, 1024:1536]
    spread = btf[0:8, 1536:2048].rearrange("p (q c) -> p q c", q=NT)
    poolw = early[:, 1536:2048].rearrange("p (g c) -> p g c", g=4)
    w0row = early[:, 2048:3072].rearrange("p (d c) -> p d c", d=2)
    s0raw = early[0:HS, 3072:4096].rearrange("p (d q c) -> p d q c", d=2, q=NT)
    pband = em[:, 0:512].rearrange("p (g t) -> p g t", g=4)
    tri = em[:, 512:1024].rearrange("p (d k t) -> p d k t", d=2, k=2)
    bdm = em[:, 1024:1280].rearrange("p (b t) -> p b t", b=2)
    low = em[:, 1280:1408]
    bones = em[:, 1408:1536]
    rawf = raw[:].rearrange("p c t -> p (c t)")
    so = rawf[:, 0:512].rearrange("p (c k) -> p c k", c=2 * NT)
    zs = rawf[:, 512:1024].rearrange("p (d q h v) -> p d q h v", d=2, q=2, h=2)
    us = pr[:, 8:12, :].rearrange("p c t -> p (c t)").rearrange("p (g q h v) -> p g q h v", g=4, q=2, h=2)
    btm = [w.rearrange("p (d q h t) -> p d q h t", d=2, q=NT, h=2)
           for w in (ring[:, 4, :], hnT[:].rearrange("p k t -> p (k t)"))]
    ktm = ring[:, 5, :].rearrange("p (d q h t) -> p d q h t", d=2, q=NT, h=2)
    hst = corr[0:8, 0, :]
    mrow_a = corr[:].rearrange("p c t -> p (c t)")[:, 0:2 * MW].rearrange("p (g n) -> p g n", g=2)

    sig = ring[:, 8, :].rearrange("p (d s c) -> p d s c", d=2, s=NS)
    aa = ring[:, 9, :].rearrange("p (d c t) -> p d c t", d=2, c=NT)
    kd = ring[:, 10, :].rearrange("p (d c t) -> p d c t", d=2, c=NT)
    mrow_b = bt[:].rearrange("p d s c t -> p (d s c t)")[:, 0:4 * MW].rearrange("p (g n) -> p g n", g=4)
    utok = ring[:, 11, 0:1024].rearrange("p (s c) -> p s c", s=NS)
    pooled = ring[:, 11, 1024:2048].rearrange("p (g t) -> p g t", g=4)
    work = ring[:, 8:12, :].rearrange("p g (k i t) -> p g k i t", k=4, i=4)
    W_M, W_X, W_AT, W_XT = 0, 1, 2, 3


    def kqm(g):
        return ring[:, 8 + g, 0:1024].rearrange("p (i k t) -> p i k t", i=4, k=2)

    xn = ring[:, 8, :].rearrange("p (s c) -> p s c", s=NS)
    junk = ring[:, 9, :].rearrange("p (s c) -> p s c", s=NS)
    bfin = raw[:].rearrange("p c t -> p (c t)").rearrange("p (d q t) -> p d q t", d=2, q=NT)
    bkt = pr[:, 0:8, :].rearrange("p c t -> p (c t)").rearrange("p (j d c) -> p j d c", j=2, d=2)

    area = qr[:].rearrange("p d s c k t -> p (d s c k t)")
    merge = ring[:, 2:4, :].rearrange("p g (m t) -> p (g m) t", m=KT)
    x2t = bt[:].rearrange("p d s c t -> p (d s c t)").rearrange("p (s c) -> p s c", s=NS)
    HA = 5
    zero = raw[:, 3, 0:P]
    XT = (2, 3, 6, 7)
    dgr = raw[:, 0, :].rearrange("p (s t) -> p s t", s=NS)
    rbc = raw[:, 1, :]
    sqp = raw[:, 2, 0:2 * NT].rearrange("p (s c) -> p s c", s=NS)
    ms = kt_[:].rearrange("p d s c t -> p (d s c t)").rearrange("p (m t) -> p m t", m=KT)
    gbc = pr[:, 0:8, :].rearrange("p m t -> p (m t)").rearrange("p (s c) -> p s c", s=NS)
    bgu = area[:, 0:2048]
    bdn = area[:, 2048:3072]
    rtw = sb("rtw", [P, KT, NE])
    rtb = sb("rtb", [NE, 1])
    wbuf = area[:, 3072:4096]
    xg = gate[:].rearrange("p c t -> p (c t)")[:, 0:512].rearrange("p (k s) -> p k s", k=KT)
    gsb = gate[:].rearrange("p c t -> p (c t)")[:, 512:1024]
    sgb = corr[:].rearrange("p c t -> p (c t)")[:, 0:512]
    lcb = corr[:].rearrange("p c t -> p (c t)")[:, 512:1024]
    act_ = pmT[:].rearrange("p c t -> p (c t)")[:, 0:512]
    actT = pmT[:].rearrange("p c t -> p (c t)")[:, 512:1024].rearrange("p (j h s) -> p j h s", j=4, h=2)
    ysb = kk[:].rearrange("p c t -> p (c t)")[:, 0:512]
    pwt = kk[:].rearrange("p c t -> p (c t)")[:, 512:768].rearrange("p (i t) -> p i t", i=NS)
    p2 = vt[:, 0, 0:256].rearrange("p (i s) -> p i s", i=NS)
    pw = vt[:, 0, 256:512].rearrange("p (i s) -> p i s", i=NS)
    sele = vt[:, 1, 0:SLOTS]
    lg = sb("lg", [P, NS, NE])
    top8 = sb("top8", [P, NS, 8])
    idx8 = sb("idx8", [P, NS, 8], U32)
    idxf = sb("idxf", [P, NS, 8])
    tw = sb("tw", [P, NS, 4])
    twn = sb("twn", [P, NS, 4])
    sel = sb("sel", [P, NS, NE])
    comb = sb("comb", [P, NS, NE])
    tick = sb("tick", [P, 1])
    rank = sb("rank", [P, NS, NE])
    lgT = vt[0:NE, 1, SLOTS:SLOTS + TT]
    gf = gate[:].rearrange("p c t -> p (c t)")
    oh4 = gf[:, 512:768].rearrange("p (s j e) -> p s j e", s=NS, j=4)
    cw4 = gf[:, 768:1024].rearrange("p (s j e) -> p s j e", s=NS, j=4)
    cnt = sb("cnt", [NE, 8])
    fl = sb("fl", [NE, 3])
    posc = sb("posc", [NE, 3])
    oh16 = sb("oh16", [NE, 3, EXTRA])
    e16 = sb("e16", [NE, 2, EXTRA])
    item = sb("item", [1, ITEMS + 1], I32)
    base = sb("base", [P, ITEMS])
    fstat = sb("fstat", [P, 4])

    banks = [ctx.enter_context(nc.psum_tensor(f"bank{i}", [P, 512], F32)) for i in range(8)]

    def ring_in(c):
        n = CHUNKS[c][2]
        rt = min(KT, CW // n)
        return ring[:, slot_of(c), 0:rt * n].rearrange("p (k n) -> p k n", k=rt)

    def arrived(eng, c):
        eng.wait_ge(S(f"slot{slot_of(c)}_full"), 16 * USE[c])

    rwv = {n: A[n] for n in ("w_in", "w_mod", "w_pool_out", "w_rwkv_out", "w_o")}

    XB = [(0, 1), (2, 3)]
    PB = [banks[0], banks[5], banks[6], banks[7]]
    ZB = [0, 6, 1, 0]
    CB = [6, 2, 0]

    def unit_bank(u):
        return banks[6 + u % 2 if u >= len(UNITS) - 2 else 5 + 2 * (u % 2)][:, 0:TT]

    FILL = [[("R", 0), ("R", 1), ("X", 0), ("X", 1)], [("R", 2)], [("R", 3), ("X", 2)], [("X", 3), ("M", 0), ("M", 1)],
            [("M", 2)], [("M", m) for m in range(3, 5)], [("M", m) for m in range(5, 7)], [("M", m) for m in range(7, 9)],
            [("M", m) for m in range(9, 14)], [("M", 14)], [("M", 15)]]
    AFTER = {n: i + 1 for names in (
        ("prmT", "xnT", "prbT", "pcnt", "pooled", "mixed", "gate", "norm", "vt", "s0", "inorm", "rk"),
        ("grow", "mean", "var", "istd", "x1T", "rbc", "logits", "lg", "rank", "pos", "list")) for i, n in enumerate(names)}
    IDENT, ZEROS, MASKS, LISTS = 1, 2, 3, 4
    NSTEP = 24
    BKSTEP = (7, 11)
    UNITS = [u for part in FILL for u in part]
    block = ctx.enter_context(nc.Block())

    @block.sync
    def _(sp):
        sp.dma_start(x[:, 0, :], A["x_prompt"][0]).then_inc(S("x_in"), 16)
        sp.dma_start(x[:, 1, :], A["x_sample"][0]).then_inc(S("x_in"), 16)

        def rows(dst, at, ap, n, s):
            sp.dma_start(dst[at:at + n, :], ap).then_inc(S(s), 16)

        def r128(ap):
            return ap.rearrange("(n p) -> n p", p=P)

        rows(rows_a, 0, r128(A["c_ctx"]), 8, "rows_a_in")
        rows(rows_a, 8, r128(A["c"][0]), 8, "rows_a_in")
        rows(rows_a, 16, r128(A["b_mod"][0]), 48, "rows_a_in")
        rows(rows_a, 64, r128(A["norm_mix_w"][0]), 8, "rows_a_in")
        rows(rows_a, 72, r128(A["norm_ffn_w"][0]), 8, "rows_a_in")
        rows(rows_a, 80, r128(A["b_merge"][0]), 16, "rows_a_in")

        def chunk(c):
            name, c0, n, r0 = CHUNKS[c]
            if c >= FRING:
                name_, count = freed(c)
                sp.wait_ge(S(name_), count)
            src = rwv[name][0].rearrange("(k p) n -> p k n", p=P)
            src = src[:, r0:min(r0 + CW // n, src.shape[1]), c0:c0 + n]
            sp.dma_start(ring_in(c), src).then_inc(S(f"slot{slot_of(c)}_full"), 16)

        for c in range(8):
            chunk(c)
        rows(rows_b, 0, r128(A["shift_mu"][0]), 15, "rows_b_in")
        rows(rows_b, 15, r128(A["pool_scale"][0]), 4, "rows_b_in")
        for d in range(2):
            rows(rows_b, 19 + 4 * d, r128(A["iclr_a0"][0, d]), 4, "rows_b_in")
        rows(rows_b, 27, r128(A["k_k"][0]), 4, "rows_b_in")
        rows(rows_b, 31, r128(A["k_a"][0]), 4, "rows_b_in")
        rows(rows_b, 35, A["r_k"][0].rearrange("(n a) c -> n (a c)", a=2), 4, "rows_b_in")
        rows(rows_b, 39, r128(A["ln_x_w"][0]), 4, "rows_b_in")
        rows(rows_b, 43, r128(A["ln_x_b"][0]), 4, "rows_b_in")
        rows(rows_b, 47, r128(A["norm_final_w"]), 8, "rows_b_in")
        for c in range(8, 10):
            chunk(c)
        sp.wait_ge(S("consts_ready"), ZEROS)
        for d in range(2):
            sp.dma_start(w2[d][d * HS:(d + 1) * HS, :], A["decay_w2"][0, d]).then_inc(S("lora_in"), 16)
            sp.dma_start(a2[d][d * HS:(d + 1) * HS, :], A["iclr_a2"][0, d]).then_inc(S("lora_in"), 16)
        sp.dma_start(gw2, A["gate_w2"][0]).then_inc(S("lora_in"), 16)
        sp.dma_start(w0row, A["decay_w0"].to_broadcast([P, 2, RW])).then_inc(S("lora_in"), 16)
        sp.dma_start(poolw, A["pool_w"][0].rearrange("g c d -> c g d")).then_inc(S("lora_in"), 16)
        for d, n in enumerate(("state_fwd", "state_bwd")):
            for q in range(NT):
                sp.dma_start(s0raw[:, d, q, :].rearrange("v (h k) -> v h k", h=2),
                             A[n][0, 0, 2 * q:2 * q + 2].rearrange("h v k -> v h k")).then_inc(S("state_in"), 16)
        sp.dma_start(rtw[:], A["router_w"][0].rearrange("(k p) e -> p k e", p=P)).then_inc(S("router_in"), 16)
        sp.dma_start(rtb[:], A["router_b"].rearrange("o e -> e o")).then_inc(S("router_in"), 16)
        for c in range(10, C_WO + 2):
            chunk(c)

        def expert_chunk(e, j):
            if j < GU_CHUNKS:
                src, dst = A["expert_w_gu"][0][bass.ds(e, 1), j * P:(j + 1) * P, :], ring[:, j, :]
                src = src.rearrange("o p n -> (o p) n")
            else:
                r = 2 * P * (j - GU_CHUNKS)
                src = A["expert_w_down"][0][bass.ds(e, 1), r:r + 2 * P, :].rearrange("o (i p) n -> p (o i) n", i=2)
                dst = ring[:, j, :].rearrange("p (i n) -> p i n", i=2)
            sp.dma_start(dst, src).then_inc(S(f"slot{j}_full"), 16)

        sp.wait_ge(S("y_mm"), 4)
        for j in range(FRING, RING):
            expert_chunk(0, j)
        for c in range(C_WO + 2, NF):
            chunk(c)
        for c in range(NF - FRING, NF):
            name, count = released(c)
            sp.wait_ge(S(name), count)
            expert_chunk(0, slot_of(c))
        sp.wait_ge(S("items_ready"), 1)
        n_items = sp.value_load(item[0:1, ITEMS:ITEMS + 1], min_val=NE, max_val=NE + EXTRA)
        with sp.Fori(1, n_items) as it:
            e = sp.value_load(item[0:1, bass.ds(it, 1)], min_val=0, max_val=NE - 1)
            for j in range(RING):
                sp.wait_ge(S("chunk_used"), it * RING + (j + 1 - RING))
                expert_chunk(e, j)
        sp.wait_ge(S("stored"), 96)

    @block.gpsimd
    def _(pool):
        g = nc.gpsimd
        n = [0]

        def step(ins):
            n[0] += 1
            ins.then_inc(S("pool_step"), 1)
            pool.wait_ge(S("pool_step"), n[0])

        def signal(ins, name, count):
            ins.then_inc(S(name), 1)
            pool.wait_ge(S(name), count)

        def keep(dst, src, pattern, op, fill, b=0, cm=1):
            step(g.affine_select(out=dst, in_=src, compare_op=op, fill=fill, base=b, pattern=pattern,
                                 channel_multiplier=cm))

        def build_spread(n):
            step(g.memset(spread, 0.0))
            signal(g.affine_select(out=spread.rearrange("p q (h c) -> p q h c", h=2), in_=spread.rearrange("p q (h c) -> p q h c", h=2),
                                   compare_op=ALU.not_equal, fill=1.0, base=0, pattern=[[-2, NT], [-1, 2], [0, HS]],
                                   channel_multiplier=1), "spread_ready", n)

        step(g.memset(ident[:], 0.0))
        step(g.memset(ones[:], 1.0))
        keep(ident[:], ident[:], [[-1, P]], ALU.not_equal, 1.0)
        step(g.memset(epsr[:], RMS_EPS))
        step(g.memset(epsg[:], GN_EPS))
        step(g.memset(cpad[:], 0.0))
        signal(g.memset(rowlo[:], 0.0), "consts_ready", IDENT)
        for d in range(2):
            o = slice((1 - d) * HS, (2 - d) * HS)
            step(g.memset(w2[d][o, :], 0.0))
            if d == 0:
                step(g.memset(a2[d][o, :], 0.0))
        signal(g.memset(a2[1][0:HS, :], 0.0), "consts_ready", ZEROS)
        keep(low, ones[:], [[-1, P]], ALU.is_gt, 0.0)
        keep(upp[:], ones[:], [[1, P]], ALU.is_gt, 0.0, cm=-1)
        keep(mqr[:, 0, 0, :], ones[:], [[1, P]], ALU.is_gt, 0.0, cm=-1)
        keep(mqr[:, 0, 1, :], ones[:], [[1, P]], ALU.is_ge, 0.0, cm=-1)
        keep(mqr[:, 1, 0, :], ones[:], [[-1, P]], ALU.is_gt, 0.0)
        keep(mqr[:, 1, 1, :], ones[:], [[-1, P]], ALU.is_ge, 0.0)
        step(g.memset(rowlo[0:HS, :], 1.0))
        step(g.memset(hm[:], 0.0))
        step(g.memset(s0t[:], 0.0))
        step(g.memset(hsum[:], 0.0))
        for h in range(2):
            r = slice(h * HS, (h + 1) * HS)
            step(g.memset(hm[r, h:h + 1], 1.0))
            for q in range(NT):
                step(g.memset(hsum[r, q, 2 * q + h:2 * q + h + 1], 1.0))
        step(g.memset(bones, 0.0))
        step(g.memset(bmean[:], 0.0))
        for h in range(2):
            step(g.memset(bones[h * HS:(h + 1) * HS, h * HS:(h + 1) * HS], 1.0))
            step(g.memset(bmean[h * HS:(h + 1) * HS, h * HS:(h + 1) * HS], 1.0 / HS))
        for i, w in enumerate(WINDOWS):
            keep(pband[:, i, :], ones[:], [[-1, P]], ALU.is_ge, 0.0, b=w // 2)
            keep(pband[:, i, :], pband[:, i, :], [[1, P]], ALU.is_gt, 0.0, b=w // 2, cm=-1)
        signal(g.memset(base[:], 0.0), "consts_ready", MASKS)
        build_spread(1)
        for i in range(1, 7):
            m = 2 ** i
            if i >= 3:
                pool.wait_ge(S("bd_used"), i - 1)
            b = bdm[:, i % 2, :]
            bv = b.rearrange("p (n m) -> p n m", m=m)
            keep(bv, ones[:].rearrange("p (n m) -> p n m", m=m), [[-m, P // m], [0, m]], ALU.is_ge, 0.0)
            signal(g.affine_select(out=bv, in_=bv, compare_op=ALU.is_gt, fill=0.0, base=m,
                                   pattern=[[m, P // m], [0, m]], channel_multiplier=-1), "bd_ready", i)
        step(g.iota(iotai[:], [[0, 2], [1, SLOTS]], base=0, channel_multiplier=0))
        step(g.tensor_copy(iota2[:], iotai[:]))
        step(g.iota(iotai[:], [[0, P]], base=0, channel_multiplier=1))
        step(g.tensor_copy(eidx[:], iotai[:]))
        step(g.tensor_copy(iota3[:], iota2[:, 0:3]))
        step(g.iota(item[:, 0:NE], [[1, NE]], base=0, channel_multiplier=0))
        step(g.memset(item[:, NE:ITEMS + 1], 0))
        signal(g.tensor_scalar(thr3[:], iota2[:, 0:3], float(SLOTS), float(SLOTS), ALU.mult, ALU.add), "consts_ready", LISTS)

        pool.wait_ge(S("grow_ready"), 1)
        pool.dma_start(scratch.rearrange("g s (k p) -> (g s k) p", p=P), grow).then_inc(S("gates_out"), 16)
        pool.wait_ge(S("gates_out"), 16)
        for s in range(NS):
            for gr in range(4):
                n_ = 4 * s + gr
                pool.wait_ge(S("ma_ready"), n_ + 1)
                idb = ident[:].unsqueeze(1).to_broadcast([P, 4, P])
                signal(g.tensor_tensor(work[:, gr, W_X, :, :], idb, work[:, gr, W_M, :, :], ALU.subtract), "xa_ready", n_ + 1)
            if s == 1:
                pool.wait_ge(S("btm_ready"), 2)
                pool.wait_ge(S("bf_ready"), 2)
                build_spread(2)
        pool.wait_ge(S("y_mm"), 4)
        for gi in range(2):
            if gi:
                pool.wait_ge(S("wo_used"), 8)
            for s in range(NS):
                pool.dma_start(gbc[:, s, :], scratch[gi, s:s + 1, :].to_broadcast([P, D])).then_inc(S("gbc_in"), 16)
            if gi == 0:
                step(g.memset(area[NE:2 * NE, 0:3072], 0.0))
                step(g.memset(area[2 * NE:P, 0:3072], 0.0))
                pool.wait_ge(S("yn_ready"), 1)
                signal(g.memset(zero, 0.0), "zero_ready", 1)
                pool.dma_start(bgu[0:NE, :], A["expert_b_gu"][0]).then_inc(S("bgu_in"), 16)
                pool.dma_start(bdn[0:NE, :], A["expert_b_down"][0]).then_inc(S("bdn_in"), 16)
                pool.dma_start(wbuf, A["norm_final_w"].rearrange("(a n) -> a n", a=1).to_broadcast([P, D])).then_inc(S("wfin_in"), 16)

    @block.tensor
    def _(pe):
        mm = nc.tensor.matmul
        tr = nc.tensor.transpose

        pe.wait_ge(S("consts_ready"), IDENT)
        pe.wait_ge(S("rows_a_in"), 96)
        tr(banks[0][:, 0:96], rows_a[:], ident[0:96, 0:96]).then_inc(S("front_mm"), 1)
        for s in range(NS):
            pe.wait_ge(S("xn_ready"), s + 1)
            for k in range(KT):
                b = banks[1 + k // 2]
                last = tr(b[:, (k % 2) * TT + s * T:(k % 2) * TT + (s + 1) * T], xn[:, s, k * P:(k + 1) * P], ident[:])
        last.then_inc(S("front_mm"), 1)

        def mod_rows(c0, out, done):
            for r in range(MC):
                arrived(pe, c0 + r)
                w = ring_in(c0 + r)
                for k in range(2):
                    for j in range(MG):
                        last = mm(out[32 * j:32 * (j + 1), :], cpad[:, 2 * r + k, :], w[:, k, j * MW:(j + 1) * MW],
                                  start=(r + k == 0), stop=(r == MC - 1 and k == 1))
                last.then_inc(S(done), 1)

        def mod_turn(rows, out, done):
            for h in range(2):
                last = tr(out[:, h * P:(h + 1) * P], rows[:, h * P:(h + 1) * P], ident[:])
            last.then_inc(S(done), 1)

        pe.wait_ge(S("cpad_ready"), 1)
        for g in range(2):
            mod_rows(C_MODA + MC * g, unit_bank(g), "moda_mm")
        for g in range(2):
            pe.wait_ge(S("mrow_ready"), g + 1)
            mod_turn(mrow_a[:, g, :], banks[6][:, g * MW:(g + 1) * MW], "modat_mm")
        pe.wait_ge(S("rows_b_in"), 160)
        tr(banks[0][:, 128:183], rows_b[:], ident[0:55, 0:55]).then_inc(S("front_mm"), 1)

        fills = [0]

        def fill(part):
            for kind, i in FILL[part]:
                u = fills[0]
                if u >= 2:
                    pe.wait_ge(S("fill_used"), u - 1)
                if kind == "R":
                    mod_rows(C_MODB + MC * i, unit_bank(u), "modb_mm")
                elif kind == "X":
                    pe.wait_ge(S("fill_used"), UNITS.index(("R", i)) + 1)
                    mod_turn(mrow_b[:, i, :], unit_bank(u), "modbt_mm")
                else:
                    c = C_MERGE + i // 2
                    arrived(pe, c)
                    for k in range(KT):
                        last = mm(unit_bank(u), ring_in(c)[:, k, (i % 2) * P:(i % 2 + 1) * P], hnT[:, k, :],
                                  start=(k == 0), stop=(k == KT - 1))
                    last.then_inc(S("merge_mm"), 1)
                fills[0] += 1

        pe.wait_ge(S("consts_ready"), MASKS)
        for _ in range(2):
            mm(banks[5][:, :], ones[:], mqr[:].rearrange("p d k t -> p (d k t)"), start=True, stop=True)

        pe.wait_ge(S("prb_ready"), 1)
        for ct in range(RTILES):
            c = C_RWKV + ct // 2
            arrived(pe, c)
            w = ring_in(c)
            if ct >= 4:
                pe.wait_ge(S("raw_copied"), ct - 3)
            o = (ct % 2) * P if ct < RTILES - 1 else 0
            for i in range(KT):
                k = (i % 2) * 4 + i // 2
                if ct == 0:
                    pe.wait_ge(S(("hna_ready", "hnd_ready")[i % 2]), i // 2 + 1)
                last = mm(PB[ct % 4][:, 0:TT], w[:, k, o:o + P], hnT[:, k, :], start=(i == 0), stop=(i == KT - 1))
            last.then_inc(S("proj_done"), 1)

        for c in range(2):
            arrived(pe, C_POOL + c)
            w = ring_in(C_POOL + c)
            for s in range(NS):
                for k in range(KT):
                    last = mm(banks[2 + s][:, 256 * c:256 * c + 256], hnT[:, k, s * T:(s + 1) * T], w[:, k, :],
                              start=(k == 0), stop=(k == KT - 1))
            last.then_inc(S("pu_mm"), 1)

        pe.wait_ge(S("consts_ready"), MASKS)
        mm(banks[4][:, :], ones[:], pband.rearrange("p g t -> p (g t)"), start=True, stop=True).then_inc(S("front_mm"), 1)

        pe.wait_ge(S("raw_copied"), RTILES)
        fill(0)
        pe.wait_ge(S("lora_in"), 112)
        pe.wait_ge(S("th_ready"), 1)
        for d in range(2):
            for s in range(NS):
                b = banks[ZB[2 * d + s]]
                if 2 * d + s == 3:
                    pe.wait_ge(S("zb_ready"), 1)
                mm(b[:, :], pr[:, 12, s * T:(s + 1) * T], w2[d], start=True, stop=True).then_inc(S("z_done"), 1)
        fill(1)
        pe.wait_ge(S("utok_ready"), 2)
        pe.wait_ge(S("pband_ready"), 1)
        for gi in range(4):
            for s in range(NS):
                last = mm(banks[2 + gi // 2][:, (gi % 2) * TT + s * T:(gi % 2) * TT + (s + 1) * T],
                          utok[:, s, gi * P:(gi + 1) * P], pband[:, gi, :], start=True, stop=True)
        last.then_inc(S("front_mm"), 1)
        pe.wait_ge(S("sig_ready"), 4)
        for d in range(2):
            for q in range(NT):
                if d == 1 and q == 2:
                    pe.wait_ge(S("a_ready"), 1)
                last = mm(banks[ZB[2 * d + q // 2]][:, (q % 2) * TT:(q % 2 + 1) * TT], a2[d][:, q * P:(q + 1) * P],
                          pr[:, 13, :], start=True, stop=True)
                if q % 2:
                    last.then_inc(S("a_done"), 1)
        fill(2)
        pe.wait_ge(S("pooled_ready"), 2)
        pe.wait_ge(S("pband_ready"), 1)
        MB = [banks[4], banks[2]]
        for gi in range(4):
            last = mm(MB[gi // 2][:, (gi % 2) * TT:(gi % 2 + 1) * TT], poolw[:, gi, :], pooled[:, gi, :], start=True, stop=True)
        last.then_inc(S("front_mm"), 1)
        pe.wait_ge(S("a_ready"), 4)
        for q in range(NT):
            last = mm(banks[(3, 0)[q // 2]][:, (q % 2) * TT:(q % 2 + 1) * TT], gw2[:, q * P:(q + 1) * P], pr[:, 14, :], start=True, stop=True)
        last.then_inc(S("front_mm"), 1)
        fill(3)
        pe.wait_ge(S("a_ready"), 4)
        pe.wait_ge(S("ksq_ready"), 1)
        for q in range(NT):
            last = mm(banks[6][0:8, 0:TT], hsum[:, q, :], raw[:, q, :], start=(q == 0), stop=(q == NT - 1))
        last.then_inc(S("front_mm"), 1)
        pe.wait_ge(S("mixed_ready"), 2)
        pe.wait_ge(S("gate_ready"), 2)
        for s in range(NS):
            for q in range(NT):
                last = tr(banks[(2, 0)[s]][:, q * P:(q + 1) * P], pr[:, 8 + q, s * T:(s + 1) * T], ident[:])
        last.then_inc(S("front_mm"), 1)
        pe.wait_ge(S("state_in"), 128)
        for d in range(2):
            for q in range(NT):
                i = d * NT + q
                last = tr(banks[4][:, i * HS:(i + 1) * HS], s0raw[:, d, q, :], ident[0:HS, 0:HS])
        last.then_inc(S("front_mm"), 1)
        fill(4)
        pe.wait_ge(S("spread_ready"), 1)
        pe.wait_ge(S("inorm_ready"), 1)
        for q in range(NT):
            last = mm(banks[(6, 1)[q // 2]][:, (q % 2) * TT:(q % 2 + 1) * TT], spread[:, q, :], hst, start=True, stop=True)
        last.then_inc(S("front_mm"), 1)
        fill(5)
        pe.wait_ge(S("kk_ready"), 1)
        pe.wait_ge(S("gate_ready"), 2)
        pe.wait_ge(S("rkk_ready"), 1)
        for q in range(NT):
            last = mm(banks[(3, 1)[q // 2]][:, (q % 2) * TT:(q % 2 + 1) * TT], bones, raw[:, q, :], start=True, stop=True)
        last.then_inc(S("front_mm"), 1)
        fill(6)
        pe.wait_ge(S("tri_ready"), 1)
        pe.wait_ge(S("kk_ready"), 1)
        pe.wait_ge(S("vt_ready"), 2)
        for i in range(8):
            d, s, t2 = i // 4, (i // 2) % 2, i % 2
            if i >= 3:
                pe.wait_ge(S("cum_used"), i - 2)
            for q in range(2):
                last = mm(banks[CB[i % 3]][:, q * 256:(q + 1) * 256], sig[:, d, s, (2 * t2 + q) * P:(2 * t2 + q + 1) * P],
                          tri[:, d, :, :].rearrange("p k t -> p (k t)"), start=True, stop=True)
            last.then_inc(S("cum_done"), 1)

        fill(7)
        fill(8)
        def states_turn(j):
            for d in range(2):
                pe.wait_ge(S("bf_ready"), 2 * j + d + 1)
                if j:
                    pe.wait_ge(S("bk_ready"), d + 1)
                else:
                    pe.wait_ge(S("fill_used"), len(UNITS))
                for q in range(NT):
                    last = tr(banks[6 + d][:, q * P:(q + 1) * P], bfin[:, d, q, :], ident[:])
                last.then_inc(S("bk_done"), 1)

        pe.wait_ge(S("gcol_ready"), 1)
        pe.wait_ge(S("cum_used"), 8)
        tr(banks[6][0:32, 0:P], gcol[:].rearrange("p g s k -> p (g s k)"), ident[:]).then_inc(S("late_mm"), 1)

        for s in range(NS):
            pe.wait_ge(S("btm_ready"), s + 1)
            pe.wait_ge(S("fill_used"), len(UNITS) - 2 * (1 - s))
            def a(g):
                d, tp = g // 2, g % 2
                if g >= 2:
                    pe.wait_ge(S("a_evac"), 4 * s + g - 1)
                elif g == 1 and s == 1:
                    pe.wait_ge(S("state_copied"), 1)
                ba, bat = banks[2 * (g % 2)], banks[2 * (g % 2) + 1]
                for i in range(4):
                    h, q = i // 2, 2 * tp + i % 2
                    mm(ba[:, i * T:(i + 1) * T], qr[:, d, s, q, 0, :], btm[s][:, d, q, h, :], start=True, stop=True)
                for i in range(4):
                    h, q = i // 2, 2 * tp + i % 2
                    last = mm(bat[:, i * T:(i + 1) * T], btm[s][:, d, q, h, :], qr[:, d, s, q, 0, :], start=True, stop=True)
                last.then_inc(S("a_mm"), 1)

            def m(k):
                g, n = k % 4, NSTEP * s + k
                if k == 1 and s == 1:
                    pe.wait_ge(S("y_evac"), 2)
                if k < 4:
                    pe.wait_ge(S("a_evac"), 4 * s + g + 1)
                    pe.wait_ge(S("xa_ready"), 4 * s + g + 1)
                else:
                    pe.wait_ge(S("x_upd"), n - 4 + 1)
                if n >= 2:
                    pe.wait_ge(S("m_evac"), n - 1)
                for i in range(4):
                    last = mm(banks[4 + k % 2][:, i * T:(i + 1) * T], work[:, g, W_AT, i, :], work[:, g, W_X, i, :], start=True, stop=True)
                last.then_inc(S("m_mm"), 1)

            def x_(k):
                g, n = k % 4, NSTEP * s + k
                pe.wait_ge(S("m_evac"), n + 1)
                if k < 2:
                    pe.wait_ge(S("a_evac"), 4 * s + k + 3)
                else:
                    pe.wait_ge(S("x_upd"), n - 2 + 1)
                bx, bxt = XB[k % 2]
                for i in range(4):
                    if k < NSTEP - 4:
                        mm(banks[bx][:, i * T:(i + 1) * T], work[:, g, W_XT, i, :], work[:, g, W_M, i, :], start=True, stop=True)
                    last = mm(banks[bxt][:, i * T:(i + 1) * T], work[:, g, W_M, i, :], work[:, g, W_XT, i, :], start=True, stop=True)
                last.then_inc(S("x_mm"), 1)

            for unit, k in ((a, 0), (a, 1), (fill, 9), (a, 2), (m, 0), (fill, 10), (a, 3), (x_, 0), (m, 1), (m, 2)):
                if unit != fill:
                    unit(k)
                elif s == 0:
                    pe.wait_ge(S("grow_ready"), 1)
                    fill(k)
            for k in range(1, NSTEP):
                x_(k)
                if k + 2 < NSTEP:
                    m(k + 2)
                if s == 0 and k in BKSTEP:
                    states_turn(BKSTEP.index(k))
            def kq(j):
                tp, d = j // 2, j % 2
                n = 4 * s + j
                if j >= 2:
                    pe.wait_ge(S("kq_evac"), n - 1)
                elif j == 0:
                    pe.wait_ge(S("x_upd"), NSTEP * (s + 1))
                    pe.wait_ge(S("ktm_ready"), s + 1)
                for i in range(4):
                    h, q = i // 2, 2 * tp + i % 2
                    mm(banks[6 + j % 2][:, i * T:(i + 1) * T], btm[s][:, d, q, h, :], qr[:, d, s, q, 1, :], start=True, stop=True)
                for i in range(4):
                    h, q = i // 2, 2 * tp + i % 2
                    last = mm(banks[2 * (j % 2) + i // 2][:, (i % 2) * 256:(i % 2 + 1) * 256], ktm[:, d, q, h, :],
                              qr[:, d, s, q, :, :].rearrange("p k t -> p (k t)"), start=True, stop=True)
                last.then_inc(S("kq_mm"), 1)

            def z(j):
                tp, d = j // 2, j % 2
                g, n = 2 * d + tp, 4 * s + j
                pe.wait_ge(S("kq_evac"), n + 1)
                if n:
                    pe.wait_ge(S("z_evac"), n)
                for i in range(4):
                    q = 2 * tp + i % 2
                    o = banks[4][:, i * T:(i + 1) * T]
                    last = mm(o, kqm(g)[:, i, 0, :], vt[:, s, q * P:(q + 1) * P], start=True, stop=(s == 0))
                    if s == 1:
                        last = mm(o, qr[:, d, s, q, 0, :], s0t[:, d * NT + q, :, :].rearrange("p h v -> p (h v)"), start=False, stop=True)
                last.then_inc(S("z_mm"), 1)

            def u(j):
                tp, d = j // 2, j % 2
                g, n = 2 * d + tp, 4 * s + j
                pe.wait_ge(S("z_evac"), n + 1)
                if n:
                    pe.wait_ge(S("u_evac"), n)
                if n and d == 0:
                    pe.wait_ge(S("y_evac"), n // 2)
                for i in range(4):
                    last = mm(banks[5][:, i * T:(i + 1) * T], work[:, g, W_XT, i, :], zs[:, d, i % 2, :, :].rearrange("p h v -> p (h v)"),
                              start=True, stop=True)
                last.then_inc(S("u_mm"), 1)

            def y(tp):
                pe.wait_ge(S("u_evac"), 4 * s + 2 * tp + 2)
                for qi in range(2):
                    q = 2 * tp + qi
                    for d in range(2):
                        g = 2 * d + tp
                        for h in range(2):
                            i = 2 * h + qi
                            o = banks[5][h * HS:(h + 1) * HS, qi * T:(qi + 1) * T]
                            mm(o, vt[:, s, q * P + h * HS:q * P + (h + 1) * HS], kqm(g)[:, i, 1, :], start=(d == 0), stop=False)
                            last = mm(o, us[:, g, qi, h, :], work[:, g, W_AT, i, :], start=False, stop=(d == 1))
                    if s == 1:
                        for d in range(2):
                            last = mm(banks[5][:, qi * T:(qi + 1) * T], s0t[:, d * NT + q, :, :].rearrange("p h v -> p (h v)"),
                                      qr[:, d, s, q, 1, :], start=False, stop=True, skip_group_check=True)
                last.then_inc(S("y_mm"), 1)

            for unit, j in ((kq, 0), (kq, 1), (z, 0), (kq, 2), (u, 0), (z, 1), (kq, 3), (u, 1), (z, 2), (y, 0),
                            (z, 3), (u, 2), (u, 3), (y, 1)):
                unit(j)
            if s == 0:
                for d in range(2):
                    for q in range(NT):
                        o = banks[2 + d][:, q * P:(q + 1) * P]
                        mm(o, us[:, 2 * d + q // 2, q % 2, :, :].rearrange("p h v -> p (h v)"), bkt[:, 0, d, q * P:(q + 1) * P],
                           start=True, stop=False)
                        last = mm(o, vt[:, s, q * P:(q + 1) * P], bkt[:, 1, d, q * P:(q + 1) * P], start=False, stop=True)
                last.then_inc(S("state_mm"), 1)
        pe.wait_ge(S("y_evac"), 4)
        for q in range(NT):
            last = mm(banks[(4, 6)[q // 2]][:, (q % 2) * TT:(q % 2 + 1) * TT], bmean[:], kk[:, q, :], start=True, stop=True)
        last.then_inc(S("late_mm"), 1)
        def branch(c0, src, done, tiles):
            for m in tiles:
                c = c0 + m // 4
                arrived(pe, c)
                if c0 == C_ROUT and m < 4:
                    pe.wait_ge(S("pout_used"), m + 5)
                elif m >= 4:
                    pe.wait_ge(S("rout_used" if c0 == C_ROUT else "pout_used"), m - 3)
                for k in range(4):
                    last = mm(banks[m % 4][:, 0:TT], ring_in(c)[:, k, (m % 4) * P:(m % 4 + 1) * P], src[:, k, :],
                              start=(k == 0), stop=(k == 3))
                last.then_inc(S(done), 1)

        branch(C_POUT, pmT, "pout_mm", range(2))
        pe.wait_ge(S("ysq_ready"), 1)
        for q in range(NT):
            last = mm(banks[5][0:8, 0:TT], hsum[:, q, :], raw[:, q, :], start=(q == 0), stop=(q == NT - 1))
        last.then_inc(S("late_mm"), 1)
        branch(C_POUT, pmT, "pout_mm", range(2, 4))
        pe.wait_ge(S("spread_ready"), 2)
        pe.wait_ge(S("istd_ready"), 1)
        for q in range(NT):
            last = mm(banks[(4, 6)[q // 2]][:, (q % 2) * TT:(q % 2 + 1) * TT], spread[:, q, :], hst, start=True, stop=True)
        last.then_inc(S("late_mm"), 1)
        branch(C_POUT, pmT, "pout_mm", range(4, KT))
        pe.wait_ge(S("yn_ready"), 1)
        branch(C_ROUT, kk, "rout_mm", range(KT))

        def x1_turn(c):
            for s in range(NS):
                pe.wait_ge(S("wo_used"), 2 * c + s + 1)
                for k in (2 * c, 2 * c + 1):
                    last = tr(banks[XT[c]][:, (k % 2) * TT + s * T:(k % 2) * TT + (s + 1) * T], x[:, s, k * P:(k + 1) * P], ident[:])
            return last

        pe.wait_ge(S("rout_used"), KT)
        for c in range(4):
            arrived(pe, C_WO + c)
            for s in range(NS):
                n = 2 * c + s
                if n >= 4:
                    pe.wait_ge(S("wo_used"), n - 3)
                for k in range(KT):
                    last = mm(banks[(0, 1, 5, 4)[n % 4]][:, 0:256], ms[:, k, s * T:(s + 1) * T], ring_in(C_WO + c)[:, k, :],
                              start=(k == 0), stop=(k == KT - 1))
                last.then_inc(S("wo_mm"), 1)
            if c:
                x1_turn(c - 1)
        x1_turn(3).then_inc(S("late_mm"), 1)
        for _ in range(2):
            mm(banks[5][:, :], ones[:], mqr[:].rearrange("p d k t -> p (d k t)"), start=True, stop=True)
        pe.wait_ge(S("dgr_ready"), 1)
        mm(banks[0][:, 0:TT], ones[:], dgr.rearrange("p s t -> p (s t)"), start=True, stop=True).then_inc(S("late_mm"), 1)
        for _ in range(2):
            mm(banks[5][:, :], ones[:], mqr[:].rearrange("p d k t -> p (d k t)"), start=True, stop=True)
        pe.wait_ge(S("router_in"), 32)
        def logits(k):
            if k < HA:
                pe.wait_ge(S("hn2a_ready"), k + 1)
            else:
                pe.wait_ge(S("hn2d_ready"), k - HA + 1)
            last = mm(banks[5][0:NE, 0:TT], rtw[:, k, :], hnT[:, k, :], start=(k == 0), stop=(k == KT - 1))
            if k == KT - 1:
                last.then_inc(S("late_mm"), 1)

        def x2_turn(k):
            for s in range(NS):
                last = tr(banks[2 * s + k // 4][:, (k % 4) * P:(k % 4 + 1) * P], hnT[:, k, s * T:(s + 1) * T], ident[:])
            if k == KT - 1:
                last.then_inc(S("x2_mm"), 1)

        def lg_turn(_):
            pe.wait_ge(S("lgT_ready"), 1)
            for s in range(NS):
                last = tr(banks[6][:, 256 + s * NE:256 + (s + 1) * NE], lgT[:, s * T:(s + 1) * T], ident[0:NE, 0:NE])
            last.then_inc(S("late_mm"), 1)

        for unit, k in ((logits, 0), (x2_turn, 0), (logits, 1), (x2_turn, 1), (logits, 2), (x2_turn, 2), (logits, 3), (logits, 4),
                        (logits, 5), (logits, 6), (logits, 7), (x2_turn, 3), (x2_turn, 4), (lg_turn, 0), (x2_turn, 5),
                        (x2_turn, 6), (x2_turn, 7)):
            unit(k)

        def zero_sums(j):
            pe.wait_ge(S("x2_ready"), j + 1)
            mm(banks[j][:, :], zero, mqr[:].rearrange("p d k t -> p (d k t)"), start=True, stop=True)

        pe.wait_ge(S("zero_ready"), 1)
        zero_sums(0)
        pe.wait_ge(S("sel_done"), 1)
        mm(banks[6][:, 0:2 * NE], upp[:], sel[:].rearrange("p s e -> p (s e)"), start=True, stop=True)
        mm(banks[6][:, NE:2 * NE], ones[:], sel[:, 0, :], start=False, stop=True, skip_group_check=True)
        for s in range(NS):
            last = mm(banks[4][0:NE, 64:65], sel[:, s, :], ones[:, 0:1], start=(s == 0), stop=(s == 1))
        last.then_inc(S("late_mm"), 1)

        def gather():
            for k in range(KT):
                for s in range(NS):
                    last = mm(banks[6][:, k * SLOTS:(k + 1) * SLOTS], x2t[:, s, k * P:(k + 1) * P], p2[:, s, 0:SLOTS],
                              start=(s == 0), stop=(s == NS - 1))
            last.then_inc(S("gathered"), 1)

        for j in (1, 2):
            zero_sums(j)
        pe.wait_ge(S("extra_ready"), 1)
        mm(banks[4][0:NE, 65:66], upp[0:NE, 0:NE], cnt[:, 1:2], start=True, stop=True)
        mm(banks[4][:, 66:67], ones[0:NE, :], cnt[:, 1:2], start=True, stop=True).then_inc(S("late_mm"), 1)
        pe.wait_ge(S("x2_ready"), 4)
        pe.wait_ge(S("sel_ready"), 1)
        for k in range(KT):
            for s in range(NS):
                last = mm(banks[6 + k // 4][:, (k % 4) * P:(k % 4 + 1) * P], x2t[:, s, k * P:(k + 1) * P], p2[:, s, :],
                          start=(s == 0), stop=(s == NS - 1))
        last.then_inc(S("gathered"), 1)
        pe.wait_ge(S("e16_ready"), 1)
        mm(banks[4][:, 96:96 + EXTRA], eidx[0:NE, :], e16[:, 0, :], start=True, stop=True)
        mm(banks[4][:, 128:128 + EXTRA], ones[0:NE, :], e16[:, 1, :], start=True, stop=True).then_inc(S("late_mm"), 1)
        zero_sums(3)
        G, L = banks[4], banks[5]

        def up_bias(b, o, start):
            for h in range(2):
                mm(b[h * SLOTS:(h + 1) * SLOTS, :], sele, bgu[:, o + h * 512:o + (h + 1) * 512], start=start, stop=False)

        pe.wait_ge(S("bgu_in"), 16)
        pe.wait_ge(S("bdn_in"), 16)
        pe.wait_ge(S("sele_ready"), 1)
        up_bias(L, FF, True)
        pe.wait_ge(S("items_ready"), 1)
        n_items = pe.value_load(item[0:1, ITEMS:ITEMS + 1], min_val=NE, max_val=NE + EXTRA)
        with pe.Fori(0, n_items) as it:
            pe.wait_ge(S("xg_ready"), it + 1)
            for j in range(GU_CHUNKS):
                pe.wait_ge(S(f"slot{j}_full"), it * 16 + 16 * (FRONT_USES[j] + 1))
                for b, o in ((G, 0), (L, FF)):
                    for h in range(2):
                        last = mm(b[h * SLOTS:(h + 1) * SLOTS, :], xg[:, j, :], ring[:, j, o + h * 512:o + (h + 1) * 512],
                                  start=(j == 0 and b is G), stop=(j == GU_CHUNKS - 1))
                last.then_inc(S("chunk_used"), 1)
                if j == 1:
                    up_bias(G, 0, False)
            pe.wait_ge(S("sel_ready"), it + 2)
            gather()
            pe.wait_ge(S("act_ready"), it + 1)
            for j in range(4):
                last = tr(L[:, j * P:(j + 1) * P], act_[:, j * P:(j + 1) * P], ident[:])
            last.then_inc(S("actT_done"), 1)
            pe.wait_ge(S("pw_ready"), it + 1)
            for s in range(NS):
                last = tr(banks[7][:, s * T:(s + 1) * T], pw[:, s, :], ident[:])
            last.then_inc(S("pwt_done"), 1)
            pe.wait_ge(S("actT_ready"), it + 1)
            for j in range(DN_CHUNKS):
                pe.wait_ge(S(f"slot{GU_CHUNKS + j}_full"), it * 16 + 16 * (FRONT_USES[GU_CHUNKS + j] + 1))
                for i in range(2):
                    c = 2 * j + i
                    for h in range(2):
                        last = mm(G[h * SLOTS:(h + 1) * SLOTS, :], actT[:, c % 4, c // 4, :],
                                  ring[:, GU_CHUNKS + j, i * D + h * 512:i * D + (h + 1) * 512],
                                  start=(c == 0), stop=(c == 7))
                last.then_inc(S("chunk_used"), 1)
                if j == 0:
                    for h in range(2):
                        mm(G[h * SLOTS:(h + 1) * SLOTS, :], sele, bdn[:, h * 512:(h + 1) * 512], start=False, stop=False)
            pe.wait_ge(S("sele_ready"), it + 2)
            up_bias(L, FF, True)
            pe.wait_ge(S("pwt_ready"), it + 1)
            pe.wait_ge(S("ysb_ready"), it + 1)
            for s in range(NS):
                for h in range(2):
                    r = slice(h * SLOTS, (h + 1) * SLOTS)
                    last = mm(banks[2 * s + h][:, :], pwt[r, s, :], ysb[r, :], start=False, stop=True, skip_group_check=True)
                last.then_inc(S(("scattered_ctx", "scattered_lat")[s]), 1)

    @block.scalar
    def _(act):
        af = nc.scalar.activation

        act.wait_ge(S("x_in"), 32)
        act.wait_ge(S("consts_ready"), IDENT)
        for s in range(NS):
            af(junk[:, s, :], x[:, s, :], ACT.Square, accum_out=stat[:, s:s + 1]).then_inc(S("sq_done"), 1)
        act.wait_ge(S("sq_done"), 2)
        af(stat[:, 2:4], stat[:, 0:2], ACT.Sqrt, bias=epsr[:], scale=1.0 / D).then_inc(S("rms1_ready"), 1)
        act.wait_ge(S("prm_ready"), 1)
        af(csig[:].rearrange("p s k -> p (s k)"), prm[:, 0:16], ACT.Sigmoid).then_inc(S("csig_ready"), 1)
        for g in range(2):
            act.wait_ge(S("moda_mm"), MC * (g + 1))
            af(mrow_a[:, g, :], unit_bank(g), ACT.Copy).then_inc(S("mrow_ready"), 1)
        act.wait_ge(S("front_mm"), AFTER["xnT"])
        act.wait_ge(S("moda_ready"), 1)
        for k in range(4):
            for s in range(NS):
                o = (k % 2) * TT + s * T
                last = af(hnT[:, k, s * T:(s + 1) * T], banks[1 + k // 2][:, o:o + T], ACT.Identity,
                          bias=moda[:, 0, k, s:s + 1], scale=moda[:, 1, k, s:s + 1])
            last.then_inc(S("hna_ready"), 1)
        for ct in range(RTILES):
            act.wait_ge(S("proj_done"), ct + 1)
            if ct >= 4:
                act.wait_ge(S("mix_done"), ct - 3)
            af(raw[:, ct % 4, :], PB[ct % 4][:, 0:TT], ACT.Copy).then_inc(S("raw_copied"), 1)
        fills = [0]

        def fill(part):
            for kind, i in FILL[part]:
                o = unit_bank(fills[0])
                if kind == "R":
                    act.wait_ge(S("modb_mm"), MC * (i + 1))
                    last = af(mrow_b[:, i, :], o, ACT.Copy)
                elif kind == "X":
                    act.wait_ge(S("modbt_mm"), i + 1)
                    last = af(modt[:, i, :, :].rearrange("p (j h) s -> p h j s", h=2),
                              o.rearrange("p (h j s) -> p h j s", h=2, j=MG)[:, :, :, 0:NS], ACT.Copy)
                else:
                    act.wait_ge(S("merge_mm"), max(i + 1, 2))
                    last = af(merge[:, i, :], o, ACT.Sigmoid, bias=prm[:, 80 + i:81 + i])
                last.then_inc(S("fill_used"), 1)
                fills[0] += 1

        fill(0)
        act.wait_ge(S("mix_done"), RTILES)
        af(pr[:, 12, :], pr[:, 12, :], ACT.Tanh)
        af(pr[:, 14, :], pr[:, 14, :], ACT.Sigmoid).then_inc(S("th_ready"), 1)
        for n in range(4):
            act.wait_ge(S("zb_ready"), n + 1)
            af(sig[:, n // 2, n % 2, :], sig[:, n // 2, n % 2, :], ACT.Sigmoid).then_inc(S("sig_ready"), 1)
        fill(1)
        for j in range(4):
            d = j // 2
            act.wait_ge(S("a_done"), j + 1)
            for q in range(2 * (j % 2), 2 * (j % 2) + 2):
                last = af(aa[:, d, q, :], banks[ZB[j]][:, (q % 2) * TT:(q % 2 + 1) * TT], ACT.Sigmoid,
                          bias=prb[:, 19 + 4 * d + q:20 + 4 * d + q])
            last.then_inc(S("a_ready"), 1)
        fill(2)
        act.wait_ge(S("front_mm"), AFTER["gate"])
        for j in range(2):
            af(gate[:, 2 * j:2 * j + 2, :].rearrange("p c t -> p (c t)"), banks[(3, 0)[j]][:, :], ACT.Copy).then_inc(S("gate_ready"), 1)
        fill(3)
        act.wait_ge(S("front_mm"), AFTER["norm"])
        af(hst, banks[6][0:8, 0:TT], ACT.Sqrt).then_inc(S("nrm_ready"), 1)
        for part in (4, 5, 6):
            fill(part)
        for i in range(8):
            d, s, t2 = i // 4, (i // 2) % 2, i % 2
            act.wait_ge(S("cum_done"), i + 1)
            ps = banks[CB[i % 3]][:].rearrange("p (q k t) -> p q k t", q=2, k=2)
            af(qr[:, d, s, 2 * t2:2 * t2 + 2, :, :].rearrange("p q k t -> p (q k t)"), banks[CB[i % 3]][:, :], ACT.Exp, scale=-DECAY)
            if s == 1:
                t0 = 0 if d == 0 else T - 1
                af(pms[:, d * NT + 2 * t2:d * NT + 2 * t2 + 2], ps[:, :, 0, t0], ACT.Exp, scale=DECAY)
            af(bt[:, d, s, 2 * t2:2 * t2 + 2, :], ps[:, :, 1, :], ACT.Exp, scale=DECAY).then_inc(S("cum_used"), 1)
        fill(7)

        def mask_heads(dst, src, s, name):
            for h in range(2):
                for d in range(2):
                    last = af(dst[:, d, :, h, :], src[:, d, s, :, :], ACT.Copy, scale=hm[:, h:h + 1])
            last.then_inc(S(name), 1)

        act.wait_ge(S("scan_ops_ready"), 1)
        mask_heads(btm[0], bt, 0, "btm_ready")
        mask_heads(ktm, kt_, 0, "ktm_ready")
        for part in range(8, len(FILL)):
            fill(part)
        act.wait_ge(S("scan_ops_ready"), 2)
        mask_heads(btm[1], bt, 1, "btm_ready")
        def own_unit_bank(ps, h):
            return ps[:, h * 2 * T:(h + 1) * 2 * T].rearrange("p (q c) -> p q c", q=2)[:, :, h * HS:(h + 1) * HS]

        def z_out(n):
            act.wait_ge(S("z_mm"), n + 1)
            if n >= 2:
                act.wait_ge(S("u_mm"), n - 1)
            for h in range(2):
                last = af(zs[:, n % 2, :, h, :], own_unit_bank(banks[4], h), ACT.Copy, scale=-1.0)
            last.then_inc(S("z_evac"), 1)

        def u_out(n):
            tp, d = (n // 2) % 2, n % 2
            act.wait_ge(S("u_mm"), n + 1)
            for h in range(2):
                last = af(us[:, 2 * d + tp, :, h, :], own_unit_bank(banks[5], h), ACT.Copy)
            last.then_inc(S("u_evac"), 1)

        for s in range(NS):
            for unit, j in ((z_out, 0), (u_out, 0), (z_out, 1), (u_out, 1), (z_out, 2), (z_out, 3), (u_out, 2), (u_out, 3)):
                unit(4 * s + j)
            if s == 0:
                act.wait_ge(S("kq_mm"), 4)
                mask_heads(ktm, kt_, 1, "ktm_ready")
                act.wait_ge(S("state_mm"), 1)
                for h in range(2):
                    r = slice(h * HS, (h + 1) * HS)
                    for dd in range(2):
                        last = af(so[r, dd * NT:(dd + 1) * NT, :], banks[2 + dd][r, :].rearrange("p (q k) -> p q k", q=NT)[:, :, r], ACT.Copy)
                last.then_inc(S("state_copied"), 1)
                act.wait_ge(S("state_copied"), 1)
                for dd in range(2):
                    for h in range(2):
                        act.dma_start(O[2 + dd][0, 0].rearrange("(q h) v k -> h v q k", h=2)[h],
                                      so[h * HS:(h + 1) * HS, dd * NT:(dd + 1) * NT, :]).then_inc(S("stored"), 16)
        act.wait_ge(S("late_mm"), AFTER["var"])
        act.wait_ge(S("y_evac"), 4)
        af(hst, banks[5][0:8, 0:TT], ACT.Sqrt, bias=epsg[0:8, :], scale=1.0 / HS).then_inc(S("gstd_ready"), 1)
        for n in range(8):
            c, s = n // 2, n % 2
            act.wait_ge(S("wo_used"), n + 1)
            af(x2t[:, s, 256 * c:256 * (c + 1)], x[:, s, 256 * c:256 * (c + 1)], ACT.Square, accum_out=sqp[:, s, c:c + 1]).then_inc(S("sq_done"), 1)
        act.wait_ge(S("sqsum_ready"), 1)
        af(stat[:, 6:8], stat[:, 4:6], ACT.Sqrt, bias=epsr[:], scale=1.0 / D).then_inc(S("rms2_ready"), 1)
        for k in range(HA):
            if k % 2 == 0:
                act.wait_ge(S("xs_ready"), k // 2 + 1)
            for s in range(NS):
                h = hnT[:, k, s * T:(s + 1) * T]
                last = af(h, h, ACT.Identity, bias=modb[:, 1, k, s:s + 1], scale=modb[:, 2, k, s:s + 1])
            last.then_inc(S("hn2a_ready"), 1)
        act.wait_ge(S("late_mm"), AFTER["logits"])
        af(lgT, banks[5][0:NE, 0:TT], ACT.Identity, bias=rtb[:, 0:1]).then_inc(S("lgT_ready"), 1)
        act.wait_ge(S("x2_mm"), 1)
        for j in range(4):
            af(x2t[:, j // 2, (j % 2) * 512:(j % 2 + 1) * 512], banks[j][:, :], ACT.Copy).then_inc(S("x2_ready"), 1)
        act.wait_ge(S("top_ready"), 1)
        for s in range(NS):
            last = af(tw[:, s, :], top8[:, s, 0:4], ACT.Exp, bias=fstat[:, s:s + 1])
        last.then_inc(S("exp_ready"), 1)

        def gathered_out(n):
            act.wait_ge(S("gathered"), n)
            af(xg.rearrange("p k s -> p (k s)"), banks[6][:, :], ACT.Copy).then_inc(S("xg_ready"), 1)

        act.wait_ge(S("gathered"), 1)
        for j in range(2):
            last = af(xg[:, 4 * j:4 * j + 4, :], banks[6 + j][:].rearrange("p (k s) -> p k s", k=4)[:, :, 0:SLOTS], ACT.Copy)
        last.then_inc(S("xg_ready"), 1)
        act.wait_ge(S("items_ready"), 1)
        n_items = act.value_load(item[0:1, ITEMS:ITEMS + 1], min_val=NE, max_val=NE + EXTRA)

        with act.Fori(0, n_items) as it:
            act.wait_ge(S("g_ready"), it + 1)
            af(sgb, gsb, ACT.Sigmoid, scale=ALPHA).then_inc(S("sg_ready"), 1)
            gathered_out(it + 2)
            act.wait_ge(S("pwt_done"), it + 1)
            af(pwt.rearrange("p s t -> p (s t)"), banks[7][:, 0:TT], ACT.Copy).then_inc(S("pwt_ready"), 1)
            act.wait_ge(S("chunk_used"), it * RING + RING)
            af(ysb, banks[4][:, :], ACT.Copy).then_inc(S("ysb_ready"), 1)

        for s in range(NS):
            act.wait_ge(S("res_ready"), s + 1)
            af(hnT[:, 4 * s:4 * s + 4, :].rearrange("p k t -> p (k t)"), x[:, s, :], ACT.Square, accum_out=fstat[:, s:s + 1]).then_inc(S("sq_done"), 1)
            act.wait_ge(S("sq_done"), 11 + s)
            af(fstat[:, 2 + s:3 + s], fstat[:, s:s + 1], ACT.Sqrt, bias=epsr[:], scale=1.0 / D).then_inc(S("rms3_ready"), 1)
        for s in range(NS):
            act.wait_ge(S("out_ready"), s + 1)
            act.dma_start(O[s][0], x[:, s, :]).then_inc(S("stored"), 16)

    @block.vector
    def _(dve):
        v = nc.vector
        MUL, ADD, SUB = ALU.mult, ALU.add, ALU.subtract
        n = [0]

        def step(ins):
            n[0] += 1
            ins.then_inc(S("dve_step"), 1)

        def sync():
            dve.wait_ge(S("dve_step"), n[0])

        def own(ins):
            step(ins)
            sync()

        def last_of(name, count):
            dve.wait_ge(S(name), count)

        def bc(ap, m):
            return ap.unsqueeze(1).to_broadcast([P, m, ap.shape[-1]])

        def col(ap, m):
            return ap.unsqueeze(2).to_broadcast([P, ap.shape[-1], m])

        dve.wait_ge(S("front_mm"), AFTER["prmT"])
        v.tensor_copy(prm[:], banks[0][:, 0:96]).then_inc(S("prm_ready"), 1)
        dve.wait_ge(S("rms1_ready"), 1)
        own(v.reciprocal(stat[:, 0:2], stat[:, 2:4]))
        for s in range(NS):
            v.tensor_scalar(xn[:, s, :], x[:, s, :], stat[:, s:s + 1], None, MUL).then_inc(S("xn_ready"), 1)
        last_of("prm_ready", 1)
        dve.wait_ge(S("csig_ready"), 1)
        v.tensor_tensor(cpad[:, :, 0:NS].rearrange("p k s -> p s k"), prm[:, 0:16].rearrange("p (s k) -> p s k", s=NS), csig[:], MUL).then_inc(S("cpad_ready"), 1)
        own(v.reduce_sum(par4[:], ident[:].rearrange("p (n j) -> p j n", j=4), axis=AX.X))
        own(v.tensor_tensor(par2[:], par4[:, 0:2], par4[:, 2:4], ADD))
        dve.wait_ge(S("front_mm"), AFTER["prbT"])
        own(v.tensor_copy(prb[:], banks[0][:, 128:183]))
        m15 = prb[:, 0:RTILES]
        step(v.tensor_scalar(mu[:, 0, :], m15, -1.0, 1.0, MUL, ADD))
        for j in range(2):
            step(v.tensor_scalar(mu[:, 1 + j, :], m15, par2[:, j:j + 1], None, MUL))
        for j in range(4):
            step(v.tensor_scalar(mu[:, 3 + j, :], m15, par4[:, j:j + 1], None, MUL))
        v.tensor_scalar(kam[:], prb[:, 31:35], -1.0, 1.0, MUL, ADD).then_inc(S("prb_ready"), 1)
        dve.wait_ge(S("modat_mm"), 2)
        for g in range(2):
            step(v.tensor_tensor(moda[:, g, :, :].rearrange("p (j h) s -> p h j s", h=2),
                                 banks[6][:, g * MW:(g + 1) * MW].rearrange("p (h j s) -> p h j s", h=2, j=MG)[:, :, :, 0:NS],
                                 prm[:, 16 + KT * g:16 + KT * (g + 1)].rearrange("p (j h) -> p h j", h=2).unsqueeze(3).to_broadcast([P, 2, MG, NS]), ADD))
        sync()
        v.scalar_tensor_tensor(moda[:, 1, :, :], moda[:, 1, :, :], 1.0, col(prm[:, 64:72], NS), ADD, MUL).then_inc(S("moda_ready"), 1)
        last_of("moda_ready", 1)
        dve.wait_ge(S("front_mm"), AFTER["xnT"])
        for k in range(4, KT):
            for s in range(NS):
                o = (k % 2) * TT + s * T
                last = v.tensor_scalar(hnT[:, k, s * T:(s + 1) * T], banks[1 + k // 2][:, o:o + T], moda[:, 1, k, s:s + 1],
                                       moda[:, 0, k, s:s + 1], MUL, ADD)
            last.then_inc(S("hnd_ready"), 1)
        dve.wait_ge(S("consts_ready"), MASKS)
        prev = ident[:]
        for i in range(7):
            m = 2 ** (i + 1)
            if m < P:
                dve.wait_ge(S("bd_ready"), i + 1)
                cur = bdm[:, (i + 1) % 2, :]
            else:
                cur = ones[:]
            own(v.tensor_tensor(lvl[:, i, 0, :], cur, prev, SUB))
            step(v.tensor_tensor(lvl[:, i, 1, :], lvl[:, i, 0, :], upp[:], MUL))
            v.tensor_tensor(lvl[:, i, 0, :], lvl[:, i, 0, :], low, MUL).then_inc(S("bd_used"), 1)
            prev = cur
        step(v.tensor_scalar(tri[:, 0, :, :], mqr[:, 0, :, :], rowlo[:], None, SUB))
        v.tensor_scalar(tri[:, 1, :, :], mqr[:, 1, :, :], rowlo[:], -1.0, ADD, ADD).then_inc(S("tri_ready"), 1)

        last_of("prb_ready", 1)
        sync()
        for ct in range(RTILES):
            dve.wait_ge(S("raw_copied"), ct + 1)
            r_ = raw[:, ct % 4, :]
            o_ = pr[:, ct, :]
            own(v.tensor_scalar(o_, r_, mu[:, 0, ct:ct + 1], None, MUL))

            def add(dst, src, j):
                return v.scalar_tensor_tensor(dst, src, mu[:, j, ct:ct + 1], dst, MUL, ADD)

            og, rg = o_[:, T:TT].rearrange("p (r c) -> p r c", c=GRID_W), r_[:, T:TT].rearrange("p (r c) -> p r c", c=GRID_W)
            step(add(o_[:, 1:T], r_[:, 0:T - 1], 1))
            own(add(og[:, :, 1:], rg[:, :, :-1], 3))
            step(add(o_[:, 0:T - 1], r_[:, 1:T], 2))
            own(add(og[:, :, :-1], rg[:, :, 1:], 4))
            own(add(og[:, 1:, :], rg[:, :-1, :], 5))
            add(og[:, :-1, :], rg[:, 1:, :], 6).then_inc(S("mix_done"), 1)
        last_of("mix_done", RTILES)

        dve.wait_ge(S("front_mm"), AFTER["pcnt"])
        cbuf = corr[:].rearrange("p c t -> p (c t)")[:, 0:512]
        pbf = pband.rearrange("p g t -> p (g t)")
        own(v.reciprocal(cbuf, banks[4][:, :]))
        own(v.tensor_tensor(pbf, pbf, cbuf, MUL))
        v.tensor_tensor(pband, pband, bc(ident[:], 4), SUB).then_inc(S("pband_ready"), 1)
        dve.wait_ge(S("pu_mm"), 2)
        for s in range(NS):
            v.tensor_copy(utok[:, s, :], banks[2 + s][:, :]).then_inc(S("utok_ready"), 1)
        for i in range(4):
            dve.wait_ge(S("z_done"), i + 1)
            v.tensor_tensor(sig[:, i // 2, i % 2, :], banks[ZB[i]][:, :], w0row[:, i // 2, :], ADD).then_inc(S("zb_ready"), 1)
        for q in range(NT):
            step(v.tensor_scalar(kk[:, q, :], pr[:, 4 + q, :], prb[:, 27 + q:28 + q], None, MUL))
        sync()
        v.tensor_tensor(raw[:], kk[:], kk[:], MUL).then_inc(S("ksq_ready"), 1)
        dve.wait_ge(S("front_mm"), AFTER["pooled"])
        for j in range(2):
            v.tensor_copy(pooled[:, 2 * j:2 * j + 2, :].rearrange("p g t -> p (g t)"), banks[2 + j][:, :]).then_inc(S("pooled_ready"), 1)
        dve.wait_ge(S("front_mm"), AFTER["mixed"])
        for j in range(2):
            for g in (2 * j, 2 * j + 1):
                last = v.tensor_scalar(pmT[:, g, :], banks[(4, 2)[j]][:, (g % 2) * TT:(g % 2 + 1) * TT], prb[:, 15 + g:16 + g], None, MUL)
            last.then_inc(S("mixed_ready"), 1)
        dve.wait_ge(S("a_ready"), 4)
        for d in range(2):
            for q in range(NT):
                step(v.tensor_scalar(kd[:, d, q, :], aa[:, d, q, :], prb[:, 31 + q:32 + q], kam[:, q:q + 1], MUL, ADD))
        sync()
        for d in range(2):
            step(v.tensor_tensor(kd[:, d, :, :], kd[:, d, :, :], pr[:, 4:8, :], MUL))
        dve.wait_ge(S("front_mm"), AFTER["vt"])
        for s in range(NS):
            v.tensor_copy(vt[:, s, :], banks[(2, 0)[s]][:, :]).then_inc(S("vt_ready"), 1)
        dve.wait_ge(S("nrm_ready"), 1)
        own(v.tensor_scalar(hst, hst, 1e-12, None, ALU.max))
        v.reciprocal(hst, hst).then_inc(S("inorm_ready"), 1)
        dve.wait_ge(S("front_mm"), AFTER["inorm"])
        for j in range(2):
            last = v.tensor_tensor(kk[:, 2 * j:2 * j + 2, :].rearrange("p c t -> p (c t)"), kk[:, 2 * j:2 * j + 2, :].rearrange("p c t -> p (c t)"),
                                   banks[(6, 1)[j]][:, :], MUL)
            if j == 0:
                step(last)
        last.then_inc(S("kk_ready"), 1)
        last_of("kk_ready", 1)
        own(v.tensor_tensor(raw[:], kd[:, 0, :, :], kd[:, 1, :, :], ADD))
        own(v.tensor_tensor(raw[:], raw[:], pr[:, 0:4, :], MUL))
        for q in range(NT):
            last = v.tensor_scalar(raw[:, q, :], raw[:, q, :], prb[:, 35 + q:36 + q], None, MUL)
        last.then_inc(S("rkk_ready"), 1)
        dve.wait_ge(S("front_mm"), AFTER["rk"])
        for j in range(2):
            step(v.tensor_tensor(corr[:, 2 * j:2 * j + 2, :].rearrange("p c t -> p (c t)"), pr[:, 8 + 2 * j:10 + 2 * j, :].rearrange("p c t -> p (c t)"),
                                 banks[(3, 1)[j]][:, :], MUL))

        dve.wait_ge(S("cum_used"), 8)
        dve.wait_ge(S("front_mm"), AFTER["s0"])
        for h in range(2):
            r = slice(h * HS, (h + 1) * HS)
            step(v.tensor_tensor(s0t[r, :, h, :], banks[4][r, :].rearrange("p (i v) -> p i v", v=HS),
                                 pms[r, :].unsqueeze(2).to_broadcast([HS, 2 * NT, HS]), MUL))
        step(v.tensor_copy(fin[:, 0, :], qr[:, 0, 0, :, 1, T - 1]))
        own(v.tensor_copy(fin[:, 1, :], qr[:, 1, 0, :, 1, 0]))
        for s in range(NS):
            ts = slice(s * T, (s + 1) * T)
            for d in range(2):
                step(v.tensor_tensor(qr[:, d, s, :, 0, :], qr[:, d, s, :, 0, :], kk[:, :, ts], MUL))
                step(v.tensor_tensor(qr[:, d, s, :, 1, :], qr[:, d, s, :, 1, :], pr[:, 0:4, ts], MUL))
                step(v.tensor_tensor(kt_[:, d, s, :, :], bt[:, d, s, :, :], kd[:, d, :, ts], MUL))
                own(v.tensor_tensor(bt[:, d, s, :, :], bt[:, d, s, :, :], aa[:, d, :, ts], MUL))
                last = v.tensor_tensor(bt[:, d, s, :, :], bt[:, d, s, :, :], kk[:, :, ts], MUL)
                if d == 0:
                    step(last)
            last.then_inc(S("scan_ops_ready"), 1)
            last_of("scan_ops_ready", s + 1)
        dve.wait_ge(S("fill_used"), UNITS.index(("X", 3)) + 1)
        own(v.tensor_tensor(modb[:].rearrange("p g k s -> p (g k) s"), modt[:].rearrange("p g k s -> p (g k) s"),
                            col(prm[:, 32:64], NS), ADD))
        step(v.scalar_tensor_tensor(modb[:, 2, :, :], modb[:, 2, :, :], 1.0, col(prm[:, 72:80], NS), ADD, MUL))
        for gi, m in enumerate((0, 3)):
            last = v.tensor_copy(gcol[:, gi, :, :], modb[:, m, :, :].rearrange("p k s -> p s k"))
            if gi == 0:
                step(last)
        last.then_inc(S("gcol_ready"), 1)
        dve.wait_ge(S("late_mm"), AFTER["grow"])
        v.tensor_copy(grow, banks[6][0:32, 0:P]).then_inc(S("grow_ready"), 1)
        def states_turn(j):
            src = (bt, kt_)[j]
            for d in range(2):
                if j:
                    dve.wait_ge(S("bk_done"), d + 1)
                v.tensor_tensor(bfin[:, d, :, :], src[:, d, 0, :, :], col(fin[:, d, :], T), MUL).then_inc(S("bf_ready"), 1)
            for d in range(2):
                dve.wait_ge(S("bk_done"), 2 * j + d + 1)
                v.tensor_copy(bkt[:, j, d, :], banks[6 + d][:, :]).then_inc(S("bk_ready"), 1)

        def b4(i):
            return banks[i][:].rearrange("p (i t) -> p i t", i=4)

        for s in range(NS):
            def a_out(g):
                d = g // 2
                dve.wait_ge(S("a_mm"), 4 * s + g + 1)
                v.tensor_tensor(work[:, g, W_M, :, :], b4(2 * (g % 2)), bc(lvl[:, 0, d, :], 4), MUL).then_inc(S("ma_ready"), 1)
                own(v.tensor_tensor(work[:, g, W_AT, :, :], b4(2 * (g % 2) + 1), bc(mqr[:, d, 0, :], 4), MUL))
                own(v.tensor_tensor(work[:, g, W_XT, :, :], work[:, g, W_AT, :, :], bc(lvl[:, 0, 1 - d, :], 4), MUL))
                v.tensor_tensor(work[:, g, W_XT, :, :], bc(ident[:], 4), work[:, g, W_XT, :, :], SUB).then_inc(S("a_evac"), 1)

            def m_out(k):
                n = NSTEP * s + k
                dve.wait_ge(S("m_mm"), n + 1)
                if k < 4:
                    dve.wait_ge(S("xa_ready"), 4 * s + k + 1)
                v.tensor_tensor(work[:, k % 4, W_M, :, :], b4(4 + k % 2), bc(lvl[:, 1 + k // 4, (k % 4) // 2, :], 4), MUL).then_inc(S("m_evac"), 1)

            def x_out(k):
                g, n = k % 4, NSTEP * s + k
                dve.wait_ge(S("x_mm"), n + 1)
                if k >= 4:
                    last_of("x_upd", n - 4 + 1)
                else:
                    last_of("a_evac", 4 * s + k + 1)
                bx, bxt = XB[k % 2]
                if k < NSTEP - 4:
                    step(v.tensor_tensor(work[:, g, W_X, :, :], work[:, g, W_X, :, :], b4(bx), SUB))
                v.tensor_tensor(work[:, g, W_XT, :, :], work[:, g, W_XT, :, :], b4(bxt), SUB).then_inc(S("x_upd"), 1)

            for unit, k in ((a_out, 0), (a_out, 1), (a_out, 2), (m_out, 0), (a_out, 3), (x_out, 0), (m_out, 1), (m_out, 2)):
                unit(k)
            for k in range(1, NSTEP):
                x_out(k)
                if k + 2 < NSTEP:
                    m_out(k + 2)
                if s == 0 and k in BKSTEP:
                    states_turn(BKSTEP.index(k))
            last_of("x_upd", NSTEP * (s + 1))

            def kq_out(j):
                tp, d = j // 2, j % 2
                g = 2 * d + tp
                dve.wait_ge(S("kq_mm"), 4 * s + j + 1)
                for i in range(2):
                    step(v.tensor_tensor(kqm(g)[:, 2 * i:2 * i + 2, :, :].rearrange("p i k t -> p i (k t)"),
                                         banks[2 * (j % 2) + i][:].rearrange("p (i c) -> p i c", i=2),
                                         bc(mqr[:, d, :, :].rearrange("p k t -> p (k t)"), 2), MUL))
                v.tensor_tensor(work[:, g, W_AT, :, :], b4(6 + j % 2), bc(mqr[:, d, 1, :], 4), MUL).then_inc(S("kq_evac"), 1)

            def y_out(tp):
                dve.wait_ge(S("y_mm"), 2 * s + tp + 1)
                v.tensor_tensor(kk[:, 2 * tp:2 * tp + 2, s * T:(s + 1) * T], banks[5][:, 0:2 * T].rearrange("p (q t) -> p q t", q=2),
                                corr[:, 2 * tp:2 * tp + 2, s * T:(s + 1) * T], ADD).then_inc(S("y_evac"), 1)

            for unit, j in ((kq_out, 0), (kq_out, 1), (kq_out, 2), (kq_out, 3), (y_out, 0), (y_out, 1)):
                unit(j)

        last_of("y_evac", 4)
        dve.wait_ge(S("late_mm"), AFTER["mean"])

        def pair(ap, j):
            return ap[:, 2 * j:2 * j + 2, :].rearrange("p c t -> p (c t)")

        for j in range(2):
            step(v.tensor_tensor(pair(kk, j), pair(kk, j), banks[(4, 6)[j]][:, :], SUB))
        sync()
        dve.wait_ge(S("stored"), 64)
        v.tensor_tensor(raw[:], kk[:], kk[:], MUL).then_inc(S("ysq_ready"), 1)
        dve.wait_ge(S("gstd_ready"), 1)
        v.reciprocal(hst, hst).then_inc(S("istd_ready"), 1)

        def merge_pool(m):
            dve.wait_ge(S("pout_mm"), m + 1)
            v.tensor_tensor(ms[:, m, :], merge[:, m, :], banks[m % 4][:, 0:TT], MUL).then_inc(S("pout_used"), 1)

        for m in range(4):
            merge_pool(m)
        dve.wait_ge(S("late_mm"), AFTER["istd"])
        for j in range(2):
            step(v.tensor_tensor(pair(kk, j), pair(kk, j), banks[(4, 6)[j]][:, :], MUL))
        sync()
        for q in range(NT):
            step(v.tensor_scalar(kk[:, q, :], kk[:, q, :], prb[:, 39 + q:40 + q], prb[:, 43 + q:44 + q], MUL, ADD))
        sync()
        v.tensor_tensor(kk[:], kk[:], gate[:], MUL).then_inc(S("yn_ready"), 1)
        for m in range(4, KT):
            merge_pool(m)
        last_of("yn_ready", 1)
        last_of("pout_used", KT)
        for m in range(KT):
            dve.wait_ge(S("rout_mm"), m + 1)
            own(v.tensor_tensor(gate[:, m % 4, :], merge[:, KT + m, :], banks[m % 4][:, 0:TT], MUL))
            v.tensor_tensor(ms[:, m, :], ms[:, m, :], gate[:, m % 4, :], ADD).then_inc(S("rout_used"), 1)
        dve.wait_ge(S("gbc_in"), 32)
        for c in range(4):
            for s in range(NS):
                i = 2 * c + s
                dve.wait_ge(S("wo_mm"), i + 1)
                cs = slice(256 * c, 256 * c + 256)
                own(v.tensor_tensor(corr[:, i % 4, :], banks[(0, 1, 5, 4)[i % 4]][:, 0:256], gbc[:, s, cs], MUL))
                v.tensor_tensor(x[:, s, cs], x[:, s, cs], corr[:, i % 4, :], ADD).then_inc(S("wo_used"), 1)
        dve.wait_ge(S("sq_done"), 10)
        v.reduce_sum(stat[:, 4:6], sqp, axis=AX.X).then_inc(S("sqsum_ready"), 1)
        dve.wait_ge(S("rms2_ready"), 1)
        own(v.reciprocal(stat[:, 4:6], stat[:, 6:8]))
        for s in range(NS):
            last = v.tensor_scalar(dgr[:, s, :], ident[:], stat[:, 4 + s:5 + s], None, MUL)
            if s == 0:
                step(last)
        last.then_inc(S("dgr_ready"), 1)
        dve.wait_ge(S("late_mm"), AFTER["rbc"])
        own(v.tensor_copy(rbc, banks[0][:, 0:TT]))
        for j in range(4):
            v.tensor_tensor(hnT[:, 2 * j:2 * j + 2, :], banks[XT[j]][:, :].rearrange("p (k t) -> p k t", k=2), bc(rbc, 2), MUL).then_inc(S("xs_ready"), 1)
        last_of("xs_ready", 4)
        last_of("gcol_ready", 1)
        for k in range(HA, KT):
            for s in range(NS):
                h = hnT[:, k, s * T:(s + 1) * T]
                last = v.tensor_scalar(h, h, modb[:, 2, k, s:s + 1], modb[:, 1, k, s:s + 1], MUL, ADD)
            last.then_inc(S("hn2d_ready"), 1)

        def choose(n, e):
            for s in range(NS):
                last = v.tensor_scalar(p2[:, s, :], iota2[:], base[:, bass.ds(n, 1)], rank[:, s, bass.ds(e, 1)], ADD, ALU.is_equal)
            last.then_inc(S("sel_ready"), 1)

        def expert_row(e):
            v.tensor_copy(sele, ident[:, bass.ds(e, 1)].to_broadcast([P, SLOTS])).then_inc(S("sele_ready"), 1)

        dve.wait_ge(S("late_mm"), AFTER["lg"])
        own(v.tensor_copy(lg[:].rearrange("p s e -> p (s e)"), banks[6][:, 256:256 + NS * NE]))
        for s in range(NS):
            step(v.max(top8[:, s, :], lg[:, s, :]))
        sync()
        v.tensor_scalar(fstat[:, 0:2], top8[:, :, 0], -1.0, None, MUL).then_inc(S("top_ready"), 1)
        for s in range(NS):
            step(v.max_index(idx8[:, s, :], top8[:, s, :], lg[:, s, :]))
        sync()
        own(v.tensor_copy(idxf[:], idx8[:]))
        dve.wait_ge(S("consts_ready"), LISTS)

        def over_choices(ap):
            return ap.unsqueeze(3).to_broadcast([P, NS, 4, NE])

        iot = iota2[:, 0:NE].unsqueeze(1).unsqueeze(1).to_broadcast([P, NS, 4, NE])
        own(v.tensor_tensor(oh4, iot, over_choices(idxf[:, :, 0:4]), ALU.is_equal))
        v.reduce_sum(sel[:], oh4.rearrange("p s j e -> p s e j"), axis=AX.X).then_inc(S("sel_done"), 1)
        last_of("sel_done", 1)
        dve.wait_ge(S("late_mm"), AFTER["rank"])
        own(v.scalar_tensor_tensor(rank[:], banks[6][:, 0:2 * NE].rearrange("p (s e) -> p s e", s=NS), 1.0, sel[:], ADD, MUL))
        own(v.tensor_scalar(rank[:], rank[:], -1.0, None, ADD))
        choose(0, 0)
        expert_row(0)
        own(v.tensor_copy(cnt[:, 0:1], banks[4][0:NE, 64:65]))
        own(v.tensor_scalar(fl[:], thr3[0:NE, :], cnt[:, 0:1], None, ALU.is_lt))
        v.reduce_sum(cnt[:, 1:2], fl[:], axis=AX.X).then_inc(S("extra_ready"), 1)
        dve.wait_ge(S("late_mm"), AFTER["pos"])
        own(v.tensor_copy(cnt[:, 2:3], banks[4][0:NE, 65:66]))
        own(v.tensor_scalar(posc[:], iota3[0:NE, :], cnt[:, 2:3], None, ADD))
        for c in range(3):
            own(v.tensor_scalar(oh16[:, c, :], iota2[0:NE, 0:EXTRA], posc[:, c:c + 1], fl[:, c:c + 1], ALU.is_equal, MUL))
        step(v.tensor_tensor(e16[:, 0, :], oh16[:, 0, :], oh16[:, 1, :], ADD))
        own(v.scalar_tensor_tensor(e16[:, 1, :], oh16[:, 1, :], 2.0, oh16[:, 0, :], MUL, ADD))
        step(v.tensor_tensor(e16[:, 0, :], e16[:, 0, :], oh16[:, 2, :], ADD))
        own(v.scalar_tensor_tensor(e16[:, 1, :], oh16[:, 2, :], 3.0, e16[:, 1, :], MUL, ADD))
        v.tensor_scalar(e16[:, 1, :], e16[:, 1, :], float(SLOTS), None, MUL).then_inc(S("e16_ready"), 1)
        dve.wait_ge(S("exp_ready"), 1)
        own(v.reduce_sum(fstat[:, 2:4], tw[:], axis=AX.X))
        own(v.reciprocal(fstat[:, 2:4], fstat[:, 2:4]))
        own(v.tensor_tensor(twn[:], tw[:], fstat[:, 2:4].unsqueeze(2).to_broadcast([P, NS, 4]), MUL))
        own(v.tensor_tensor(cw4, oh4, over_choices(twn[:]), MUL))
        v.reduce_sum(comb[:], cw4.rearrange("p s j e -> p s e j"), axis=AX.X).then_inc(S("comb_ready"), 1)
        dve.wait_ge(S("late_mm"), AFTER["list"])
        step(v.tensor_copy(item[0:1, NE:NE + EXTRA], banks[4][0:1, 96:96 + EXTRA]))
        step(v.tensor_copy(base[:, NE:NE + EXTRA], banks[4][:, 128:128 + EXTRA]))
        own(v.tensor_scalar(item[0:1, ITEMS:ITEMS + 1], banks[4][0:1, 66:67], float(NE), None, ADD))

        v.tensor_copy(tick[:], ones[:, 0:1]).then_inc(S("items_ready"), 1)
        dve.wait_ge(S("items_ready"), 1)
        n_items = dve.value_load(item[0:1, ITEMS:ITEMS + 1], min_val=NE, max_val=NE + EXTRA)
        with dve.Fori(0, n_items) as it:
            e = dve.value_load(item[0:1, bass.ds(it, 1)], min_val=0, max_val=NE - 1)
            nxt = dve.value_load(item[0:1, bass.ds(it + 1, 1)], min_val=0, max_val=NE - 1)
            dve.wait_ge(S("sel_ready"), it + 1)
            for s in range(NS):
                last = v.tensor_scalar(pw[:, s, :], p2[:, s, :], comb[:, s, bass.ds(e, 1)], None, MUL)
            last.then_inc(S("pw_ready"), 1)
            dve.wait_ge(S("pw_ready"), it + 1)
            dve.wait_ge(S("gathered"), it + 1)
            choose(it + 1, nxt)
            dve.wait_ge(S("chunk_used"), it * RING + GU_CHUNKS)
            v.tensor_scalar(gsb, banks[4][:, :], LIMIT, None, ALU.min).then_inc(S("g_ready"), 1)
            v.tensor_scalar(lcb, banks[5][:, :], LIMIT, -LIMIT, ALU.min, ALU.max).then_inc(S("lin_done"), 1)
            dve.wait_ge(S("lin_done"), it + 1)
            v.scalar_tensor_tensor(lcb, lcb, 1.0, gsb, ADD, MUL).then_inc(S("gl_done"), 1)
            dve.wait_ge(S("gl_done"), it + 1)
            dve.wait_ge(S("sg_ready"), it + 1)
            v.tensor_tensor(act_, lcb, sgb, MUL).then_inc(S("act_ready"), 1)
            dve.wait_ge(S("actT_done"), it + 1)
            v.tensor_copy(actT.rearrange("p j h s -> p (j h s)"), banks[5][:, :]).then_inc(S("actT_ready"), 1)
            dve.wait_ge(S("chunk_used"), it * RING + GU_CHUNKS + 2)
            expert_row(nxt)

        dve.wait_ge(S("gbc_in"), 64)
        dve.wait_ge(S("wfin_in"), 16)
        for s in range(NS):
            dve.wait_ge(S(("scattered_ctx", "scattered_lat")[s]), n_items)
            for h in range(2):
                cs = slice(512 * h, 512 * h + 512)
                step(v.tensor_tensor(gbc[:, s, cs], gbc[:, s, cs], banks[2 * s + h][:, :], MUL))
            sync()
            v.tensor_tensor(x[:, s, :], x[:, s, :], gbc[:, s, :], ADD).then_inc(S("res_ready"), 1)
        for s in range(NS):
            dve.wait_ge(S("rms3_ready"), s + 1)
            own(v.reciprocal(fstat[:, 2 + s:3 + s], fstat[:, 2 + s:3 + s]))
            last_of("res_ready", s + 1)
            v.scalar_tensor_tensor(x[:, s, :], x[:, s, :], fstat[:, 2 + s:3 + s], wbuf, MUL, MUL).then_inc(S("out_ready"), 1)

    return ctx


_INS = ['x_prompt', 'x_sample', 'state_fwd', 'state_bwd', 'c', 'c_ctx', 'w_mod', 'b_mod', 'norm_mix_w', 'w_in', 'b_merge',
        'pool_w', 'pool_scale', 'w_pool_out', 'shift_mu', 'decay_w0', 'decay_w2', 'iclr_a0', 'iclr_a2', 'gate_w2',
        'k_k', 'k_a', 'r_k', 'ln_x_w', 'ln_x_b', 'w_rwkv_out', 'w_o', 'norm_ffn_w', 'router_w', 'router_b',
        'expert_w_gu', 'expert_b_gu', 'expert_w_down', 'expert_b_down', 'norm_final_w']
_OUTS = [(1, 128, 1024), (1, 128, 1024), (1, 1, 8, 64, 64), (1, 1, 8, 64, 64)]


def kernel(**inputs):
    import numpy as np
    import concourse.bacc as bacc
    from concourse.bass_utils import run_bass_kernel_spmd

    nc = bacc.Bacc("TRN2", target_bir_lowering=False, num_devices=1)
    arrays, A = {}, {}
    for name in _INS:
        a = np.ascontiguousarray(inputs[name])
        arrays[f"in_{name}"] = a
        A[name] = nc.dram_tensor(f"in_{name}", a.shape, mybir.dt.from_np(a.dtype), kind="ExternalInput").ap()
    outs = [nc.dram_tensor(f"out_{i}", s, F32, kind="ExternalOutput").ap() for i, s in enumerate(_OUTS)]
    scratch = nc.dram_tensor("gate_rows", (2, NS, D), F32, kind="Internal").ap()
    ctx = trunk_kernel(nc, A, outs, scratch)
    ctx.close()
    r = run_bass_kernel_spmd(nc, [arrays], core_ids=[0])
    return tuple(r.results[0][f"out_{i}"] for i in range(4))
```
